# Optimizing a Trainium2 kernel written in Bass

```python
import jax, jax.numpy as jnp
from jax import lax
import numpy as np

D_MODEL = 1024
BATCH = 1
SEQ = 128
DEPTH = 2
DEC_BATCH = 1
DEC_SEQ = 256
PAST_LEN = 128

GRID_W = 64
HEAD_DIM = 64
A_HEADS = 8
A_KV_HEADS = 2
A_GROUP = A_HEADS // A_KV_HEADS
Q_BLOCK = 128
ROPE_THETA = 10000.0
ROT_AXIS_DIM = HEAD_DIM // 2
B_HEADS = 8
B_HEAD_DIM = 64
B_WIDTH = B_HEADS * B_HEAD_DIM
A_Q_WIDTH = A_HEADS * HEAD_DIM
A_KV_WIDTH = A_KV_HEADS * HEAD_DIM
MIX_WIDTH = A_Q_WIDTH + B_WIDTH
IN_WIDTH = A_Q_WIDTH + 2 * A_KV_WIDTH + 5 * B_WIDTH
GLA_CHUNK = 16
CONV_DIM = D_MODEL
CONV_WIDTH = 31
MOE_GROUPS = 4
EXPERTS_PER_GROUP = 4
N_EXPERTS = MOE_GROUPS * EXPERTS_PER_GROUP
EXPERT_DIM = 256
TOP_K = 2
N_AB_LAYERS = (DEPTH + 1) // 2
N_CONV_LAYERS = DEPTH // 2
EPS = 1e-6

kernel_name = "hybrid_dit_gqa_hgrn2_conformer_hmoe_step"

def rms_norm(x, g):
    xf = x.astype(jnp.float32)
    y = xf * lax.rsqrt(jnp.mean(xf * xf, axis=-1, keepdims=True) + EPS)
    return (y * g.astype(jnp.float32)).astype(x.dtype)

def layer_norm(x, g, b):
    xf = x.astype(jnp.float32)
    mu = jnp.mean(xf, axis=-1, keepdims=True)
    var = jnp.mean(jnp.square(xf - mu), axis=-1, keepdims=True)
    y = (xf - mu) * lax.rsqrt(var + EPS) * g.astype(jnp.float32) + b.astype(jnp.float32)
    return y.astype(x.dtype)

def adaln(cond, w, b):
    m = jax.nn.silu(cond) @ w + b
    return jnp.split(m[:, None, :], 6, axis=-1)

def modulate(x, g, shift, scale):
    return rms_norm(x, g) * (1 + scale) + shift

def axial_rope_tables(n_tokens):
    rows = n_tokens // GRID_W
    row = jnp.repeat(jnp.arange(rows, dtype=jnp.float32), GRID_W)
    col = jnp.tile(jnp.arange(GRID_W, dtype=jnp.float32), rows)
    inv = ROPE_THETA ** (-jnp.arange(0, ROT_AXIS_DIM, 2, dtype=jnp.float32) / ROT_AXIS_DIM)
    ang_r = row[:, None] * inv[None, :]
    ang_c = col[:, None] * inv[None, :]
    return (jnp.cos(ang_r), jnp.sin(ang_r), jnp.cos(ang_c), jnp.sin(ang_c))

def _rotate(x, cos, sin):
    x1, x2 = jnp.split(x, 2, axis=-1)
    cos = cos[None, :, None, :].astype(x.dtype)
    sin = sin[None, :, None, :].astype(x.dtype)
    return jnp.concatenate([x1 * cos - x2 * sin, x2 * cos + x1 * sin], axis=-1)

def apply_axial_rope(x, tables):
    cr, sr, cc, sc = tables
    xr, xc = jnp.split(x, 2, axis=-1)
    return jnp.concatenate([_rotate(xr, cr, sr), _rotate(xc, cc, sc)], axis=-1)

def gqa_attend(q, k, v):
    bsz, t = q.shape[:2]
    n_blk = t // Q_BLOCK
    scale = HEAD_DIM ** -0.5
    q_blocks = jnp.moveaxis(q.reshape(bsz, n_blk, Q_BLOCK, A_KV_HEADS, A_GROUP, HEAD_DIM), 1, 0)

    def attend_block(qb):
        s = jnp.einsum("bqhgd,bkhd->bhgqk", qb, k).astype(jnp.float32) * scale
        p = jax.nn.softmax(s, axis=-1).astype(v.dtype)
        return jnp.einsum("bhgqk,bkhd->bqhgd", p, v)

    o = lax.map(attend_block, q_blocks)
    return jnp.moveaxis(o, 0, 1).reshape(bsz, t, A_Q_WIDTH)

def gla_chunked(q, k, v, log_f, s0):
    bsz, t, h, dk = q.shape
    dv = v.shape[-1]
    n = t // GLA_CHUNK
    rs = lambda a: a.reshape(bsz, n, GLA_CHUNK, h, a.shape[-1]).astype(jnp.float32)
    qc, kc, vc, gc = rs(q), rs(k), rs(v), rs(log_f)
    g_cum = jnp.cumsum(gc, axis=2)
    g_last = g_cum[:, :, -1]
    causal = jnp.tril(jnp.ones((GLA_CHUNK, GLA_CHUNK), dtype=bool))
    diff = g_cum[:, :, :, None] - g_cum[:, :, None, :]
    decay = jnp.exp(jnp.where(causal[None, None, :, :, None, None], diff, -jnp.inf))
    a = jnp.einsum("bnihd,bnijhd,bnjhd->bnhij", qc, decay, kc)
    o_intra = jnp.einsum("bnhij,bnjhe->bnihe", a, vc)
    upd = jnp.einsum("bnchd,bnche->bnhde", kc * jnp.exp(g_last[:, :, None] - g_cum), vc)
    chunk_decay = jnp.exp(g_last)

    def step(s, inp):
        dec, u = inp
        return dec[..., None] * s + u, s

    s_final, s_starts = lax.scan(step, s0.astype(jnp.float32),
                                 (jnp.moveaxis(chunk_decay, 1, 0), jnp.moveaxis(upd, 1, 0)))
    s_starts = jnp.moveaxis(s_starts, 0, 1)
    o_inter = jnp.einsum("bnchd,bnhde->bnche", qc * jnp.exp(g_cum), s_starts)
    o = (o_intra + o_inter).reshape(bsz, t, h, dv)
    return o.astype(v.dtype), s_final.astype(q.dtype)

def forget_gates(raw, lb):
    lb = lb.astype(jnp.float32).reshape(B_HEADS, B_HEAD_DIM)
    f = lb + (1.0 - lb) * jax.nn.sigmoid(raw.astype(jnp.float32))
    return 1.0 - f, jnp.log(f)

def hgrn2_bidirectional(q, v, gate, gates, s0, out_gain):
    (k_f, lf_f), (k_b, lf_b) = gates
    o_f, s_f = gla_chunked(q, k_f, v, lf_f, s0[:, 0])
    rev = lambda a: jnp.flip(a, axis=1)
    o_b, s_b = gla_chunked(rev(q), rev(k_b), rev(v), rev(lf_b), s0[:, 1])
    o = rms_norm(o_f + rev(o_b), out_gain) * jax.nn.silu(gate)
    bsz, t = q.shape[:2]
    return o.reshape(bsz, t, B_WIDTH), jnp.stack([s_f, s_b], axis=1)

def ab_project(h, w_in, q_gain, k_gain, lb):
    bsz, t, _ = h.shape
    cuts = [A_Q_WIDTH, A_Q_WIDTH + A_KV_WIDTH, A_Q_WIDTH + 2 * A_KV_WIDTH]
    cuts = cuts + [cuts[-1] + B_WIDTH * i for i in range(1, 5)]
    qa, ka, va, qb, f_fwd, f_bwd, ib, gb = jnp.split(h @ w_in, cuts, axis=-1)
    qa = rms_norm(qa.reshape(bsz, t, A_KV_HEADS, A_GROUP, HEAD_DIM), q_gain)
    ka = rms_norm(ka.reshape(bsz, t, A_KV_HEADS, HEAD_DIM), k_gain)
    va = va.reshape(bsz, t, A_KV_HEADS, HEAD_DIM)
    heads_b = lambda a: a.reshape(bsz, t, B_HEADS, B_HEAD_DIM)
    gates = (forget_gates(heads_b(f_fwd), lb[0]), forget_gates(heads_b(f_bwd), lb[1]))
    return qa, ka, va, heads_b(qb), heads_b(ib), heads_b(gb), gates

def ab_mixer_context(h, w_in, w_out, q_gain, k_gain, lb, out_gain):
    qa, ka, va, qb, ib, gb, gates = ab_project(h, w_in, q_gain, k_gain, lb)
    oa = gqa_attend(qa, ka, va)
    s0 = jnp.zeros((h.shape[0], 2, B_HEADS, B_HEAD_DIM, B_HEAD_DIM), jnp.float32)
    ob, s_end = hgrn2_bidirectional(qb, ib, gb, gates, s0, out_gain)
    out = jnp.concatenate([oa, ob], axis=-1) @ w_out
    return out, ka, va, s_end

def ab_mixer_latent(h, w_in, w_out, q_gain, k_gain, lb, out_gain, rope, ctx_k, ctx_v, ctx_state):
    bsz, t, _ = h.shape
    qa, ka, va, qb, ib, gb, gates = ab_project(h, w_in, q_gain, k_gain, lb)
    qa = apply_axial_rope(qa.reshape(bsz, t, A_HEADS, HEAD_DIM), rope)
    qa = qa.reshape(bsz, t, A_KV_HEADS, A_GROUP, HEAD_DIM)
    ka = apply_axial_rope(ka, rope)
    k_all = jnp.concatenate([ctx_k.astype(ka.dtype), ka], axis=1)
    v_all = jnp.concatenate([ctx_v.astype(va.dtype), va], axis=1)
    oa = gqa_attend(qa, k_all, v_all)
    ob, _ = hgrn2_bidirectional(qb, ib, gb, gates, ctx_state, out_gain)
    return jnp.concatenate([oa, ob], axis=-1) @ w_out

def conformer_conv(h, pw1, dw, dw_b, ln_g, ln_b, pw2):
    a, b = jnp.split(h @ pw1, 2, axis=-1)
    u = a * jax.nn.sigmoid(b)
    u = lax.conv_general_dilated(u, dw[:, None, :].astype(u.dtype), window_strides=(1,),
                                 padding=[(CONV_WIDTH // 2, CONV_WIDTH // 2)],
                                 dimension_numbers=("NWC", "WIO", "NWC"),
                                 feature_group_count=CONV_DIM) + dw_b
    u = jax.nn.silu(layer_norm(u, ln_g, ln_b))
    return u @ pw2

def hier_moe(h, w_group, b_group, w_expert, b_expert, w1, w3, w2):
    bsz, t, d = h.shape
    x = h.reshape(bsz * t, d)
    n_tok = x.shape[0]
    p_group = jax.nn.softmax((x @ w_group + b_group).astype(jnp.float32), axis=-1)
    g_val, g_idx = lax.top_k(p_group, 1)
    logits_e = (x @ w_expert + b_expert).astype(jnp.float32).reshape(n_tok, MOE_GROUPS, EXPERTS_PER_GROUP)
    logits_sel = jnp.take_along_axis(logits_e, g_idx[:, :, None], axis=1)[:, 0]
    p_exp = jax.nn.softmax(logits_sel, axis=-1)
    e_val, e_idx = lax.top_k(p_exp, TOP_K)
    e_val = e_val / jnp.sum(e_val, axis=-1, keepdims=True)
    expert_id = g_idx * EXPERTS_PER_GROUP + e_idx
    weight = g_val * e_val
    combine = jnp.sum(jax.nn.one_hot(expert_id, N_EXPERTS, dtype=jnp.float32) * weight[..., None], axis=1)
    hid = jax.nn.silu(jnp.einsum("nd,edf->nef", x, w1)) * jnp.einsum("nd,edf->nef", x, w3)
    y = jnp.einsum("nef,efd->nd", hid * combine[..., None].astype(hid.dtype), w2)
    return y.reshape(bsz, t, d)

def setup_inputs(seed: int = 0) -> dict:
    key = jax.random.key(seed)
    ks = iter(jax.random.split(key, 48))
    f32 = jnp.float32
    nrm = lambda shape, scale: scale * jax.random.normal(next(ks), shape, f32)
    gain = lambda shape: 1.0 + 0.1 * jax.random.normal(next(ks), shape, f32)
    return {
        "x_prompt": nrm((BATCH, SEQ, D_MODEL), 1.0),
        "x_sample": nrm((DEC_BATCH, DEC_SEQ, D_MODEL), 1.0),
        "cache_k": nrm((DEC_BATCH, N_AB_LAYERS, PAST_LEN, A_KV_HEADS, HEAD_DIM), 1.0),
        "cache_v": nrm((DEC_BATCH, N_AB_LAYERS, PAST_LEN, A_KV_HEADS, HEAD_DIM), 1.0),
        "state_hgrn": nrm((DEC_BATCH, N_AB_LAYERS, 2, B_HEADS, B_HEAD_DIM, B_HEAD_DIM), 0.5),
        "c": nrm((DEC_BATCH, D_MODEL), 1.0),
        "c_ctx": nrm((D_MODEL,), 1.0),
        "ada_w": nrm((DEPTH, D_MODEL, 6 * D_MODEL), 0.5 * D_MODEL ** -0.5),
        "ada_b": nrm((DEPTH, 6 * D_MODEL), 0.02),
        "norm1_g": gain((DEPTH, D_MODEL)),
        "norm2_g": gain((DEPTH, D_MODEL)),
        "mix_w_in": nrm((N_AB_LAYERS, D_MODEL, IN_WIDTH), D_MODEL ** -0.5),
        "mix_w_out": nrm((N_AB_LAYERS, MIX_WIDTH, D_MODEL), MIX_WIDTH ** -0.5),
        "attn_q_gain": gain((N_AB_LAYERS, HEAD_DIM)),
        "attn_k_gain": gain((N_AB_LAYERS, HEAD_DIM)),
        "hgrn_lower_bound": nrm((N_AB_LAYERS, 2, B_WIDTH), 0.5),
        "hgrn_out_gain": gain((N_AB_LAYERS, B_HEAD_DIM)),
        "conv_pw1": nrm((N_CONV_LAYERS, D_MODEL, 2 * CONV_DIM), D_MODEL ** -0.5),
        "conv_dw": nrm((N_CONV_LAYERS, CONV_WIDTH, CONV_DIM), CONV_WIDTH ** -0.5),
        "conv_dw_b": nrm((N_CONV_LAYERS, CONV_DIM), 0.02),
        "conv_ln_g": gain((N_CONV_LAYERS, CONV_DIM)),
        "conv_ln_b": nrm((N_CONV_LAYERS, CONV_DIM), 0.02),
        "conv_pw2": nrm((N_CONV_LAYERS, CONV_DIM, D_MODEL), CONV_DIM ** -0.5),
        "moe_w_group": nrm((DEPTH, D_MODEL, MOE_GROUPS), D_MODEL ** -0.5),
        "moe_b_group": nrm((DEPTH, MOE_GROUPS), 0.01),
        "moe_w_expert": nrm((DEPTH, D_MODEL, N_EXPERTS), D_MODEL ** -0.5),
        "moe_b_expert": nrm((DEPTH, N_EXPERTS), 0.01),
        "moe_w1": nrm((DEPTH, N_EXPERTS, D_MODEL, EXPERT_DIM), D_MODEL ** -0.5),
        "moe_w3": nrm((DEPTH, N_EXPERTS, D_MODEL, EXPERT_DIM), D_MODEL ** -0.5),
        "moe_w2": nrm((DEPTH, N_EXPERTS, EXPERT_DIM, D_MODEL), EXPERT_DIM ** -0.5),
        "final_g": gain((D_MODEL,)),
    }

def reference(x_prompt, x_sample, cache_k, cache_v, state_hgrn, c, c_ctx, ada_w, ada_b, norm1_g, norm2_g,
              mix_w_in, mix_w_out, attn_q_gain, attn_k_gain, hgrn_lower_bound, hgrn_out_gain,
              conv_pw1, conv_dw, conv_dw_b, conv_ln_g, conv_ln_b, conv_pw2,
              moe_w_group, moe_b_group, moe_w_expert, moe_b_expert, moe_w1, moe_w3, moe_w2, final_g):
    rope = axial_rope_tables(x_sample.shape[1])
    lb_soft = jax.nn.softmax(hgrn_lower_bound.astype(jnp.float32), axis=0)
    lower_bounds = jnp.cumsum(lb_soft, axis=0) - lb_soft[0]
    xp, xs = x_prompt, x_sample
    new_k, new_v, new_s = [], [], []
    for l in range(DEPTH):
        p_sh1, p_sc1, p_g1, p_sh2, p_sc2, p_g2 = adaln(c_ctx[None, :], ada_w[l], ada_b[l])
        s_sh1, s_sc1, s_g1, s_sh2, s_sc2, s_g2 = adaln(c, ada_w[l], ada_b[l])
        hp = modulate(xp, norm1_g[l], p_sh1, p_sc1)
        hs = modulate(xs, norm1_g[l], s_sh1, s_sc1)
        if l % 2 == 0:
            e = l // 2
            ab_w = (mix_w_in[e], mix_w_out[e], attn_q_gain[e], attn_k_gain[e], lower_bounds[e], hgrn_out_gain[e])
            mp, k_ctx, v_ctx, s_ctx = ab_mixer_context(hp, *ab_w)
            ms = ab_mixer_latent(hs, *ab_w, rope, cache_k[:, e], cache_v[:, e], state_hgrn[:, e])
            new_k.append(k_ctx)
            new_v.append(v_ctx)
            new_s.append(s_ctx)
        else:
            o = l // 2
            cw = (conv_pw1[o], conv_dw[o], conv_dw_b[o], conv_ln_g[o], conv_ln_b[o], conv_pw2[o])
            mp = conformer_conv(hp, *cw)
            ms = conformer_conv(hs, *cw)
        xp = xp + p_g1 * mp
        xs = xs + s_g1 * ms
        mw = (moe_w_group[l], moe_b_group[l], moe_w_expert[l], moe_b_expert[l], moe_w1[l], moe_w3[l], moe_w2[l])
        xp = xp + p_g2 * hier_moe(modulate(xp, norm2_g[l], p_sh2, p_sc2), *mw)
        xs = xs + s_g2 * hier_moe(modulate(xs, norm2_g[l], s_sh2, s_sc2), *mw)
    y_prompt = rms_norm(xp, final_g)
    y_sample = rms_norm(xs, final_g)
    new_cache_k = jnp.stack(new_k, axis=1)
    new_cache_v = jnp.stack(new_v, axis=1)
    new_state_hgrn = jnp.stack(new_s, axis=1)
    return (y_prompt, y_sample, new_cache_k, new_cache_v, new_state_hgrn)


_drawn_inputs = setup_inputs


def setup_inputs(seed=0):
    import zlib

    import numpy as np

    out = dict(_drawn_inputs(seed))
    spreads = {}
    factors = {'cache_k': 4.292,
     'cache_v': 3.914,
     'state_hgrn': 29.397,
     'attn_q_gain': 8.0,
     'conv_dw_b': 6.373,
     'conv_ln_b': 6.978,
     'moe_b_group': 24.121,
     'moe_b_expert': 28.001,
     'conv_ln_g': 2.831,
     'hgrn_out_gain': 2.863}
    for name, (base, spread) in spreads.items():
        noise = np.random.default_rng([zlib.crc32(name.encode()), seed]).standard_normal(out[name].shape)
        drawn = base * np.exp(spread * noise) if base else spread * noise
        out[name] = __import__('jax').numpy.asarray(drawn.astype(out[name].dtype))
    for name, factor in factors.items():
        out[name] = (out[name] * factor).astype(out[name].dtype)
    return out
```

```python
from contextlib import ExitStack

import numpy as np

import concourse.bass as bass
from concourse import mybir

F32 = mybir.dt.float32
F32R = mybir.dt.float32r

ALU = mybir.AluOpType
ACT = mybir.ActivationFunctionType
AX = mybir.AxisListType.X

P = 128
D = 1024
KC = D // P
TOK = 384
NB = TOK // P
GROUPS = ((0, 0, 128), (1, 128, 384))
HD = 64
HEADS = 8
EPS = 1e-6
EXPERTS = 16
TAPS = 31
PAD = TAPS // 2
UW = PAD + 128 + PAD + 256 + PAD
CONV_N = UW - 2 * PAD
RAW = 3
UNITS = 6
AHEAD = 4
LEVELS = 7

SH1, SC1, G1, SH2, SC2, G2 = (KC * i for i in range(6))

CCTX, CC, N1, N2, NF, LB, DWB, LNG, LNB, QG, KG, OG = 0, 8, 16, 32, 48, 56, 64, 72, 80, 88, 89, 90
PROWS = (91, 96, 120, 128)

C_ID, C_ROT, C_COS, C_SIN, C_SEL, C_ONE, C_DESC, C_MASK = 0, 128, 256, 512, 768, 770, 771, 776
C_W = C_MASK + (LEVELS + 1) * P


def shape_constants():
    c = np.zeros((P, C_W), np.float32)
    c[:, C_ID:C_ID + P] = np.eye(P, dtype=np.float32)
    inv = (10000.0 ** (-np.arange(0, 32, 2, dtype=np.float32) / 32)).astype(np.float32)
    t = np.arange(256)
    for p in range(P):
        d = p % 64
        pos = (t // 64 if d < 32 else t % 64).astype(np.float32)
        ang = (pos * inv[d % 16]).astype(np.float32)
        c[p, C_COS:C_COS + 256] = np.cos(ang)
        c[p, C_SIN:C_SIN + 256] = np.sin(ang)
        if d % 32 < 16:
            c[p + 16, C_ROT + p] = -1.0
        else:
            c[p - 16, C_ROT + p] = 1.0
    c[:64, C_SEL] = 1.0
    c[64:, C_SEL + 1] = 1.0
    c[:, C_ONE] = 1.0
    c[:, C_DESC:C_DESC + 4] = [4.0, 3.0, 2.0, 1.0]
    c[:, C_MASK:] = level_masks()
    return c


def level_masks():
    m = np.zeros((P, LEVELS + 1, P), np.float32)
    j, i = np.meshgrid(np.arange(P), np.arange(P), indexing="ij")
    m[:, 0] = j == i
    for l in range(1, LEVELS + 1):
        h = 1 << (l - 1)
        m[:, l] = (j // (2 * h) == i // (2 * h)) & (j // h != i // h)
    return m.reshape(P, (LEVELS + 1) * P)


IN_ORDER = [5, 6, 7, 8, 3, 4, 9, 10, 0, 1, 2, 11, 12]
N_IN = 2 * len(IN_ORDER)
GRAM_AFTER = {13 + l: l for l in range(LEVELS + 1)}
X_AFTER = {12 + l: l for l in range(1, LEVELS + 1)}
VAT_Q = 2 * IN_ORDER.index(2) + 1


def expert_slots(layer):
    s = [("w1", layer, 0), ("w3", layer, 0)]
    for e in range(1, EXPERTS):
        s += [("w1", layer, e), ("w3", layer, e), ("w2", layer, e - 1)]
    return s + [("w2", layer, EXPERTS - 1)]


def plan_slots():
    ada = [("ada", l, j) for l in range(2) for j in range(24)]
    plan, ada = ada[:8], ada[8:]
    for j in IN_ORDER:
        plan += [("in", 0, j), ada.pop(0)]
    plan += ada + [("out", 0, j) for j in range(4)]
    p1 = [("pw1", 0, j) for a in range(4) for j in (a, a + 4)] + [("pw2", 0, j) for j in range(4)]
    bases = (len(plan), len(plan) + 3 * EXPERTS, len(plan) + 3 * EXPERTS + len(p1))
    return plan + expert_slots(0) + p1 + expert_slots(1), bases


def plan_units(slots):
    units, freed, n_ada, n = [], [None] * len(slots), 0, 0
    while n < len(slots):
        kind = slots[n][0]
        if kind == "ada":
            n_ada += 1
            freed[n] = ("ada_used", n_ada)
            n += 1
        elif kind in ("w1", "pw1"):
            for half in range(2):
                for z in range(2):
                    units.append((n + z, half, False))
                    freed[n + z] = ("lo_done", len(units))
            n += 2
        else:
            for half in range(2):
                units.append((n, half, kind == "w2"))
            freed[n] = ("lo_done", len(units))
            n += 1
    return units, freed


SLOTS, (B_MOE0, B_P1, B_MOE1) = plan_slots()
UNIT, FREED = plan_units(SLOTS)
U_OUT = N_IN
U_MOE0 = U_OUT + 8
U_PW1 = U_MOE0 + 6 * EXPERTS
U_PW2 = U_PW1 + 16
U_MOE1 = U_PW2 + 8
U_END = U_MOE1 + 6 * EXPERTS
assert len(UNIT) == U_END

ITEMS = [(b, n) for b in range(NB) for n in range(HEADS)]
UPDATES = [(True, 1), (False, 2), (True, 0), (False, 0)]
Z_LEN = 17792
BLK = (0, PAD + 128, PAD + 256)


def build(nc, A):
    with ExitStack() as ctx:
        sems = {}

        def S(name):
            if name not in sems:
                sems[name] = ctx.enter_context(nc.semaphore(name))
            return sems[name]

        def ge(eng, name, v):
            if isinstance(v, int) and v <= 0:
                return
            eng.wait_ge(S(name), v)

        def sb(name, shape, dt=F32):
            return ctx.enter_context(nc.sbuf_tensor(name, shape, dt))

        ps = ctx.enter_context(nc.psum_tensor("ps", [P, 8 * 512], F32))

        def bank(b, n=512, o=0):
            return ps[:, b * 512 + o:b * 512 + o + n]

        raw = sb("raw", [P, RAW, 2048])
        whi = sb("whi", [P, UNITS, 1024], F32R)
        wlo = sb("wlo", [P, UNITS, 1024], F32R)
        xT = sb("xT", [P, KC, TOK])
        hf = sb("hf", [P, KC * TOK])
        hhi = sb("hhi", [P, KC, TOK], F32R)
        hlo = sb("hlo", [P, KC, TOK], F32R)
        hidhi = sb("hidhi", [P, 2, 2, TOK], F32R)
        hidlo = sb("hidlo", [P, 2, 2, TOK], F32R)
        con = sb("con", [P, C_W])
        pcol = sb("pcol", [P, 4, P])
        scond = sb("scond", [P, KC, 2])
        mod = sb("mod", [P, 2, 48, 2])
        amp = sb("amp", [P, 4, KC, 2])
        lbw = sb("lbw", [P, 5, 8])
        wr = sb("wr", [P, 2, KC, 20])
        rb = sb("rb", [P, 2, 20])
        std = sb("std", [P, 32])
        rstd = sb("rstd", [P, 32])
        totc = sb("totc", [P, 2, 4, NB])
        send = sb("send", [P, 2, 4, HD])
        ck = sb("ck", [P, 2, 2, HD])
        nmax = sb("nmax", [P, len(ITEMS)])
        rsum = sb("rsum", [P, 2, len(ITEMS)])
        Z = sb("Z", [P, Z_LEN])
        ident = con[:, C_ID:C_ID + P]
        ones = con[:, C_ONE:C_ONE + 1]
        mask = con[:, C_MASK:].rearrange("p (l i) -> p l i", i=P).bitcast(mybir.dt.uint32)
        hfk = hf[:, :].rearrange("p (k t) -> p k t", k=KC)

        xtok = Z[:, 0:3072].rearrange("p (b d) -> p b d", b=NB)
        prow = Z[:, 3072:3584].rearrange("p (g r) -> p g r", g=4)
        QQ, QP = Z[:, 0:1536], Z[:, 1536:3072]
        KS, KR = Z[:, 3072:4608], Z[:, 4608:6144]
        Xs = [Z[:, 6144:7680], Z[:, 7680:9216]]
        q_t = Z[:, 9216:10752]
        v_t = Z[:, 10752:12288].rearrange("p (b d) -> p b d", b=NB)
        AT = Z[:, 12288:15360].rearrange("p (b n i) -> p b n i", b=NB, n=HEADS)
        qk = Z[:, 15360:17280].rearrange("p (c t) -> p c t", c=5)
        vat = Z[:, 17280:17792].rearrange("p (b d) -> p b d", b=4)
        ff, fb = hf[:, 0:1536], hf[:, 1536:3072]
        sgb = q_t.rearrange("p (c t) -> p c t", c=4)
        KT = [Z[:, 6144 + 512 * g:6656 + 512 * g] for g in range(4)]
        kall = Z[:, 8192:9216].rearrange("p (h t) -> p h t", h=2)
        Sbd = hf[:, 0:2048].rearrange("p (s c e) -> p s c e", s=4, c=4)
        o_f, osq = Z[:, 3072:4608], Z[:, 4608:6144]
        o_t = o_f.rearrange("p (c t) -> p c t", c=4)
        qsq = Z[:, 0:1920].rearrange("p (c t) -> p c t", c=5)
        kout = Z[:, 1920:2048]
        prob = [Z[:, 2048 + TOK * z:2048 + TOK * (z + 1)] for z in range(2)]
        rsx = Z[:, 12288:14208].rearrange("p (n d) -> p n d", d=HD)
        PT = [Z[:, 14208 + TOK * z:14208 + TOK * (z + 1)] for z in range(2)]
        comb = Z[:, 0:6144]
        acc = Z[:, 6144:9216].rearrange("p (c t) -> p c t", c=KC)
        sact = Z[:, 9216:9984].rearrange("p (c t) -> p c t", c=2)
        tact = Z[:, 9984:10752].rearrange("p (c t) -> p c t", c=2)
        combT = Z[0:16, 10752:11136]
        rt = Z[:, 11136:12288].rearrange("p (s b n) -> p s b n", s=24, b=NB)
        upad = Z[:, 0:3432].rearrange("p (c t) -> p c t", c=KC)
        cacc = Z[:, 3432:6624].rearrange("p (c t) -> p c t", c=KC)
        usig = Z[:, 6624:7392].rearrange("p (c t) -> p c t", c=2)
        cen = Z[:, 7392:10464].rearrange("p (c t) -> p c t", c=KC)
        ytok = Z[:, 0:3072].rearrange("p (b d) -> p b d", b=NB)

        comb_dram = nc.dram_tensor("comb_scratch", [2, EXPERTS * TOK], F32, kind="Internal").ap()

        raw_k = lambda r: raw[:, r, :].rearrange("p (k n) -> p k n", k=KC)
        raw_2 = lambda r: raw[:, r, :].rearrange("p (k n) -> p k n", k=2)

        def raw_unit(n, half, down):
            return raw_2(n % RAW)[:, :, 512 * half:512 * half + 512] if down \
                else raw_k(n % RAW)[:, :, 128 * half:128 * half + 128]

        def unit_view(t, u, down):
            return t[:, u % UNITS, :].rearrange("p (k n) -> p k n", k=2 if down else KC)

        block = ctx.enter_context(nc.Block())

        @block.sync
        def _(sp):
            def load(n, dst, src):
                sp.dma_start(dst, src).then_inc(S(f"raw_full{n % RAW}"), 16)

            def fetch(n, what, where, j):
                if what in ("w1", "w3", "w2"):
                    src = A["moe_" + what][where, j].rearrange("(k p) n -> p k n", p=P)
                    load(n, raw_2(n % RAW) if what == "w2" else raw_k(n % RAW), src)
                else:
                    w = {"ada": A["ada_w"], "in": A["mix_w_in"], "out": A["mix_w_out"],
                         "pw1": A["conv_pw1"], "pw2": A["conv_pw2"]}[what][where]
                    load(n, raw_k(n % RAW), w[:, 256 * j:256 * j + 256].rearrange("(k p) n -> p k n", p=P))

            def static(a, b):
                for n in range(a, b):
                    if n >= RAW:
                        name, v = FREED[n - RAW]
                        sp.wait_ge(S(name), v)
                    fetch(n, *SLOTS[n])

            for layer, first, base in ((0, 0, B_MOE0), (1, B_P1, B_MOE1)):
                static(first, base + 5)
                with sp.Fori(0, 7) as i:
                    for j in range(6):
                        n = base + 5 + j
                        what, _, e = SLOTS[n]
                        sp.wait_ge(S("lo_done"), 12 * i + FREED[n - RAW][1])
                        fetch(n, what, layer, 2 * i + e)
                static(base + 47, base + 48)
            sp.wait_ge(S("out_kv"), 32)
            sp.wait_ge(S("out_state"), 64)
            sp.wait_ge(S("out_y"), 48)
            sp.wait_ge(S("comb_stored"), 32)

        @block.gpsimd
        def _(pool):
            def lo(u, value):
                n, half, down = UNIT[u]
                pool.wait_ge(S("hi_done"), value)
                nc.gpsimd.tensor_tensor(unit_view(wlo, u, down), raw_unit(n, half, down),
                                        unit_view(whi, u, down).bitcast(F32), ALU.subtract)\
                    .then_inc(S("lo_done"), 1)

            for first, base in ((0, U_MOE0), (U_MOE0 + 94, U_MOE1)):
                for u in range(first, base + 10):
                    lo(u, u + 1)
                with pool.Fori(0, 7) as i:
                    for j in range(12):
                        lo(base + 10 + j, 12 * i + (base + 11 + j))
            for u in range(U_MOE1 + 94, U_END):
                lo(u, u + 1)

        @block.scalar
        def _(act):
            def hi(u, i=None):
                if u >= U_END:
                    return
                n, half, down = UNIT[u]
                full, used = 16 * (n // RAW + 1), u - UNITS + 1
                act.wait_ge(S(f"raw_full{n % RAW}"), full if i is None else 32 * i + full)
                ge(act, "unit_used", used if i is None else 12 * i + used)
                nc.scalar.activation(unit_view(whi, u, down), raw_unit(n, half, down), ACT.Copy)\
                    .then_inc(S("hi_done"), 1)

            rows = [(0, CCTX, 8, A["c_ctx"].rearrange("(k p) -> k p", p=P)),
                    (0, CC, 8, A["c"][0].rearrange("(k p) -> k p", p=P)),
                    (0, N1, 16, A["norm1_g"].rearrange("l (k p) -> (l k) p", p=P)),
                    (0, N2, 16, A["norm2_g"].rearrange("l (k p) -> (l k) p", p=P)),
                    (0, NF, 8, A["final_g"].rearrange("(k p) -> k p", p=P)),
                    (0, LB, 8, A["hgrn_lower_bound"][0].rearrange("z (k p) -> (z k) p", p=P)),
                    (0, DWB, 8, A["conv_dw_b"][0].rearrange("(k p) -> k p", p=P)),
                    (0, LNG, 8, A["conv_ln_g"][0].rearrange("(k p) -> k p", p=P)),
                    (0, LNB, 8, A["conv_ln_b"][0].rearrange("(k p) -> k p", p=P)),
                    (1, 0, 96, A["ada_b"].rearrange("l (k p) -> (l k) p", p=P)),
                    (2, 0, 120, A["conv_dw"][0, 0:15].rearrange("t (k p) -> (t k) p", p=P)),
                    (3, 0, 128, A["conv_dw"][0, 15:31].rearrange("t (k p) -> (t k) p", p=P))]
            act.dma_start(con[:, :], A["shape_constants"]).then_inc(S("in_con"), 16)
            for g, r, n, src in rows:
                act.dma_start(prow[r:r + n, g, :], src).then_inc(S("in_rows"), 16)
            for r, name in ((QG, "attn_q_gain"), (KG, "attn_k_gain"), (OG, "hgrn_out_gain")):
                for z in range(2):
                    act.dma_start(prow[r:r + 1, 0, HD * z:HD * z + HD], A[name]).then_inc(S("in_rows"), 16)
            act.dma_start(xtok[:, 0, :], A["x_prompt"][0]).then_inc(S("in_x"), 16)
            for b in range(2):
                act.dma_start(xtok[:, 1 + b, :], A["x_sample"][0, P * b:P * b + P, :]).then_inc(S("in_x"), 16)
            for l in range(2):
                act.dma_start(wr[:, l, :, 0:4], A["moe_w_group"][l].rearrange("(k p) g -> p k g", p=P)).then_inc(S("in_small"), 16)
                act.dma_start(wr[:, l, :, 4:20], A["moe_w_expert"][l].rearrange("(k p) g -> p k g", p=P)).then_inc(S("in_small"), 16)
                act.dma_start(rb[:, l, 0:4], A["moe_b_group"][l].partition_broadcast(P)).then_inc(S("in_small"), 16)
                act.dma_start(rb[:, l, 4:20], A["moe_b_expert"][l].partition_broadcast(P)).then_inc(S("in_small"), 16)
            for z in range(2):
                act.dma_start(ck[:, :, z, :], A["cache_k"][0, 0]).then_inc(S("in_small"), 16)

            act.wait_ge(S("pcol_ready"), 4)
            nc.scalar.activation(scond[:, :, :].rearrange("p k g -> p g k"),
                                 pcol[:, 0, 0:16].rearrange("p (g k) -> p g k", g=2), ACT.Silu)\
                .then_inc(S("scond_ready"), 1)
            act.wait_ge(S("lb_shifted"), 1)
            nc.scalar.activation(lbw[:, 1, :], lbw[:, 0, :], ACT.Exp).then_inc(S("lb_exp"), 1)

            def norm_act(n):
                for k in range(KC):
                    if n == 0:
                        act.wait_ge(S("xT_ready"), k + 1)
                    elif k == 0:
                        act.wait_ge(S("x_new"), n)
                    nc.scalar.activation(hfk[:, k, :], xT[:, k, :], ACT.Square).then_inc(S("sq_ready"), 1)
                act.wait_ge(S("ssum_ready"), n + 1)
                nc.scalar.activation(std[:, 0:3], bank(3, 3), ACT.Sqrt, scale=1.0 / D, bias=EPS).then_inc(S("std_ready"), 1)

            def split_h(n):
                for k in range(KC):
                    act.wait_ge(S("hf_ready"), KC * n + k + 1)
                    nc.scalar.activation(hhi[:, k, :], hfk[:, k, :], ACT.Copy).then_inc(S("hhi_ready"), 1)

            norm_act(0)
            split_h(0)
            for u in range(AHEAD):
                hi(u)

            for q in range(N_IN):
                b, slot, half = q % 3, IN_ORDER[q // 2], q % 2
                done = S(f"pb_free{b}")
                act.wait_ge(S("unit_used"), q + 1)
                if slot in (5, 6, 7, 8):
                    c = (slot - 5) * 2 + half
                    if q == 0:
                        act.wait_ge(S("hlo_ready"), KC)
                    nc.scalar.activation(hfk[:, c, :], bank(b, TOK), ACT.Sigmoid).then_inc(done, 1)
                elif slot in (3, 4):
                    c = (slot - 3) * 2 + half
                    nc.scalar.activation(q_t[:, c * TOK:(c + 1) * TOK], bank(b, TOK), ACT.Copy).then_inc(done, 1)
                elif slot in (9, 10):
                    c = (slot - 9) * 2 + half
                    nc.scalar.activation(v_t[:, :, c * P:(c + 1) * P], bank(b, TOK).rearrange("p (b d) -> p b d", b=NB),
                                         ACT.Copy).then_inc(done, 1)
                elif slot in (0, 1):
                    nc.scalar.activation(qk[:, slot * 2 + half, :], bank(b, TOK), ACT.Copy).then_inc(done, 1)
                elif slot == 2 and half == 0:
                    nc.scalar.activation(qk[:, 4, :], bank(b, TOK), ACT.Copy).then_inc(done, 1)
                elif slot == 2:
                    nc.scalar.activation(vat[:, 0, :], bank(b, P), ACT.Copy).then_inc(S("vat_prompt"), 1)
                    nc.scalar.activation(vat[:, 2:4, :], bank(b, 256, P).rearrange("p (b d) -> p b d", b=2),
                                         ACT.Copy).then_inc(done, 1)
                else:
                    if q == N_IN - 4:
                        act.wait_ge(S("gram_done"), NB)
                        act.wait_ge(S("qinit_done"), 2)
                    nc.scalar.activation(sgb[:, (slot - 11) * 2 + half, :], bank(b, TOK), ACT.Silu).then_inc(done, 1)
                if q + AHEAD < N_IN:
                    hi(q + AHEAD)
                if q in X_AFTER:
                    l = X_AFTER[q]
                    h = 1 << (l - 1)
                    halves = lambda t: t.rearrange("p (n z h) -> p n z h", z=2, h=h)
                    act.wait_ge(S("k_ready"), 8)
                    ge(act, "ks_level", 2 * (l - 1))
                    ge(act, "gram_done", NB * (l - 1))
                    nc.scalar.activation(halves(Xs[l % 2])[:, :, 0, :], halves(KS)[:, :, 0, :], ACT.Copy).then_inc(S("x_lower"), 1)
                    nc.scalar.activation(halves(Xs[l % 2])[:, :, 1, :], halves(KR)[:, :, 1, :], ACT.Copy).then_inc(S("x_ready"), 1)

            act.wait_ge(S("vat_prompt"), 1)
            act.dma_start(A["out3"][0, 0].rearrange("t h d -> t (h d)"), vat[:, 0, :]).then_inc(S("out_kv"), 16)
            act.dma_start(vat[:, 1, :], A["cache_v"][0, 0].rearrange("t h d -> t (h d)")).then_inc(S("in_cv"), 16)
            act.wait_ge(S("sbd_zero"), 1)
            for which, way in ((0, 0), (2, 1)):
                for z in range(2):
                    act.dma_start(Sbd[HD * z:HD * z + HD, which, :, HD * z:HD * z + HD],
                                  A["state_hgrn"][0, 0, way].rearrange("(c z) d e -> z d c e", z=2)[z])\
                       .then_inc(S("in_state"), 16)
            for g in range(4):
                act.wait_ge(S("kt_T"), g + 1)
                nc.scalar.activation(KT[g], bank(3 + g % 2), ACT.Copy).then_inc(S("kt_ready"), 1)
            act.wait_ge(S("state_ready"), 8)
            for way in range(2):
                for z in range(2):
                    act.dma_start(A["out4"][0, 0, way].rearrange("(c z) d e -> z d c e", z=2)[z],
                                  send[HD * z:HD * z + HD, way, :, :]).then_inc(S("out_state"), 16)
            act.wait_ge(S("ckT_ready"), 1)
            nc.scalar.activation(kall[:, :, 128:256], bank(5, 256).rearrange("p (h t) -> p h t", h=2), ACT.Copy)\
                .then_inc(S("kcache_ready"), 1)
            for b in range(NB):
                act.wait_ge(S("o_full"), b + 1)
                nc.scalar.activation(o_t[:, :, P * b:P * b + P], bank(b).rearrange("p (c t) -> p c t", c=4), ACT.Copy)\
                    .then_inc(S("o_copied"), 1)
            act.wait_ge(S("o_copied"), NB)
            nc.scalar.activation(osq, o_f, ACT.Square).then_inc(S("osq_ready"), 1)
            act.wait_ge(S("osum_ready"), 1)
            nc.scalar.activation(std[:, 0:24], bank(3, 24), ACT.Sqrt, scale=1.0 / HD, bias=EPS).then_inc(S("ostd_ready"), 1)
            nc.scalar.activation(qsq, qk, ACT.Square).then_inc(S("qsq_ready"), 1)
            for c in range(4):
                act.wait_ge(S("of_ready"), c + 1)
                nc.scalar.activation(hhi[:, 4 + c, :], o_t[:, c, :], ACT.Copy).then_inc(S("obhi_ready"), 1)
            act.wait_ge(S("qsum_ready"), 1)
            nc.scalar.activation(std[:, 0:30], bank(3, 30), ACT.Sqrt, scale=1.0 / HD, bias=EPS).then_inc(S("qstd_ready"), 1)
            act.wait_ge(S("kout_T"), 1)
            nc.scalar.activation(kout, bank(6, P), ACT.Copy).then_inc(S("kout_ready"), 1)
            act.wait_ge(S("kout_ready"), 1)
            act.dma_start(A["out2"][0, 0].rearrange("t h d -> t (h d)"), kout).then_inc(S("out_kv"), 16)
            act.wait_ge(S("roped"), 5)
            for kv in range(2):
                for z in range(2):
                    for s0, s1, d0 in ((0, 128, 0), (128, 384, 256)):
                        act.dma_start(kall[HD * z:HD * z + HD, kv, d0:d0 + s1 - s0],
                                      qk[HD * kv:HD * kv + HD, 4, s0:s1]).then_inc(S("kall_ready"), 16)

            for i in range(len(ITEMS) + 1):
                if i < len(ITEMS):
                    w = P if ITEMS[i][0] == 0 else TOK
                    act.wait_ge(S("nmax_ready"), i + 1)
                    ge(act, "pT_done", i - 1)
                    nc.scalar.activation(prob[i % 2][:, 0:w], bank(3 + i % 2, w), ACT.Exp, bias=nmax[:, i:i + 1],
                                         accum_out=rsum[:, 0, i:i + 1]).then_inc(S("prob_ready"), 1)
                if i >= 1:
                    w = P if ITEMS[i - 1][0] == 0 else TOK
                    act.wait_ge(S("pT_done"), i)
                    ge(act, "pv_done", i - 2)
                    nc.scalar.activation(PT[(i - 1) % 2][:, 0:w], bank(5 + (i - 1) % 2, w), ACT.Copy).then_inc(S("PT_ready"), 1)
                if i in (9, 17, 24):
                    b = {9: 0, 17: 1, 24: 2}[i]
                    act.wait_ge(S("pv_done"), 8 * b + 8)
                    nc.scalar.activation(hhi[:, 0:4, P * b:P * b + P], bank(b).rearrange("p (c t) -> p c t", c=4),
                                         ACT.Copy).then_inc(S("oahi_ready"), 1)

            for u in range(U_OUT, U_OUT + AHEAD):
                hi(u)
            for j in range(8):
                act.wait_ge(S("unit_used"), U_OUT + j + 1)
                hi(U_OUT + j + AHEAD)

            def experts(layer, U0):
                C0 = EXPERTS * layer

                def silu(e, u, f):
                    act.wait_ge(S("unit_used"), u + 2 * f + 1)
                    ge(act, "hmul_done", 2 * (e + C0 - 1) + f + 1)
                    nc.scalar.activation(sact[:, f, :], bank(2 * f, TOK), ACT.Silu).then_inc(S("silu_ready"), 1)

                def hid(e, par, f):
                    act.wait_ge(S("tact_ready"), 2 * (e + C0) + f + 1)
                    nc.scalar.activation(hidhi[:, par, f, :], tact[:, f, :], ACT.Copy).then_inc(S("hidhi_ready"), 1)

                def up(e, u, par, split):
                    silu(e, u, 0)
                    split(0)
                    split(1)
                    hid(e, par, 0)
                    silu(e, u, 1)
                    split(2)
                    split(3)
                    hid(e, par, 1)

                act.wait_ge(S("rt_group"), layer + 1)
                nc.scalar.activation(rt[:, 2, :, 0:4], rt[:, 1, :, 0:4], ACT.Exp).then_inc(S("rt_exp"), 1)
                act.wait_ge(S("rt_second"), layer + 1)
                nc.scalar.activation(rt[:, 13, :, 0:1], rt[:, 12, :, 0:1], ACT.Exp).then_inc(S("rt_exp"), 1)
                act.wait_ge(S("combT_ready"), layer + 1)
                act.dma_start(comb_dram[layer].rearrange("(e t) -> e t", e=EXPERTS), combT).then_inc(S("comb_stored"), 16)
                act.wait_ge(S("comb_stored"), 16 * layer + 16)
                act.dma_start(comb, comb_dram[layer].partition_broadcast(P)).then_inc(S("comb_ready"), 16)

                up(0, U0, 0, lambda j: hi(U0 + j + AHEAD))
                up(1, U0 + 4, 1, lambda j: hi(U0 + 4 + j + AHEAD))
                hi(U0 + 8 + AHEAD)
                hi(U0 + 9 + AHEAD)
                with act.Fori(0, 6) as i:
                    for z in range(2):
                        ub = U0 + 10 + 6 * z
                        split = lambda j, ub=ub: hi(ub + j + AHEAD, i)
                        up(2 * i + (2 + z), 12 * i + ub, z, split)
                        split(4)
                        split(5)
                for z in range(2):
                    ub = U0 + 82 + 6 * z
                    split = lambda j, ub=ub: hi(ub + j + AHEAD)
                    up(14 + z, ub, z, split)
                    split(4)
                    split(5)
                hi(U0 + 94 + AHEAD)
                hi(U0 + 95 + AHEAD)

            norm_act(1)
            split_h(1)
            experts(0, U_MOE0)

            norm_act(2)
            split_h(2)
            for j in range(16):
                u = U_PW1 + j
                act.wait_ge(S("unit_used"), u + 1)
                if j % 2:
                    g = j // 2
                    ge(act, "u_ready", 2 * (g - 1))
                    nc.scalar.activation(usig[:, g % 2, :], bank(j % 4, TOK), ACT.Sigmoid).then_inc(S("usig_ready"), 1)
                hi(u + AHEAD)
            act.wait_ge(S("csum_ready"), 1)
            nc.scalar.activation(std[:, 0:3], bank(3, 3), ACT.Copy, scale=1.0 / D).then_inc(S("cmean_ready"), 1)
            act.wait_ge(S("cen_ready"), 1)
            nc.scalar.activation(hfk[:, :, :], cen, ACT.Square).then_inc(S("csq_ready"), 1)
            act.wait_ge(S("cvar_ready"), 1)
            nc.scalar.activation(std[:, 3:6], bank(3, 3), ACT.Sqrt, scale=1.0 / D, bias=EPS).then_inc(S("cstd_ready"), 1)
            for k in range(KC):
                act.wait_ge(S("cn_ready"), k + 1)
                nc.scalar.activation(hfk[:, k, :], cen[:, k, :], ACT.Silu, scale=pcol[:, 0, LNG + k:LNG + k + 1],
                                     bias=pcol[:, 0, LNB + k:LNB + k + 1]).then_inc(S("cs_ready"), 1)
                act.wait_ge(S("cs_ready"), k + 1)
                nc.scalar.activation(hhi[:, k, :], hfk[:, k, :], ACT.Copy).then_inc(S("chi_ready"), 1)
            for j in range(8):
                act.wait_ge(S("unit_used"), U_PW2 + j + 1)
                hi(U_PW2 + j + AHEAD)
            norm_act(3)
            split_h(3)
            experts(1, U_MOE1)

            norm_act(4)
            for i in range(2 * NB):
                b, h = i // 2, i % 2
                act.wait_ge(S("yT_ready"), i + 1)
                nc.scalar.activation(ytok[:, b, 512 * h:512 * h + 512], bank(5 + i % 2), ACT.Copy).then_inc(S("ytok_ready"), 1)
                if h:
                    act.wait_ge(S("ytok_ready"), i + 1)
                    dst = A["out0"][0] if b == 0 else A["out1"][0, P * (b - 1):P * b, :]
                    act.dma_start(dst, ytok[:, b, :]).then_inc(S("out_y"), 16)

        @block.vector
        def _(dve):
            V = nc.vector
            count = [0]

            def link(ins, back=0):
                count[0] += 1
                ins.then_inc(S("dve_link"), 1)
                ge(dve, "dve_link", count[0] - back)

            def mul(out, a, b):
                return V.tensor_tensor(out, a, b, ALU.mult)

            for g in range(4):
                dve.wait_ge(S("prow_T"), 4)
                V.tensor_copy(pcol[:, g, 0:PROWS[g]], bank(7, PROWS[g], P * g)).then_inc(S("pcol_ready"), 1)
            dve.wait_ge(S("pcol_ready"), 4)
            lbs = pcol[:, 0, LB:LB + 8]
            V.tensor_tensor(lbw[:, 0, :], lbs, lbs, ALU.subtract).then_inc(S("lb_shifted"), 1)
            link(V.tensor_scalar_mul(pcol[:, 0, QG:QG + 1], pcol[:, 0, QG:QG + 1], HD ** -0.5))
            dve.wait_ge(S("lb_exp"), 1)
            link(V.reciprocal(lbw[:, 2, :], lbw[:, 1, :]))
            link(mul(lbw[:, 3, :], lbw[:, 1, :], lbw[:, 2, :]))
            link(V.tensor_tensor(lbw[:, 3, :], lbw[:, 3, :], lbw[:, 3, :], ALU.subtract))
            link(V.tensor_scalar(lbw[:, 4, :], lbw[:, 3, :], -1.0, 1.0, ALU.mult, ALU.add))
            for k in range(KC):
                dve.wait_ge(S("x_T"), k + 1)
                V.tensor_copy(xT[:, k, :], bank(3 + k % 4, TOK)).then_inc(S("xT_ready"), 1)

            def modulation(l, c0, c1):
                link(V.tensor_tensor(mod[:, l, c0:c1, :], bank(7, 2 * (c1 - c0), 96 * l + 2 * c0)
                                     .rearrange("p (c g) -> p c g", g=2),
                                     pcol[:, 1, 48 * l + c0:48 * l + c1].unsqueeze(2).broadcast_to([P, c1 - c0, 2]),
                                     ALU.add))

            def amplitude(m, l, sc, gain):
                link(V.tensor_scalar_add(amp[:, m, :, :], mod[:, l, sc:sc + KC, :], 1.0))
                link(mul(amp[:, m, :, :], amp[:, m, :, :],
                         pcol[:, 0, gain:gain + KC].unsqueeze(2).broadcast_to([P, KC, 2])))

            def inv_std(n):
                dve.wait_ge(S("std_ready"), n + 1)
                V.reciprocal(rstd[:, 0:3], std[:, 0:3]).then_inc(S("rstd_ready"), 1)

            def modulate(n, l, sh):
                dve.wait_ge(S("rbc_ready"), n + 1)

                def lo_part(k):
                    dve.wait_ge(S("hhi_ready"), KC * n + k + 1)
                    V.tensor_tensor(hlo[:, k, :], hfk[:, k, :], hhi[:, k, :].bitcast(F32), ALU.subtract)\
                        .then_inc(S("hlo_ready"), 1)
                for k in range(KC):
                    link(mul(hfk[:, k, :], xT[:, k, :], bank(4, TOK)))
                    for g, t0, t1 in GROUPS:
                        ins = V.tensor_scalar(hfk[:, k, t0:t1], hfk[:, k, t0:t1], amp[:, n, k, g:g + 1],
                                              mod[:, l, sh + k, g:g + 1], ALU.mult, ALU.add)
                        if g == 0:
                            ins.then_inc(S("hf_part"), 1)
                        else:
                            ins.then_inc(S("hf_ready"), 1)
                    if k:
                        lo_part(k - 1)
                lo_part(KC - 1)

            inv_std(0)
            dve.wait_ge(S("ada_used"), 8)
            modulation(0, 0, 16)
            amplitude(0, 0, SC1, N1)
            modulate(0, 0, SH1)

            for c in range(8):
                z, cc = c // 4, c % 4
                g = hfk[:, c, :]
                dve.wait_ge(S(f"pb_free{c % 3}"), c // 3 + 1)
                link(V.tensor_scalar(g, g, lbw[:, 4, c:c + 1], lbw[:, 3, c:c + 1], ALU.mult, ALU.add))
                V.tensor_scalar((KS, KR)[z][:, cc * TOK:(cc + 1) * TOK], g, -1.0, 1.0, ALU.mult, ALU.add)\
                    .then_inc(S("k_ready"), 1)
            for q in range(8, 12):
                dve.wait_ge(S(f"pb_free{q % 3}"), q // 3 + 1)
            mul(QP, q_t, ff).then_inc(S("qinit_done"), 1)
            mul(QQ, q_t, fb).then_inc(S("qinit_done"), 1)

            dve.wait_ge(S("in_con"), 16)
            for l in range(LEVELS + 1):
                if l:
                    h = 1 << (l - 1)
                    nb = 1536 // (2 * h)
                    halves = lambda t: t.rearrange("p (n z h) -> p n z h", z=2, h=h)
                    tot = lambda t, z: halves(t)[:, :, z, h - 1:h]
                    wide = lambda t, z: tot(t, z).broadcast_to([P, nb, h])
                    dve.wait_ge(S("x_ready"), l)
                    ge(dve, "ks_level", 2 * (l - 1))
                    mul(halves(KS)[:, :, 0, :], halves(KS)[:, :, 0, :], wide(ff, 1)).then_inc(S("ks_level"), 1)
                    mul(halves(KR)[:, :, 1, :], halves(KR)[:, :, 1, :], wide(fb, 0)).then_inc(S("ks_level"), 1)
                for b in range(NB):
                    i = NB * l + b
                    dve.wait_ge(S("gram_done"), i + 1)
                    V.copy_predicated(AT[:, b, :, :], mask[:, l, :].unsqueeze(1).broadcast_to([P, HEADS, P]),
                                      bank(3 + 2 * (i % 2), 1024).rearrange("p (n i) -> p n i", n=HEADS))\
                        .then_inc(S("gram_copied"), 1)
                if l:
                    dve.wait_ge(S("gram_done"), NB * (l + 1))
                    ge(dve, "q_level", 2 * (l - 1))
                    mul(halves(QP)[:, :, 1, :], halves(QP)[:, :, 1, :], wide(ff, 0)).then_inc(S("q_level"), 1)
                    mul(halves(QQ)[:, :, 0, :], halves(QQ)[:, :, 0, :], wide(fb, 1)).then_inc(S("q_level"), 1)
                    dve.wait_ge(S("ks_level"), 2 * l)
                    dve.wait_ge(S("q_level"), 2 * l)
                    mul(tot(ff, 1), tot(ff, 1), tot(ff, 0)).then_inc(S("tot_level"), 1)
                    link(mul(tot(fb, 1), tot(fb, 1), tot(fb, 0)))
            blocks = lambda t: t.rearrange("p (c b t) -> p c b t", c=4, b=NB)[:, :, :, P - 1]
            dve.wait_ge(S("tot_level"), LEVELS)
            V.tensor_copy(totc[:, 0, :, :], blocks(ff)).then_inc(S("totc_ready"), 1)
            link(V.tensor_copy(totc[:, 1, :, :], blocks(fb)))
            V.memset(hf[:, 0:2048], 0.0).then_inc(S("sbd_zero"), 1)

            dve.wait_ge(S("in_state"), 64)
            for g, (fwd, b) in enumerate(UPDATES):
                dve.wait_ge(S("u_full"), g + 1)
                for z in range(2):
                    r = slice(HD * z, HD * z + HD)
                    U = bank(5 + g % 2).rearrange("p (c e) -> p c e", c=4)[r, :, HD * z:HD * z + HD]
                    if g < 2:
                        src, dst = (0, 1) if fwd else (2, 3)
                        w = 0 if fwd else 1
                        link(mul(Sbd[r, dst, :, HD * z:HD * z + HD], Sbd[r, src, :, HD * z:HD * z + HD],
                                 totc[r, w, :, b:b + 1].broadcast_to([HD, 4, HD])))
                        V.tensor_tensor(Sbd[r, dst, :, HD * z:HD * z + HD], U, Sbd[r, dst, :, HD * z:HD * z + HD], ALU.add)\
                            .then_inc(S("state_ready"), 1)
                    else:
                        V.tensor_copy(send[r, g - 2, :, :], U).then_inc(S("state_ready"), 1)

            dve.wait_ge(S("ostd_ready"), 1)
            link(V.reciprocal(rstd[:, 0:24], std[:, 0:24]))
            V.tensor_copy(rsx[:, 0:24, :], rstd[:, 0:24].unsqueeze(2).broadcast_to([P, 24, HD])).then_inc(S("rsx_ready"), 1)
            dve.wait_ge(S(f"pb_free{(N_IN - 1) % 3}"), (N_IN - 1) // 3 + 1)
            for c in range(4):
                dve.wait_ge(S("obc_ready"), c + 1)
                link(V.scalar_tensor_tensor(out=o_t[:, c, :], in0=o_t[:, c, :], scalar=pcol[:, 0, OG:OG + 1],
                                            in1=bank(4 + c % 2, TOK), op0=ALU.mult, op1=ALU.mult))
                mul(o_t[:, c, :], o_t[:, c, :], sgb[:, c, :]).then_inc(S("of_ready"), 1)
                if c:
                    dve.wait_ge(S("obhi_ready"), c)
                    V.tensor_tensor(hlo[:, 3 + c, :], o_t[:, c - 1, :], hhi[:, 3 + c, :].bitcast(F32), ALU.subtract).then_inc(S("mixlo_ready"), 1)
            dve.wait_ge(S("obhi_ready"), 4)
            V.tensor_tensor(hlo[:, 7, :], o_t[:, 3, :], hhi[:, 7, :].bitcast(F32), ALU.subtract).then_inc(S("mixlo_ready"), 1)

            dve.wait_ge(S("qstd_ready"), 1)
            link(V.reciprocal(rstd[:, 0:30], std[:, 0:30]))
            V.tensor_copy(rsx[:, 0:30, :], rstd[:, 0:30].unsqueeze(2).broadcast_to([P, 30, HD])).then_inc(S("rsx_ready"), 1)
            for c in range(5):
                gain = KG if c == 4 else QG
                dve.wait_ge(S("qbc_ready"), c + 1)
                V.scalar_tensor_tensor(out=qk[:, c, :], in0=qk[:, c, :], scalar=pcol[:, 0, gain:gain + 1],
                                       in1=bank(4 + c % 2, TOK), op0=ALU.mult, op1=ALU.mult).then_inc(S("qn_ready"), 1)
                dve.wait_ge(S("qrot_ready"), c + 1)
                link(mul(qsq[:, c, 0:256], bank(3 if c % 2 else 6, 256), con[:, C_SIN:C_SIN + 256]))
                link(mul(qk[:, c, 128:384], qk[:, c, 128:384], con[:, C_COS:C_COS + 256]))
                V.tensor_tensor(qk[:, c, 128:384], qk[:, c, 128:384], qsq[:, c, 0:256], ALU.add).then_inc(S("roped"), 1)

            for i in range(len(ITEMS) + 1):
                if i < len(ITEMS):
                    w = P if ITEMS[i][0] == 0 else TOK
                    dve.wait_ge(S("score_ready"), i + 1)
                    V.tensor_reduce(nmax[:, i:i + 1], bank(3 + i % 2, w), axis=AX, op=ALU.max, negate=True)\
                        .then_inc(S("nmax_ready"), 1)
                if i >= 1:
                    j = i - 1
                    w = P if ITEMS[j][0] == 0 else TOK
                    dve.wait_ge(S("prob_ready"), j + 1)
                    link(V.reciprocal(rsum[:, 1, j:j + 1], rsum[:, 0, j:j + 1]))
                    V.tensor_scalar_mul(prob[j % 2][:, 0:w], prob[j % 2][:, 0:w], rsum[:, 1, j:j + 1])\
                        .then_inc(S("pnorm_ready"), 1)
                if i in (10, 18, 24):
                    b = {10: 0, 18: 1, 24: 2}[i]
                    dve.wait_ge(S("oahi_ready"), b + 1)
                    V.tensor_tensor(hlo[:, 0:4, P * b:P * b + P], bank(b).rearrange("p (c t) -> p c t", c=4),
                                    hhi[:, 0:4, P * b:P * b + P].bitcast(F32), ALU.subtract).then_inc(S("mixlo_ready"), 1)

            dve.wait_ge(S("ada_used"), 48)
            modulation(0, 16, 48)
            modulation(1, 0, 48)
            amplitude(1, 0, SC2, N2)
            amplitude(2, 1, SC1, N1 + KC)
            amplitude(3, 1, SC2, N2 + KC)

            def residual(src, l, gate, k, last):
                for g, t0, t1 in GROUPS:
                    ins = V.scalar_tensor_tensor(out=xT[:, k, t0:t1], in0=src[:, t0:t1], scalar=mod[:, l, gate + k, g:g + 1],
                                                 in1=xT[:, k, t0:t1], op0=ALU.mult, op1=ALU.add)
                    if g:
                        ins.then_inc(S("x_new" if last and k == KC - 1 else "x_chunk"), 1)

            for j in range(8):
                dve.wait_ge(S("unit_used"), U_OUT + j + 1)
                residual(bank(j % 3, TOK), 0, G1, j, True)

            R = lambda s, n=4: rt[:, s, :, 0:n]

            def first_of(out, x, m, tmp):
                link(V.tensor_tensor(tmp, x, m.broadcast_to([P, NB, 4]), ALU.is_equal))
                link(mul(tmp, tmp, con[:, C_DESC:C_DESC + 4].unsqueeze(1).broadcast_to([P, NB, 4])))
                link(V.tensor_reduce(R(15, 1), tmp, axis=AX, op=ALU.max))
                link(V.tensor_tensor(out, tmp, R(15, 1).broadcast_to([P, NB, 4]), ALU.is_equal))

            def router(l):
                lg = rt[:, 16:18, :, :].rearrange("p a b n -> p (a b n)")[:, 0:60].rearrange("p (b n) -> p b n", b=NB)
                lgg = lg[:, :, 0:4]
                four = lambda t: t.rearrange("p b (g j) -> p b g j", g=4)
                dve.wait_ge(S("logits_ready"), l + 1)
                link(V.tensor_tensor(lg, bank(7, 60).rearrange("p (b n) -> p b n", b=NB),
                                     rb[:, l, :].unsqueeze(1).broadcast_to([P, NB, 20]), ALU.add))
                link(V.tensor_reduce(R(0, 1), lgg, axis=AX, op=ALU.max))
                V.tensor_tensor(R(1), lgg, R(0, 1).broadcast_to([P, NB, 4]), ALU.subtract).then_inc(S("rt_group"), 1)
                first_of(R(3), lgg, R(0, 1), R(4))
                for b in range(NB):
                    link(mul(four(rt[:, 5, b:b + 1, :]), four(lg[:, b:b + 1, 4:20]),
                             R(3)[:, b:b + 1, :].unsqueeze(3).broadcast_to([P, 1, 4, 4])))
                link(V.tensor_reduce(R(6), rt[:, 5, :, :].rearrange("p b (g j) -> p b j g", g=4), axis=AX, op=ALU.add))
                link(V.tensor_reduce(R(7, 1), R(6), axis=AX, op=ALU.max))
                first_of(R(8), R(6), R(7, 1), R(4))
                link(V.tensor_scalar_mul(R(9), R(8), -3.0e38))
                link(V.tensor_tensor(R(9), R(9), R(6), ALU.add))
                link(V.tensor_reduce(R(10, 1), R(9), axis=AX, op=ALU.max))
                first_of(R(11), R(9), R(10, 1), R(4))
                V.tensor_tensor(R(12, 1), R(10, 1), R(7, 1), ALU.subtract).then_inc(S("rt_second"), 1)
                dve.wait_ge(S("rt_exp"), 2 * l + 2)
                link(V.tensor_reduce(R(14, 1), R(2), axis=AX, op=ALU.add))
                link(V.reciprocal(R(14, 1), R(14, 1)))
                link(V.tensor_scalar_add(R(18, 1), R(13, 1), 1.0))
                link(V.reciprocal(R(18, 1), R(18, 1)))
                link(mul(R(18, 1), R(18, 1), R(14, 1)))
                link(mul(R(19, 1), R(18, 1), R(13, 1)))
                link(mul(R(8), R(8), R(18, 1).broadcast_to([P, NB, 4])))
                link(mul(R(11), R(11), R(19, 1).broadcast_to([P, NB, 4])))
                link(V.tensor_tensor(R(8), R(8), R(11), ALU.add))
                for b in range(NB):
                    ins = mul(four(rt[:, 20, b:b + 1, :]), R(3)[:, b:b + 1, :].unsqueeze(3).broadcast_to([P, 1, 4, 4]),
                              R(8)[:, b:b + 1, :].unsqueeze(2).broadcast_to([P, 1, 4, 4]))
                    ins.then_inc(S("combine_ready"), 1)
                dve.wait_ge(S("combine_T"), l + 1)
                V.tensor_copy(combT, ps[0:16, 7 * 512:7 * 512 + TOK]).then_inc(S("combT_ready"), 1)

            def experts(l):
                C0 = EXPERTS * l

                def hid(e, par, u, comb_e):
                    n = 2 * (e + C0)
                    for f in range(2):
                        dve.wait_ge(S("silu_ready"), n + f + 1)
                        dve.wait_ge(S("unit_used"), u + 2 * f + 2)
                        ge(dve, "hidlo_ready", n - 2 + f + 1)
                        mul(tact[:, f, :], sact[:, f, :], bank(2 * f + 1, TOK)).then_inc(S("hmul_done"), 1)
                        dve.wait_ge(S("hmul_done"), n + f + 1)
                        mul(tact[:, f, :], tact[:, f, :], comb_e).then_inc(S("tact_ready"), 1)
                    for f in range(2):
                        dve.wait_ge(S("hidhi_ready"), n + f + 1)
                        V.tensor_tensor(hidlo[:, par, f, :], tact[:, f, :], hidhi[:, par, f, :].bitcast(F32),
                                        ALU.subtract).then_inc(S("hidlo_ready"), 1)

                def gather(e, u):
                    for d in range(2):
                        for z in range(2):
                            t = 4 * (e + C0) + 2 * d + z
                            if z:
                                dve.wait_ge(S("unit_used"), u + d + 1)
                            else:
                                dve.wait_ge(S("y_ready"), 2 * (e + C0) + d + 1)
                            ge(dve, "y_free", t - 3)
                            k = 4 * d + 2 * z
                            src = ps[:, (4 + 2 * z) * 512:(6 + 2 * z) * 512].rearrange("p (c t) -> p c t", c=2)[:, :, 0:TOK]
                            V.tensor_tensor(acc[:, k:k + 2, :], acc[:, k:k + 2, :], src, ALU.add).then_inc(S("y_free"), 1)

                U0 = (U_MOE0, U_MOE1)[l]
                link(V.memset(acc, 0.0))
                dve.wait_ge(S("comb_ready"), 16 * l + 16)
                hid(0, 0, U0, comb[:, 0:TOK])
                hid(1, 1, U0 + 4, comb[:, TOK:2 * TOK])
                gather(0, U0 + 8)
                with dve.Fori(0, 7) as i:
                    for z in range(2):
                        e = 2 * i + (2 + z)
                        hid(e, z, 12 * i + (U0 + 10 + 6 * z), comb[:, bass.ds(TOK * e, TOK)])
                        gather(2 * i + (1 + z), 12 * i + (U0 + 14 + 6 * z))
                gather(EXPERTS - 1, U0 + 94)
                dve.wait_ge(S("y_free"), 4 * (C0 + EXPERTS))
                for k in range(KC):
                    residual(acc[:, k, :], l, G2, k, True)

            inv_std(1)
            modulate(1, 0, SH2)
            router(0)
            experts(0)

            inv_std(2)
            link(V.memset(upad, 0.0))
            modulate(2, 1, SH1)
            tapw = lambda t, k: pcol[:, 2, 8 * t + k:8 * t + k + 1] if t < 15 else pcol[:, 3, 8 * (t - 15) + k:8 * (t - 15) + k + 1]
            for pair in range(4):
                for k in (2 * pair, 2 * pair + 1):
                    dve.wait_ge(S("usig_ready"), k + 1)
                    a = bank((2 * k) % 4, TOK)
                    mul(upad[:, k, PAD:PAD + P], a[:, 0:P], usig[:, k % 2, 0:P]).then_inc(S("u_ready"), 1)
                    mul(upad[:, k, 2 * PAD + P:2 * PAD + 3 * P], a[:, P:TOK], usig[:, k % 2, P:TOK]).then_inc(S("u_ready"), 1)
                dve.wait_ge(S("u_ready"), 4 * pair + 4)
                for t in range(TAPS):
                    for k in (2 * pair, 2 * pair + 1):
                        if t == 0:
                            link(V.tensor_scalar(cacc[:, k, :], upad[:, k, 0:CONV_N], tapw(0, k),
                                                 pcol[:, 0, DWB + k:DWB + k + 1], ALU.mult, ALU.add), back=1)
                        else:
                            ins = V.scalar_tensor_tensor(out=cacc[:, k, :], in0=upad[:, k, t:t + CONV_N], scalar=tapw(t, k),
                                                         in1=cacc[:, k, :], op0=ALU.mult, op1=ALU.add)
                            if t < TAPS - 1:
                                link(ins, back=0 if t == TAPS - 2 and k % 2 else 1)
                            else:
                                ins.then_inc(S("conv_ready"), 1)
            dve.wait_ge(S("cmean_bc"), 1)
            for b0, b1, o in ((0, 1, 0), (1, 3, BLK[1])):
                n = P * (b1 - b0)
                ins = V.tensor_tensor(cen[:, :, P * b0:P * b1], cacc[:, :, o:o + n],
                                      bank(4, n, P * b0).unsqueeze(1).broadcast_to([P, KC, n]), ALU.subtract)
                if b0 == 0:
                    link(ins)
            ins.then_inc(S("cen_ready"), 1)
            dve.wait_ge(S("cstd_ready"), 1)
            V.reciprocal(rstd[:, 0:3], std[:, 3:6]).then_inc(S("crstd_ready"), 1)
            dve.wait_ge(S("crstd_bc"), 1)
            for k in range(KC):
                mul(cen[:, k, :], cen[:, k, :], bank(4, TOK)).then_inc(S("cn_ready"), 1)
            for k in range(KC):
                dve.wait_ge(S("chi_ready"), k + 1)
                V.tensor_tensor(hlo[:, k, :], hfk[:, k, :], hhi[:, k, :].bitcast(F32), ALU.subtract).then_inc(S("clo_ready"), 1)
            for j in range(8):
                dve.wait_ge(S("unit_used"), U_PW2 + j + 1)
                residual(bank(j % 4, TOK), 1, G1, j, True)

            inv_std(3)
            modulate(3, 1, SH2)
            router(1)
            experts(1)

            inv_std(4)
            dve.wait_ge(S("rbc_ready"), 5)
            for k in range(KC):
                V.scalar_tensor_tensor(out=hfk[:, k, :], in0=xT[:, k, :], scalar=pcol[:, 0, NF + k:NF + k + 1],
                                       in1=bank(4, TOK), op0=ALU.mult, op1=ALU.mult).then_inc(S("yf_ready"), 1)

        @block.tensor
        def _(pe):
            mm = nc.tensor.matmul
            slot = [0]

            def ada(n_slots):
                for _ in range(n_slots):
                    n = ada_at[slot[0]]
                    _, l, j = SLOTS[n]
                    pe.wait_ge(S(f"raw_full{n % RAW}"), 16 * (n // RAW + 1))
                    for h in range(2):
                        out = bank(7, 2, 96 * l + 2 * (2 * j + h))
                        for k in range(KC):
                            last = mm(out, raw_k(n % RAW)[:, k, P * h:P * h + P], scond[:, k, :],
                                      start=(k == 0), stop=(k == KC - 1))
                    last.then_inc(S("ada_used"), 1)
                    slot[0] += 1

            ada_at = [n for n, s in enumerate(SLOTS) if s[0] == "ada"]

            def three(out, ahi, alo, bhi, blo, start, stop):
                mm(out, ahi, bhi, start=start, stop=False)
                mm(out, ahi, blo, start=False, stop=False)
                return mm(out, alo, bhi, start=False, stop=stop)

            def unit_ready(u, i=None):
                pe.wait_ge(S("lo_done"), u + 1 if i is None else 12 * i + (u + 1))

            def project(u, b, i=None, per_chunk=None):
                unit_ready(u, i)
                wh, wl = unit_view(whi, u, False), unit_view(wlo, u, False)
                for k in range(KC):
                    if per_chunk:
                        pe.wait_ge(S(per_chunk[0]), per_chunk[1] + k + 1)
                    last = three(bank(b, TOK), wh[:, k, :], wl[:, k, :], hhi[:, k, :], hlo[:, k, :], k == 0, k == KC - 1)
                last.then_inc(S("unit_used"), 1)

            def project_tok(u, b):
                unit_ready(u)
                wh, wl = unit_view(whi, u, False), unit_view(wlo, u, False)
                for t in range(NB):
                    r = slice(P * t, P * t + P)
                    for k in range(KC):
                        last = three(bank(b, P, P * t), hhi[:, k, r], hlo[:, k, r], wh[:, k, :], wl[:, k, :], k == 0, k == KC - 1)
                last.then_inc(S("unit_used"), 1)

            def column_sums(src, off, done, b=3):
                for t in range(NB):
                    for k in range(KC):
                        last = mm(bank(b, 1, t), src[:, k, off[t]:off[t] + P], ones, start=(k == 0), stop=(k == KC - 1))
                last.then_inc(S(done), 1)

            def broadcast(col, done):
                for t in range(NB):
                    last = mm(bank(4, P, P * t), col[:, t:t + 1].broadcast_to([P, P]), ident, start=True, stop=True)
                last.then_inc(S(done), 1)

            def norm(n):
                pe.wait_ge(S("sq_ready"), KC * (n + 1))
                column_sums(hfk, (0, P, 2 * P), "ssum_ready")
                pe.wait_ge(S("rstd_ready"), n + 1)
                broadcast(rstd, "rbc_ready")

            pe.wait_ge(S("in_con"), 16)
            pe.wait_ge(S("in_rows"), 16 * 18)
            for g in range(4):
                nc.tensor.transpose(bank(7, PROWS[g], P * g), prow[0:PROWS[g], g, :], ident[0:PROWS[g], 0:PROWS[g]])\
                    .then_inc(S("prow_T"), 1)
            pe.wait_ge(S("in_x"), 48)
            for k in range(KC):
                ge(pe, "xT_ready", k - 3)
                for t in range(NB):
                    last = nc.tensor.transpose(bank(3 + k % 4, P, P * t), xtok[:, t, P * k:P * k + P], ident)
                last.then_inc(S("x_T"), 1)
            norm(0)
            pe.wait_ge(S("scond_ready"), 1)
            pe.wait_ge(S("pcol_ready"), 4)
            ada(8)

            pair_cols = lambda c, b: slice(TOK * c + P * b, TOK * c + P * b + P)
            zt = Z[:, :].tensor

            def query_side(z, l, c, b):
                h = 1 << (l - 1)
                o = TOK * c + P * b
                return bass.AP(zt, HD * z * Z_LEN + o, [[Z_LEN, HD], [2 * h, P // (2 * h)], [1536 + h, 2], [1, h]])

            def gram(l):
                if l == 0:
                    pe.wait_ge(S("k_ready"), 8)
                    for q in range(8, 12):
                        pe.wait_ge(S(f"pb_free{q % 3}"), q // 3 + 1)
                else:
                    pe.wait_ge(S("x_ready"), l)
                    if l == 1:
                        pe.wait_ge(S("qinit_done"), 2)
                    ge(pe, "q_level", 2 * (l - 1))
                for b in range(NB):
                    i = NB * l + b
                    ge(pe, "gram_copied", i - 1)
                    for c in range(4):
                        for z in range(2):
                            r = slice(HD * z, HD * z + HD)
                            out = bank(3 + 2 * (i % 2) + z, P, P * c)
                            cols = pair_cols(c, b)
                            if l == 0:
                                mm(out, KS[r, cols], q_t[r, cols], start=True, stop=False)
                                last = mm(out, KR[r, cols], q_t[r, cols], start=False, stop=True)
                            else:
                                last = mm(out, Xs[l % 2][r, cols], query_side(z, l, c, b), start=True, stop=True)
                    last.then_inc(S("gram_done"), 1)

            for q in range(N_IN):
                ge(pe, f"pb_free{q % 3}", q // 3)
                if IN_ORDER[q // 2] in (9, 10) or q == VAT_Q:
                    project_tok(q, q % 3)
                else:
                    project(q, q % 3, per_chunk=("hlo_ready", 0) if q == 0 else None)
                if q % 2:
                    ada(1)
                if q in GRAM_AFTER:
                    gram(GRAM_AFTER[q])

            pe.wait_ge(S("ks_level"), 2 * LEVELS)
            for g, (fwd, b) in enumerate(UPDATES):
                src = KS if fwd else KR
                if g < 2:
                    pe.wait_ge(S("gram_copied"), NB * (LEVELS + 1))
                else:
                    pe.wait_ge(S("kt_ready"), g - 1)
                for c in range(4):
                    last = nc.tensor.transpose(bank(3 + g % 2, P, P * c), src[:, pair_cols(c, b)], ident)
                last.then_inc(S("kt_T"), 1)
            for q in range(N_IN - 3, N_IN):
                pe.wait_ge(S(f"pb_free{q % 3}"), q // 3 + 1)
            for g, (fwd, b) in enumerate(UPDATES):
                pe.wait_ge(S("kt_ready"), g + 1)
                ge(pe, "state_ready", 2 * (g - 1))
                for c in range(4):
                    last = mm(bank(5 + g % 2, P, P * c), KT[g][:, P * c:P * c + P], v_t[:, b, P * c:P * c + P], start=True, stop=True)
                last.then_inc(S("u_full"), 1)
                ada(1)
            pe.wait_ge(S("q_level"), 2 * LEVELS)
            for b in range(NB):
                if b == 1:
                    pe.wait_ge(S("state_ready"), 4)
                for c in range(4):
                    out = bank(b, P, P * c)
                    if b:
                        f, w = (0, 3) if b == 1 else (1, 2)
                        mm(out, Sbd[:, f, c, :], QP[:, pair_cols(c, b)], start=True, stop=False)
                        mm(out, Sbd[:, w, c, :], QQ[:, pair_cols(c, b)], start=False, stop=False)
                    for z in range(2):
                        r = slice(HD * z, HD * z + HD)
                        last = mm(ps[r, 512 * b + P * c:512 * b + P * c + P], v_t[:, b, P * c + HD * z:P * c + HD * z + HD],
                                  AT[:, b, 4 * z + c, :], start=(b == 0), stop=True)
                last.then_inc(S("o_full"), 1)
            pe.wait_ge(S("in_small"), 160)
            pe.wait_ge(S("state_ready"), 8)
            for h in range(2):
                last = nc.tensor.transpose(bank(5, P, P * h), ck[:, h, :, :].rearrange("p z d -> p (z d)"), ident)
            last.then_inc(S("ckT_ready"), 1)
            pe.wait_ge(S("osq_ready"), 1)
            sel = con[:, C_SEL:C_SEL + 2]
            for c in range(4):
                for b in range(NB):
                    last = mm(bank(3, 2, 2 * (NB * c + b)), osq[:, pair_cols(c, b)], sel, start=True, stop=True)
            last.then_inc(S("osum_ready"), 1)
            pe.wait_ge(S("rsx_ready"), 1)
            pe.wait_ge(S("kcache_ready"), 1)
            for c in range(4):
                ge(pe, "of_ready", c - 1)
                for b in range(NB):
                    n = 2 * (NB * c + b)
                    last = mm(bank(4 + c % 2, P, P * b), rsx[:, n:n + 2, :].rearrange("p n d -> p (n d)"), ident, start=True, stop=True)
                last.then_inc(S("obc_ready"), 1)
            pe.wait_ge(S("qsq_ready"), 1)
            pe.wait_ge(S("ostd_ready"), 1)
            for c in range(5):
                for b in range(NB):
                    last = mm(bank(3, 2, 2 * (NB * c + b)), qsq[:, c, P * b:P * b + P], sel, start=True, stop=True)
            last.then_inc(S("qsum_ready"), 1)
            pe.wait_ge(S("rsx_ready"), 2)
            pe.wait_ge(S("of_ready"), 4)
            for c in range(5):
                for b in range(NB):
                    n = 2 * (NB * c + b)
                    last = mm(bank(4 + c % 2, P, P * b), rsx[:, n:n + 2, :].rearrange("p n d -> p (n d)"), ident, start=True, stop=True)
                last.then_inc(S("qbc_ready"), 1)
                pe.wait_ge(S("qn_ready"), c + 1)
                mm(bank(3 if c % 2 else 6, 256), con[:, C_ROT:C_ROT + P], qk[:, c, 128:384], start=True, stop=True)\
                    .then_inc(S("qrot_ready"), 1)
                ge(pe, "roped", c)
            pe.wait_ge(S("roped"), 5)
            nc.tensor.transpose(bank(6, P), qk[:, 4, 0:P], ident).then_inc(S("kout_T"), 1)
            pe.wait_ge(S("kall_ready"), 128)
            pe.wait_ge(S("in_cv"), 16)
            pe.wait_ge(S("kout_ready"), 1)
            pe.wait_ge(S("o_copied"), NB)

            for i in range(len(ITEMS) + 2):
                if i < len(ITEMS):
                    b, n = ITEMS[i]
                    r = slice(HD * (n % 2), HD * (n % 2) + HD)
                    k0, k1 = (0, P) if b == 0 else (P, 512)
                    ge(pe, "prob_ready", i - 1)
                    mm(bank(3 + i % 2, k1 - k0), qk[r, n // 2, P * b:P * b + P], kall[r, n // 4, k0:k1],
                       start=True, stop=True).then_inc(S("score_ready"), 1)
                if 1 <= i <= len(ITEMS):
                    j = i - 1
                    pe.wait_ge(S("pnorm_ready"), j + 1)
                    ge(pe, "PT_ready", j - 1)
                    for t in range(1 if ITEMS[j][0] == 0 else NB):
                        last = nc.tensor.transpose(bank(5 + j % 2, P, P * t), prob[j % 2][:, P * t:P * t + P], ident)
                    last.then_inc(S("pT_done"), 1)
                if i >= 2:
                    j = i - 2
                    b, n = ITEMS[j]
                    z, kv = n % 2, n // 4
                    pe.wait_ge(S("PT_ready"), j + 1)
                    blocks = [0] if b == 0 else [1, 2, 3]
                    for t, vb in enumerate(blocks):
                        last = mm(ps[HD * z:HD * z + HD, 512 * b + P * (n // 2):512 * b + P * (n // 2) + P],
                                  vat[:, vb, HD * kv:HD * kv + HD], PT[j % 2][:, P * t:P * t + P],
                                  start=(t == 0), stop=(t == len(blocks) - 1))
                    last.then_inc(S("pv_done"), 1)
                if slot[0] < 48:
                    ada(1)
            assert slot[0] == 48

            pe.wait_ge(S("mixlo_ready"), 4 + NB)
            for j in range(8):
                ge(pe, "x_chunk", j - 2)
                project(U_OUT + j, j % 3)

            def experts(l, U0):
                C0 = EXPERTS * l
                h_chunks = ("hlo_ready", KC * (1 if l == 0 else 3))

                def up(e, u, i=None, per_chunk=None):
                    n = 2 * (e + C0)
                    for f in range(2):
                        ge(pe, "silu_ready", n - 2 + f + 1)
                        project(u + 2 * f, 2 * f, i, per_chunk if f == 0 else None)
                        ge(pe, "hmul_done", n - 2 + f + 1)
                        project(u + 2 * f + 1, 2 * f + 1, i)

                def down(e, u, par, i=None):
                    for d in range(2):
                        unit_ready(u + d, i)
                        if d == 0:
                            pe.wait_ge(S("hidlo_ready"), 2 * (e + C0) + 2)
                        wh, wl = unit_view(whi, u + d, True), unit_view(wlo, u + d, True)
                        for z in range(2):
                            ge(pe, "y_free", 4 * (e + C0) + 2 * d + z - 1)
                            for c in (2 * z, 2 * z + 1):
                                for k in range(2):
                                    last = three(bank(4 + c, TOK), wh[:, k, P * c:P * c + P], wl[:, k, P * c:P * c + P],
                                                 hidhi[:, par, k, :], hidlo[:, par, k, :], k == 0, k == 1)
                            last.then_inc(S("unit_used" if z else "y_ready"), 1)

                pe.wait_ge(S("hf_ready"), h_chunks[1] + KC)
                for t in range(NB):
                    for k in range(KC):
                        last = mm(bank(7, 20, 20 * t), hfk[:, k, P * t:P * t + P], wr[:, l, k, :],
                                  start=(k == 0), stop=(k == KC - 1))
                last.then_inc(S("logits_ready"), 1)
                up(0, U0, per_chunk=h_chunks)
                pe.wait_ge(S("combine_ready"), NB * (l + 1))
                for t in range(NB):
                    last = nc.tensor.transpose(ps[0:16, 7 * 512 + P * t:7 * 512 + P * t + P], rt[:, 20, t, :], ident)
                last.then_inc(S("combine_T"), 1)
                up(1, U0 + 4)
                pe.wait_ge(S("combT_ready"), l + 1)
                down(0, U0 + 8, 0)
                with pe.Fori(0, 7) as i:
                    for z in range(2):
                        up(2 * i + (2 + z), U0 + 10 + 6 * z, i)
                        down(2 * i + (1 + z), U0 + 14 + 6 * z, 1 - z, i)
                down(EXPERTS - 1, U0 + 94, 1)

            norm(1)
            experts(0, U_MOE0)

            norm(2)
            for j in range(16):
                g = j // 2
                ge(pe, "usig_ready" if j % 2 else "u_ready", g - 1 if j % 2 else 2 * (g - 1))
                project(U_PW1 + j, j % 4, per_chunk=("hlo_ready", 2 * KC) if j == 0 else None)
            pe.wait_ge(S("conv_ready"), KC)
            column_sums(cacc, BLK, "csum_ready")
            pe.wait_ge(S("cmean_ready"), 1)
            broadcast(std, "cmean_bc")
            pe.wait_ge(S("csq_ready"), 1)
            column_sums(hfk, (0, P, 2 * P), "cvar_ready")
            pe.wait_ge(S("crstd_ready"), 1)
            broadcast(rstd, "crstd_bc")
            for j in range(8):
                ge(pe, "x_chunk", 14 + j - 3 if j >= 4 else 0)
                project(U_PW2 + j, j % 4, per_chunk=("clo_ready", 0) if j == 0 else None)
            norm(3)
            experts(1, U_MOE1)

            norm(4)
            pe.wait_ge(S("yf_ready"), KC)
            for i in range(2 * NB):
                t, h = i // 2, i % 2
                ge(pe, "ytok_ready", i - 1)
                for c in range(4):
                    last = nc.tensor.transpose(bank(5 + i % 2, P, P * c), hfk[:, 4 * h + c, P * t:P * t + P], ident)
                last.then_inc(S("yT_ready"), 1)


INPUTS = ["x_prompt", "x_sample", "cache_k", "cache_v", "state_hgrn", "c", "c_ctx", "ada_w", "ada_b", "norm1_g",
          "norm2_g", "mix_w_in", "mix_w_out", "attn_q_gain", "attn_k_gain", "hgrn_lower_bound", "hgrn_out_gain",
          "conv_pw1", "conv_dw", "conv_dw_b", "conv_ln_g", "conv_ln_b", "conv_pw2", "moe_w_group", "moe_b_group",
          "moe_w_expert", "moe_b_expert", "moe_w1", "moe_w3", "moe_w2", "final_g"]
OUTPUTS = [(1, 128, D), (1, 256, D), (1, 1, 128, 2, HD), (1, 1, 128, 2, HD), (1, 1, 2, HEADS, HD, HD)]


def kernel(**inputs):
    import concourse.bacc as bacc
    from concourse.bass_utils import run_bass_kernel_spmd

    nc = bacc.Bacc("TRN2", target_bir_lowering=False, num_devices=1, dynamic_dma_scratch_size=1024)
    arrays = {n: np.ascontiguousarray(inputs[n]) for n in INPUTS}
    arrays["shape_constants"] = shape_constants()
    aps = {n: nc.dram_tensor(n, a.shape, mybir.dt.from_np(a.dtype), kind="ExternalInput").ap()
           for n, a in arrays.items()}
    for i, shape in enumerate(OUTPUTS):
        aps[f"out{i}"] = nc.dram_tensor(f"out{i}", shape, F32, kind="ExternalOutput").ap()
    build(nc, aps)
    r = run_bass_kernel_spmd(nc, [arrays], core_ids=[0]).results[0]
    return tuple(r[f"out{i}"] for i in range(len(OUTPUTS)))
```

```python
from contextlib import ExitStack

import numpy as np

import concourse.bass as bass
from concourse import mybir

F32 = mybir.dt.float32
F32R = mybir.dt.float32r

ALU = mybir.AluOpType
ACT = mybir.ActivationFunctionType
AX = mybir.AxisListType.X

P = 128
D = 1024
KC = D // P
TOK = 384
NB = TOK // P
GROUPS = ((0, 0, 128), (1, 128, 384))
HD = 64
HEADS = 8
EPS = 1e-6
EXPERTS = 16
TAPS = 31
PAD = TAPS // 2
UW = PAD + 128 + PAD + 256 + PAD
CONV_N = UW - 2 * PAD
RAW = 3
UNITS = 6
AHEAD = 4
LEVELS = 7

SH1, SC1, G1, SH2, SC2, G2 = (KC * i for i in range(6))

CCTX, CC, N1, N2, NF, LB, DWB, LNG, LNB, QG, KG, OG = 0, 8, 16, 32, 48, 56, 64, 72, 80, 88, 89, 90
PROWS = (91, 96, 120, 128)

C_ID, C_ROT, C_COS, C_SIN, C_SEL, C_ONE, C_DESC, C_MASK = 0, 128, 256, 512, 768, 896, 1024, 1028
C_W = C_MASK + (LEVELS + 1) * P


def shape_constants():
    c = np.zeros((P, C_W), np.float32)
    c[:, C_ID:C_ID + P] = np.eye(P, dtype=np.float32)
    inv = (10000.0 ** (-np.arange(0, 32, 2, dtype=np.float32) / 32)).astype(np.float32)
    t = np.arange(256)
    for p in range(P):
        d = p % 64
        pos = (t // 64 if d < 32 else t % 64).astype(np.float32)
        ang = (pos * inv[d % 16]).astype(np.float32)
        c[p, C_COS:C_COS + 256] = np.cos(ang)
        c[p, C_SIN:C_SIN + 256] = np.sin(ang)
        if d % 32 < 16:
            c[p + 16, C_ROT + p] = -1.0
        else:
            c[p - 16, C_ROT + p] = 1.0
    c[:64, C_SEL:C_SEL + 64] = 1.0
    c[64:, C_SEL + 64:C_SEL + 128] = 1.0
    c[:, C_ONE:C_ONE + P] = 1.0
    c[:, C_DESC:C_DESC + 4] = [4.0, 3.0, 2.0, 1.0]
    c[:, C_MASK:] = level_masks()
    return c


def level_masks():
    m = np.zeros((P, LEVELS + 1, P), np.float32)
    j, i = np.meshgrid(np.arange(P), np.arange(P), indexing="ij")
    m[:, 0] = j == i
    for l in range(1, LEVELS + 1):
        h = 1 << (l - 1)
        m[:, l] = (j // (2 * h) == i // (2 * h)) & (j // h != i // h)
    return m.reshape(P, (LEVELS + 1) * P)


IN_ORDER = [5, 6, 7, 8, 3, 4, 9, 10, 2, 0, 1, 11, 12]
ADA_AFTER = [1, 1, 1, 1, 1, 1, 1, 1, 0, 2, 1, 1, 1]
N_IN = 2 * len(IN_ORDER)
GRAM_AFTER = {12: 0, 14: 1, 16: 2, 19: 3, 22: 4}
X_AFTER = {13: 1, 15: 2, 18: 3, 21: 4}
VAT_Q = 2 * IN_ORDER.index(2) + 1


def expert_slots(layer):
    s = [("w1", layer, 0), ("w3", layer, 0)]
    for e in range(1, EXPERTS):
        s += [("w1", layer, e), ("w3", layer, e), ("w2", layer, e - 1)]
    return s + [("w2", layer, EXPERTS - 1)]


def plan_slots():
    ada = [("ada", l, j) for l in range(2) for j in range(24)]
    plan, ada = ada[:8], ada[8:]
    for j, n in zip(IN_ORDER, ADA_AFTER):
        plan, ada = plan + [("in", 0, j)] + ada[:n], ada[n:]
    plan += ada[:-16] + [("out", 0, j) for j in range(4)]
    ada, p1 = ada[-16:], []
    for a in range(4):
        p1 += [("pw1", 0, a), ("pw1", 0, a + 4)] + ada[2 * a:2 * a + 2]
    p1 += ada[8:] + [("pw2", 0, j) for j in range(4)]
    bases = (len(plan), len(plan) + 3 * EXPERTS, len(plan) + 3 * EXPERTS + len(p1))
    return plan + expert_slots(0) + p1 + expert_slots(1), bases


def plan_units(slots):
    units, freed, n_ada, n = [], [None] * len(slots), 0, 0
    while n < len(slots):
        kind = slots[n][0]
        if kind == "ada":
            n_ada += 1
            freed[n] = ("ada_used", n_ada)
            n += 1
        elif kind in ("w1", "pw1"):
            for half in range(2):
                for z in range(2):
                    units.append((n + z, half, False))
                    freed[n + z] = ("lo_done", len(units))
            n += 2
        else:
            for half in range(2):
                units.append((n, half, kind == "w2"))
            freed[n] = ("lo_done", len(units))
            n += 1
    return units, freed


SUM_ORDER = [4, 0, 1, 2, 3]

POOL_CHUNKS = (0, 1)
DVE_CHUNKS = tuple(k for k in range(KC) if k not in POOL_CHUNKS)
PRODS = 4
CONV_TAPS_AT = [0] * 5 + [2] * 11


def tapw(pcol, t, k):
    return pcol[:, 2, 8 * t + k:8 * t + k + 1] if t < 15 else pcol[:, 3, 8 * (t - 15) + k:8 * (t - 15) + k + 1]


SLOTS, (B_MOE0, B_P1, B_MOE1) = plan_slots()
UNIT, FREED = plan_units(SLOTS)
U_OUT = N_IN
U_MOE0 = U_OUT + 8
U_PW1 = U_MOE0 + 6 * EXPERTS
U_PW2 = U_PW1 + 16
U_MOE1 = U_PW2 + 8
U_END = U_MOE1 + 6 * EXPERTS
assert len(UNIT) == U_END

ITEMS = [(b, n) for b in range(NB) for n in range(HEADS)]
UPDATES = [(True, 1), (False, 2), (True, 0), (False, 0)]

TAIL = [("square",), ("x", 5), ("sum", 4), ("gram", 5, 0), ("rot", 4), ("sum", 0), ("kout",), ("gram", 5, 1), ("rot", 0),
        ("sum", 1), ("gram", 5, 2), ("decay", 5), ("x", 6), ("rot", 1), ("sum", 2), ("ckt",), ("gram", 6, 0), ("rot", 2),
        ("sum", 3), ("gram", 6, 1), ("rot", 3), ("att", 0), ("gram", 6, 2), ("att", 1), ("decay", 6), ("x", 7),
        ("att", 2), ("ada", 1), ("att", 3), ("gram", 7, 0), ("att", 4), ("gram", 7, 1), ("att", 5), ("gram", 7, 2),
        ("att", 6), ("decay", 7), ("ada", 1), ("att", 7), ("kt", 0), ("att", 8), ("kt", 1), ("ada", 1), ("rows", 2),
        ("att", 9), ("state", 0), ("kt", 2), ("att", 10), ("state", 1), ("kt", 3), ("cols", 2), ("att", 11),
        ("state", 2), ("att", 12), ("state", 3), ("hout", 0), ("att", 13), ("hout", 1), ("ada", 1), ("att", 14),
        ("hout", 2), ("att", 15), ("hsum",), ("ada", 1), ("att", 16), ("hnorm", 0), ("ada", 1), ("att", 17),
        ("hnorm", 1), ("ada", 1), ("att", 18), ("hnorm", 2), ("ada", 1), ("att", 19), ("hnorm", 3), ("ada", 1),
        ("att", 20), ("ada", 1), ("att", 21), ("ada", 1), ("rows", 3), ("att", 22), ("att", 23), ("cols", 3),
        ("att", 24), ("att", 25)]

Z_LEN = 17792
BLK = (0, PAD + 128, PAD + 256)


def build(nc, A):
    with ExitStack() as ctx:
        sems = {}

        def S(name):
            if name not in sems:
                sems[name] = ctx.enter_context(nc.semaphore(name))
            return sems[name]

        def ge(eng, name, v):
            if isinstance(v, int) and v <= 0:
                return
            eng.wait_ge(S(name), v)

        def sb(name, shape, dt=F32):
            return ctx.enter_context(nc.sbuf_tensor(name, shape, dt))

        ps = ctx.enter_context(nc.psum_tensor("ps", [P, 8 * 512], F32))

        def bank(b, n=512, o=0):
            return ps[:, b * 512 + o:b * 512 + o + n]

        raw = sb("raw", [P, RAW, 2048])
        xT = sb("xT", [P, KC, TOK])
        hf = sb("hf", [P, KC * TOK])
        hhi = sb("hhi", [P, KC, TOK], F32R)
        hlo = sb("hlo", [P, KC, TOK], F32R)
        con = sb("con", [P, C_W])
        pcol = sb("pcol", [P, 4, P])
        scond = sb("scond", [P, KC, 2])
        mod = sb("mod", [P, 2, 48, 2])
        amp = sb("amp", [P, 4, KC, 2])
        lbw = sb("lbw", [P, 5, 8])
        wr = sb("wr", [P, 2, KC, 20])
        rb = sb("rb", [P, 2, 20])
        sums = sb("sums", [P, CONV_N])[:, :]
        std = sb("std", [P, TOK])[:, :]
        rstd = sb("rstd", [P, TOK])[:, :]
        totc = sb("totc", [P, 2, 4, NB])
        send = sb("send", [P, 2, 4, HD])
        ck = sb("ck", [P, 2, 2, HD])
        nmax = sb("nmax", [P, len(ITEMS)])
        rsum = sb("rsum", [P, 2, len(ITEMS)])
        Z = sb("Z", [P, Z_LEN])
        with nc.sbuf_tensor("whi", [P, UNITS, 1024], F32R) as whi, nc.sbuf_tensor("wlo", [P, UNITS, 1024], F32R) as wlo, \
                nc.sbuf_tensor("hid", [P, 2, 2, 2, TOK], F32R) as hid:
            hidhi, hidlo = hid[:, 0], hid[:, 1]
        with nc.sbuf_tensor("att", [P, 2 * UNITS * 1024], F32) as att, nc.sbuf_tensor("adarow", [2, 2048], F32) as adarow:
            pass
        ident = con[:, C_ID:C_ID + P]
        ones = con[:, C_ONE:C_ONE + P]
        head_ones = con[:, C_SEL:C_SEL + P]
        mask = con[:, C_MASK:].rearrange("p (l i) -> p l i", i=P).bitcast(mybir.dt.uint32)
        hfk = hf[:, :].rearrange("p (k t) -> p k t", k=KC)

        xtok = Z[:, 0:3072].rearrange("p (b d) -> p b d", b=NB)
        prow = Z[:, 3072:3584].rearrange("p (g r) -> p g r", g=4)
        QQ, QP = Z[:, 0:1536], Z[:, 1536:3072]
        KS, KR = Z[:, 3072:4608], Z[:, 4608:6144]
        Xs = [Z[:, 6144:7680], Z[:, 7680:9216]]
        q_t = Z[:, 9216:10752]
        v_t = Z[:, 10752:12288].rearrange("p (b d) -> p b d", b=NB)
        AT = Z[:, 12288:15360].rearrange("p (b n i) -> p b n i", b=NB, n=HEADS)
        qk = Z[:, 15360:17280].rearrange("p (c t) -> p c t", c=5)
        vat = Z[:, 17280:17792].rearrange("p (b d) -> p b d", b=4)
        ff, fb = hf[:, 0:1536], hf[:, 1536:3072]
        sgb = q_t.rearrange("p (c t) -> p c t", c=4)
        KT = [Z[:, 6144 + 512 * g:6656 + 512 * g] for g in range(4)]
        Sbd = hf[:, 0:2048].rearrange("p (s c e) -> p s c e", s=4, c=4)
        o_f, osq = Z[:, 3072:4608], Z[:, 4608:6144]
        o_t = o_f.rearrange("p (c t) -> p c t", c=4)
        ostd = Z[:, 12288:13824].rearrange("p (c t) -> p c t", c=4)
        hstd = att[:, 0:1920].rearrange("p (c t) -> p c t", c=5)
        qsq = att[:, 1920:3840].rearrange("p (c t) -> p c t", c=5)
        kout = att[:, 3840:3968]
        kall = att[:, 3968:4992].rearrange("p (h t) -> p h t", h=2)
        prob = [att[:, 4992 + TOK * z:4992 + TOK * (z + 1)] for z in range(2)]
        PT = [att[:, 5760 + TOK * z:5760 + TOK * (z + 1)] for z in range(2)]
        comb = Z[:, 0:6144]
        acc = Z[:, 6144:9216].rearrange("p (c t) -> p c t", c=KC)
        sact = Z[:, 9216:9984].rearrange("p (c t) -> p c t", c=2)
        tact = Z[:, 9984:10752].rearrange("p (c t) -> p c t", c=2)
        combT = Z[0:16, 10752:11136]
        rt = Z[:, 11136:12288].rearrange("p (s b n) -> p s b n", s=24, b=NB)
        upad = Z[:, 0:3432].rearrange("p (c t) -> p c t", c=KC)
        cacc = Z[:, 3432:6624].rearrange("p (c t) -> p c t", c=KC)
        usig = Z[:, 6624:7392].rearrange("p (c t) -> p c t", c=2)
        prod = Z[:, 10464:10464 + PRODS * CONV_N].rearrange("p (r t) -> p r t", r=PRODS)
        cen = Z[:, 7392:10464].rearrange("p (c t) -> p c t", c=KC)
        ytok = Z[:, 0:3072].rearrange("p (b d) -> p b d", b=NB)

        comb_dram = nc.dram_tensor("comb_scratch", [2, EXPERTS * TOK], F32, kind="Internal").ap()

        raw_k = lambda r: raw[:, r, :].rearrange("p (k n) -> p k n", k=KC)
        raw_2 = lambda r: raw[:, r, :].rearrange("p (k n) -> p k n", k=2)

        def raw_unit(n, half, down):
            return raw_2(n % RAW)[:, :, 512 * half:512 * half + 512] if down \
                else raw_k(n % RAW)[:, :, 128 * half:128 * half + 128]

        def unit_view(t, u, down):
            return t[:, u % UNITS, :].rearrange("p (k n) -> p k n", k=2 if down else KC)

        block = ctx.enter_context(nc.Block())

        @block.sync
        def _(sp):
            def load(n, dst, src):
                sp.dma_start(dst, src).then_inc(S(f"raw_full{n % RAW}"), 16)

            def fetch(n, what, where, j):
                if what in ("w1", "w3", "w2"):
                    src = A["moe_" + what][where, j].rearrange("(k p) n -> p k n", p=P)
                    load(n, raw_2(n % RAW) if what == "w2" else raw_k(n % RAW), src)
                else:
                    w = {"ada": A["ada_w"], "in": A["mix_w_in"], "out": A["mix_w_out"],
                         "pw1": A["conv_pw1"], "pw2": A["conv_pw2"]}[what][where]
                    load(n, raw_k(n % RAW), w[:, 256 * j:256 * j + 256].rearrange("(k p) n -> p k n", p=P))

            def static(a, b):
                for n in range(a, b):
                    if n >= RAW:
                        name, v = FREED[n - RAW]
                        sp.wait_ge(S(name), v)
                    fetch(n, *SLOTS[n])

            for layer, first, base in ((0, 0, B_MOE0), (1, B_P1, B_MOE1)):
                static(first, base + 5)
                with sp.Fori(0, 7) as i:
                    for j in range(6):
                        n = base + 5 + j
                        what, _, e = SLOTS[n]
                        sp.wait_ge(S("lo_done"), 12 * i + FREED[n - RAW][1])
                        fetch(n, what, layer, 2 * i + e)
                static(base + 47, base + 48)
            sp.wait_ge(S("out_kv"), 32)
            sp.wait_ge(S("out_state"), 64)
            sp.wait_ge(S("out_y"), 48)
            sp.wait_ge(S("comb_stored"), 32)

        @block.gpsimd
        def _(pool):
            def lo(u, value):
                n, half, down = UNIT[u]
                pool.wait_ge(S("hi_done"), value)
                nc.gpsimd.tensor_tensor(unit_view(wlo, u, down), raw_unit(n, half, down),
                                        unit_view(whi, u, down).bitcast(F32), ALU.subtract)\
                    .then_inc(S("lo_done"), 1)

            def lo_h(hi_sem, n):
                for k in range(KC):
                    pool.wait_ge(S(hi_sem), KC * n + k + 1)
                    nc.gpsimd.tensor_tensor(hlo[:, k, :], hfk[:, k, :], hhi[:, k, :].bitcast(F32), ALU.subtract)\
                        .then_inc(S("hlo_ready" if hi_sem == "hhi_ready" else "clo_ready"), 1)

            taps = [0]

            def tap():
                g = taps[0]
                k = POOL_CHUNKS[g % 2]
                pool.wait_ge(S("prod_ready"), g + 1)
                if g < 2:
                    nc.gpsimd.tensor_scalar(cacc[:, k, :], prod[:, g % PRODS, :], pcol[:, 0, DWB + k:DWB + k + 1], None, ALU.add)\
                        .then_inc(S("padd_done"), 1)
                else:
                    pool.wait_ge(S("padd_done"), g - 1)
                    nc.gpsimd.tensor_tensor(cacc[:, k, :], cacc[:, k, :], prod[:, g % PRODS, :], ALU.add)\
                        .then_inc(S("padd_done"), 1)
                taps[0] += 1

            for n, first, base in ((0, 0, U_MOE0), (2, U_MOE0 + 94, U_MOE1)):
                for u in range(first, base + 10):
                    if u == first + AHEAD + (2 if n else 0) and n:
                        lo_h("hhi_ready", 2)
                    if u == U_PW2 + AHEAD:
                        lo_h("chi_ready", 0)
                    if u == base + AHEAD:
                        lo_h("hhi_ready", n + 1)
                    if u == 0:
                        lo_h("hhi_ready", 0)
                    if u == U_PW2:
                        while taps[0] < 2 * TAPS:
                            tap()
                    lo(u, u + 1)
                    if 0 <= u - AHEAD - U_PW1 < 12:
                        for _ in range(CONV_TAPS_AT[u - AHEAD - U_PW1]):
                            tap()
                with pool.Fori(0, 7) as i:
                    for j in range(12):
                        lo(base + 10 + j, 12 * i + (base + 11 + j))
            for u in range(U_MOE1 + 94, U_END):
                lo(u, u + 1)

        @block.scalar
        def _(act):
            def hi(u, i=None):
                if u >= U_END:
                    return
                n, half, down = UNIT[u]
                full, used = 16 * (n // RAW + 1), u - UNITS + 1
                act.wait_ge(S(f"raw_full{n % RAW}"), full if i is None else 32 * i + full)
                ge(act, "unit_used", used if i is None else 12 * i + used)
                nc.scalar.activation(unit_view(whi, u, down), raw_unit(n, half, down), ACT.Copy)\
                    .then_inc(S("hi_done"), 1)

            rows = [(0, CCTX, 8, A["c_ctx"].rearrange("(k p) -> k p", p=P)),
                    (0, CC, 8, A["c"][0].rearrange("(k p) -> k p", p=P)),
                    (0, N1, 16, A["norm1_g"].rearrange("l (k p) -> (l k) p", p=P)),
                    (0, N2, 16, A["norm2_g"].rearrange("l (k p) -> (l k) p", p=P)),
                    (0, NF, 8, A["final_g"].rearrange("(k p) -> k p", p=P)),
                    (0, LB, 8, A["hgrn_lower_bound"][0].rearrange("z (k p) -> (z k) p", p=P)),
                    (0, DWB, 8, A["conv_dw_b"][0].rearrange("(k p) -> k p", p=P)),
                    (0, LNG, 8, A["conv_ln_g"][0].rearrange("(k p) -> k p", p=P)),
                    (0, LNB, 8, A["conv_ln_b"][0].rearrange("(k p) -> k p", p=P)),
                    (1, 0, 96, A["ada_b"].rearrange("l (k p) -> (l k) p", p=P)),
                    (2, 0, 120, A["conv_dw"][0, 0:15].rearrange("t (k p) -> (t k) p", p=P)),
                    (3, 0, 128, A["conv_dw"][0, 15:31].rearrange("t (k p) -> (t k) p", p=P))]
            act.dma_start(con[:, :], A["shape_constants"]).then_inc(S("in_con"), 16)
            for g, r, n, src in rows:
                act.dma_start(prow[r:r + n, g, :], src).then_inc(S("in_rows"), 16)
            for r, name in ((QG, "attn_q_gain"), (KG, "attn_k_gain"), (OG, "hgrn_out_gain")):
                for z in range(2):
                    act.dma_start(prow[r:r + 1, 0, HD * z:HD * z + HD], A[name]).then_inc(S("in_rows"), 16)
            act.dma_start(xtok[:, 0, :], A["x_prompt"][0]).then_inc(S("in_x"), 16)
            for b in range(2):
                act.dma_start(xtok[:, 1 + b, :], A["x_sample"][0, P * b:P * b + P, :]).then_inc(S("in_x"), 16)
            for l in range(2):
                act.dma_start(wr[:, l, :, 0:4], A["moe_w_group"][l].rearrange("(k p) g -> p k g", p=P)).then_inc(S("in_small"), 16)
                act.dma_start(wr[:, l, :, 4:20], A["moe_w_expert"][l].rearrange("(k p) g -> p k g", p=P)).then_inc(S("in_small"), 16)
                act.dma_start(rb[:, l, 0:4], A["moe_b_group"][l].partition_broadcast(P)).then_inc(S("in_small"), 16)
                act.dma_start(rb[:, l, 4:20], A["moe_b_expert"][l].partition_broadcast(P)).then_inc(S("in_small"), 16)
            for z in range(2):
                act.dma_start(ck[:, :, z, :], A["cache_k"][0, 0]).then_inc(S("in_small"), 16)

            act.wait_ge(S("pcol_ready"), 4)
            nc.scalar.activation(scond[:, :, :].rearrange("p k g -> p g k"),
                                 pcol[:, 0, 0:16].rearrange("p (g k) -> p g k", g=2), ACT.Silu)\
                .then_inc(S("scond_ready"), 1)
            act.wait_ge(S("lb_shifted"), 1)
            nc.scalar.activation(lbw[:, 1, :], lbw[:, 0, :], ACT.Exp).then_inc(S("lb_exp"), 1)

            def norm_act(n):
                for k in range(KC):
                    if n == 0:
                        act.wait_ge(S("xT_ready"), k + 1)
                    elif k == 0:
                        act.wait_ge(S("x_new"), n)
                    nc.scalar.activation(hfk[:, k, :], xT[:, k, :], ACT.Square).then_inc(S("sq_ready"), 1)
                act.wait_ge(S("ssum_ready"), n + 1)
                nc.scalar.activation(std, bank(4, TOK), ACT.Sqrt, scale=1.0 / D, bias=EPS).then_inc(S("std_ready"), 1)

            def ada_rows(b):
                act.wait_ge(S("ada_used"), 8 * b + 8)
                ge(act, "modT_ready", b)
                for q in range(4):
                    nc.scalar.activation(adarow[:, 512 * q:512 * q + 512], ps[32 * q:32 * q + 2, 7 * 512:8 * 512], ACT.Copy)\
                        .then_inc(S("adarow_ready"), 1)

            def split_h(n):
                for k in range(KC):
                    act.wait_ge(S("hf_ready"), KC * n + k + 1)
                    nc.scalar.activation(hhi[:, k, :], hfk[:, k, :], ACT.Copy).then_inc(S("hhi_ready"), 1)

            norm_act(0)
            ada_rows(0)
            split_h(0)
            for u in range(AHEAD):
                hi(u)

            def key_side(l):
                h = 1 << (l - 1)
                halves = lambda t: t.rearrange("p (n z h) -> p n z h", z=2, h=h)
                act.wait_ge(S("k_ready"), 8)
                ge(act, "ks_level", 2 * (l - 1))
                ge(act, "gram_done", NB * (l - 1))
                nc.scalar.activation(halves(Xs[l % 2])[:, :, 0, :], halves(KS)[:, :, 0, :], ACT.Copy).then_inc(S("x_lower"), 1)
                nc.scalar.activation(halves(Xs[l % 2])[:, :, 1, :], halves(KR)[:, :, 1, :], ACT.Copy).then_inc(S("x_ready"), 1)

            for q in range(N_IN):
                b, slot, half = q % 3, IN_ORDER[q // 2], q % 2
                done = S(f"pb_free{b}")
                act.wait_ge(S("unit_used"), q + 1)
                if slot in (5, 6, 7, 8):
                    c = (slot - 5) * 2 + half
                    if q == 0:
                        act.wait_ge(S("hlo_ready"), KC)
                    nc.scalar.activation(hfk[:, c, :], bank(b, TOK), ACT.Sigmoid).then_inc(done, 1)
                elif slot in (3, 4):
                    c = (slot - 3) * 2 + half
                    nc.scalar.activation(q_t[:, c * TOK:(c + 1) * TOK], bank(b, TOK), ACT.Copy).then_inc(done, 1)
                elif slot in (9, 10):
                    c = (slot - 9) * 2 + half
                    nc.scalar.activation(v_t[:, :, c * P:(c + 1) * P], bank(b, TOK).rearrange("p (b d) -> p b d", b=NB),
                                         ACT.Copy).then_inc(done, 1)
                elif slot in (0, 1):
                    nc.scalar.activation(qk[:, slot * 2 + half, :], bank(b, TOK), ACT.Copy).then_inc(done, 1)
                elif slot == 2 and half == 0:
                    nc.scalar.activation(qk[:, 4, :], bank(b, TOK), ACT.Copy).then_inc(done, 1)
                elif slot == 2:
                    nc.scalar.activation(vat[:, 0, :], bank(b, P), ACT.Copy).then_inc(S("vat_prompt"), 1)
                    nc.scalar.activation(vat[:, 2:4, :], bank(b, 256, P).rearrange("p (b d) -> p b d", b=2),
                                         ACT.Copy).then_inc(done, 1)
                else:
                    if q == N_IN - 4:
                        act.wait_ge(S("gram_done"), NB)
                        act.wait_ge(S("qinit_done"), 2)
                    nc.scalar.activation(sgb[:, (slot - 11) * 2 + half, :], bank(b, TOK), ACT.Silu).then_inc(done, 1)
                if q == 16:
                    ada_rows(1)
                if q + AHEAD < N_IN:
                    hi(q + AHEAD)
                if q in X_AFTER:
                    key_side(X_AFTER[q])

            for step, *at in TAIL:
                if step == "x":
                    key_side(at[0])
                elif step == "square":
                    for b in range(3):
                        act.wait_ge(S(f"pb_free{b}"), (N_IN - b + 2) // 3)
                    nc.scalar.activation(qsq, qk, ACT.Square).then_inc(S("qsq_ready"), 1)
                    act.wait_ge(S("vat_prompt"), 1)
                    act.dma_start(A["out3"][0, 0].rearrange("t h d -> t (h d)"), vat[:, 0, :]).then_inc(S("out_kv"), 16)
                    act.dma_start(vat[:, 1, :], A["cache_v"][0, 0].rearrange("t h d -> t (h d)")).then_inc(S("in_cv"), 16)
                elif step == "sum":
                    i = SUM_ORDER.index(at[0])
                    act.wait_ge(S("qsum_ready"), i + 1)
                    nc.scalar.activation(hstd[:, at[0], :], bank(2 * (i % 2), TOK), ACT.Sqrt, scale=1.0 / HD, bias=EPS)\
                        .then_inc(S("qstd_ready"), 1)
                elif step == "kout":
                    act.wait_ge(S("roped"), 1)
                    for kv in range(2):
                        for z in range(2):
                            for s0, s1, d0 in ((0, 128, 0), (128, 384, 256)):
                                act.dma_start(kall[HD * z:HD * z + HD, kv, d0:d0 + s1 - s0],
                                              qk[HD * kv:HD * kv + HD, 4, s0:s1]).then_inc(S("kall_ready"), 16)
                    act.wait_ge(S("kout_T"), 1)
                    nc.scalar.activation(kout, bank(1, P), ACT.Copy).then_inc(S("kout_ready"), 1)
                    act.wait_ge(S("kout_ready"), 1)
                    act.dma_start(A["out2"][0, 0].rearrange("t h d -> t (h d)"), kout).then_inc(S("out_kv"), 16)
                elif step == "ckt":
                    act.wait_ge(S("ckT_ready"), 1)
                    nc.scalar.activation(kall[:, :, 128:256], bank(1, 256).rearrange("p (h t) -> p h t", h=2), ACT.Copy)\
                        .then_inc(S("kcache_ready"), 1)
                elif step == "att":
                    i = at[0]
                    if i < len(ITEMS):
                        w = P if ITEMS[i][0] == 0 else TOK
                        act.wait_ge(S("nmax_ready"), i + 1)
                        ge(act, "pT_done", i - 1)
                        nc.scalar.activation(prob[i % 2][:, 0:w], bank(0, w), ACT.Exp, bias=nmax[:, i:i + 1],
                                             accum_out=rsum[:, 0, i:i + 1]).then_inc(S("prob_ready"), 1)
                    if 1 <= i <= len(ITEMS):
                        w = P if ITEMS[i - 1][0] == 0 else TOK
                        act.wait_ge(S("pT_done"), i)
                        ge(act, "pv_done", i - 2)
                        nc.scalar.activation(PT[(i - 1) % 2][:, 0:w], bank(1, w), ACT.Copy).then_inc(S("PT_ready"), 1)
                    if i in (9, 17, 25):
                        b = (i - 9) // 8
                        act.wait_ge(S("pv_done"), 8 * b + 8)
                        nc.scalar.activation(hhi[:, 0:4, P * b:P * b + P], bank(2).rearrange("p (c t) -> p c t", c=4),
                                             ACT.Copy).then_inc(S("oahi_ready"), 1)
                elif step == "decay" and at[0] == LEVELS:
                    act.wait_ge(S("sbd_zero"), 1)
                    for which, way in ((0, 0), (2, 1)):
                        for z in range(2):
                            act.dma_start(Sbd[HD * z:HD * z + HD, which, :, HD * z:HD * z + HD],
                                          A["state_hgrn"][0, 0, way].rearrange("(c z) d e -> z d c e", z=2)[z])\
                               .then_inc(S("in_state"), 16)
                elif step == "kt":
                    g = at[0]
                    act.wait_ge(S("kt_T"), g + 1)
                    nc.scalar.activation(KT[g], bank(3 + g % 2), ACT.Copy).then_inc(S("kt_ready"), 1)
                elif step == "rows":
                    ada_rows(at[0])
                elif step == "hout":
                    b = at[0]
                    act.wait_ge(S("o_full"), b + 1)
                    nc.scalar.activation(o_t[:, :, P * b:P * b + P], bank(3 + b).rearrange("p (c t) -> p c t", c=4), ACT.Copy)\
                        .then_inc(S("o_copied"), 1)
                elif step == "hsum":
                    act.wait_ge(S("o_copied"), NB)
                    nc.scalar.activation(osq, o_f, ACT.Square).then_inc(S("osq_ready"), 1)
                    act.wait_ge(S("state_ready"), 8)
                    for way in range(2):
                        for z in range(2):
                            act.dma_start(A["out4"][0, 0, way].rearrange("(c z) d e -> z d c e", z=2)[z],
                                          send[HD * z:HD * z + HD, way, :, :]).then_inc(S("out_state"), 16)
                    for c in range(4):
                        act.wait_ge(S("osum_ready"), c + 1)
                        nc.scalar.activation(ostd[:, c, :], bank(3 + c, TOK), ACT.Sqrt, scale=1.0 / HD, bias=EPS)\
                            .then_inc(S("ostd_ready"), 1)
                elif step == "hnorm":
                    c = at[0]
                    act.wait_ge(S("of_ready"), c + 1)
                    nc.scalar.activation(hhi[:, 4 + c, :], o_t[:, c, :], ACT.Copy).then_inc(S("obhi_ready"), 1)

            act.wait_ge(S("pv_done"), len(ITEMS))
            for u in range(U_OUT, U_OUT + AHEAD):
                hi(u)
            for j in range(8):
                act.wait_ge(S("unit_used"), U_OUT + j + 1)
                hi(U_OUT + j + AHEAD)

            def experts(layer, U0):
                C0 = EXPERTS * layer

                def silu(e, u, f):
                    act.wait_ge(S("unit_used"), u + 2 * f + 1)
                    ge(act, "hmul_done", 2 * (e + C0 - 1) + f + 1)
                    nc.scalar.activation(sact[:, f, :], bank(2 * f, TOK), ACT.Silu).then_inc(S("silu_ready"), 1)

                def hid(e, par, f):
                    act.wait_ge(S("tact_ready"), 2 * (e + C0) + f + 1)
                    nc.scalar.activation(hidhi[:, par, f, :], tact[:, f, :], ACT.Copy).then_inc(S("hidhi_ready"), 1)

                def up(e, u, par, split):
                    silu(e, u, 0)
                    split(0)
                    split(1)
                    hid(e, par, 0)
                    silu(e, u, 1)
                    split(2)
                    split(3)
                    hid(e, par, 1)

                act.wait_ge(S("rt_group"), layer + 1)
                nc.scalar.activation(rt[:, 2, :, 0:4], rt[:, 1, :, 0:4], ACT.Exp).then_inc(S("rt_exp"), 1)
                act.wait_ge(S("rt_second"), layer + 1)
                nc.scalar.activation(rt[:, 13, :, 0:1], rt[:, 12, :, 0:1], ACT.Exp).then_inc(S("rt_exp"), 1)
                act.wait_ge(S("combT_ready"), layer + 1)
                act.dma_start(comb_dram[layer].rearrange("(e t) -> e t", e=EXPERTS), combT).then_inc(S("comb_stored"), 16)
                act.wait_ge(S("comb_stored"), 16 * layer + 16)
                act.dma_start(comb, comb_dram[layer].partition_broadcast(P)).then_inc(S("comb_ready"), 16)

                up(0, U0, 0, lambda j: hi(U0 + j + AHEAD))
                up(1, U0 + 4, 1, lambda j: hi(U0 + 4 + j + AHEAD))
                hi(U0 + 8 + AHEAD)
                hi(U0 + 9 + AHEAD)
                with act.Fori(0, 6) as i:
                    for z in range(2):
                        ub = U0 + 10 + 6 * z
                        split = lambda j, ub=ub: hi(ub + j + AHEAD, i)
                        up(2 * i + (2 + z), 12 * i + ub, z, split)
                        split(4)
                        split(5)
                for z in range(2):
                    ub = U0 + 82 + 6 * z
                    split = lambda j, ub=ub: hi(ub + j + AHEAD)
                    up(14 + z, ub, z, split)
                    split(4)
                    split(5)
                hi(U0 + 94 + AHEAD)
                hi(U0 + 95 + AHEAD)

            norm_act(1)
            split_h(1)
            experts(0, U_MOE0)

            norm_act(2)
            split_h(2)

            def products(g):
                t, k = g // 2, POOL_CHUNKS[g % 2]
                act.wait_ge(S("u_ready"), 2 * k + 2)
                ge(act, "padd_done", g - PRODS + 1)
                nc.scalar.activation(prod[:, g % PRODS, :], upad[:, k, t:t + CONV_N], ACT.Copy, scale=tapw(pcol, t, k))\
                    .then_inc(S("prod_ready"), 1)

            g = 0
            for j in range(16):
                u = U_PW1 + j
                act.wait_ge(S("unit_used"), u + 1)
                if j % 2:
                    ge(act, "u_ready", 2 * (j // 2 - 1))
                    nc.scalar.activation(usig[:, (j // 2) % 2, :], bank(j % 4, TOK), ACT.Sigmoid).then_inc(S("usig_ready"), 1)
                if j < 12:
                    hi(u + AHEAD)
                for _ in range(CONV_TAPS_AT[j]):
                    products(g)
                    g += 1
            ada_rows(4)
            while g < 2 * TAPS:
                products(g)
                g += 1
                if g == 48:
                    ada_rows(5)
            for u in range(U_PW2, U_PW2 + AHEAD):
                hi(u)
            for k in range(KC):
                act.wait_ge(S("cen_ready"), k + 1)
                nc.scalar.activation(hfk[:, k, :], cen[:, k, :], ACT.Square).then_inc(S("csq_ready"), 1)
            act.wait_ge(S("cvar_ready"), 1)
            nc.scalar.activation(std, bank(4, TOK), ACT.Sqrt, scale=1.0 / D, bias=EPS).then_inc(S("cstd_ready"), 1)
            for k in range(KC):
                act.wait_ge(S("cn_ready"), k + 1)
                nc.scalar.activation(hfk[:, k, :], cen[:, k, :], ACT.Silu, scale=pcol[:, 0, LNG + k:LNG + k + 1],
                                     bias=pcol[:, 0, LNB + k:LNB + k + 1]).then_inc(S("cs_ready"), 1)
                act.wait_ge(S("cs_ready"), k + 1)
                nc.scalar.activation(hhi[:, k, :], hfk[:, k, :], ACT.Copy).then_inc(S("chi_ready"), 1)
            for j in range(8):
                act.wait_ge(S("unit_used"), U_PW2 + j + 1)
                hi(U_PW2 + j + AHEAD)
            norm_act(3)
            split_h(3)
            experts(1, U_MOE1)

            norm_act(4)
            for i in range(2 * NB):
                b, h = i // 2, i % 2
                act.wait_ge(S("yT_ready"), i + 1)
                nc.scalar.activation(ytok[:, b, 512 * h:512 * h + 512], bank(5 + i % 2), ACT.Copy).then_inc(S("ytok_ready"), 1)
                if h:
                    act.wait_ge(S("ytok_ready"), i + 1)
                    dst = A["out0"][0] if b == 0 else A["out1"][0, P * (b - 1):P * b, :]
                    act.dma_start(dst, ytok[:, b, :]).then_inc(S("out_y"), 16)

        @block.vector
        def _(dve):
            V = nc.vector
            count = [0]

            def link(ins, back=0):
                count[0] += 1
                ins.then_inc(S("dve_link"), 1)
                ge(dve, "dve_link", count[0] - back)

            def mul(out, a, b):
                return V.tensor_tensor(out, a, b, ALU.mult)

            for g in range(4):
                dve.wait_ge(S("prow_T"), 4)
                V.tensor_copy(pcol[:, g, 0:PROWS[g]], bank(7, PROWS[g], P * g)).then_inc(S("pcol_ready"), 1)
            dve.wait_ge(S("pcol_ready"), 4)
            lbs = pcol[:, 0, LB:LB + 8]
            V.tensor_tensor(lbw[:, 0, :], lbs, lbs, ALU.subtract).then_inc(S("lb_shifted"), 1)
            link(V.tensor_scalar_mul(pcol[:, 0, QG:QG + 1], pcol[:, 0, QG:QG + 1], HD ** -0.5))
            dve.wait_ge(S("lb_exp"), 1)
            link(V.reciprocal(lbw[:, 2, :], lbw[:, 1, :]))
            link(mul(lbw[:, 3, :], lbw[:, 1, :], lbw[:, 2, :]))
            link(V.tensor_tensor(lbw[:, 3, :], lbw[:, 3, :], lbw[:, 3, :], ALU.subtract))
            link(V.tensor_scalar(lbw[:, 4, :], lbw[:, 3, :], -1.0, 1.0, ALU.mult, ALU.add))
            for k in range(KC):
                dve.wait_ge(S("x_T"), k + 1)
                V.tensor_copy(xT[:, k, :], bank(3 + k % 4, TOK)).then_inc(S("xT_ready"), 1)

            def modulation(b):
                l, c0 = b // 3, 16 * (b % 3)
                dve.wait_ge(S("modT_ready"), b + 1)
                V.tensor_tensor(mod[:, l, c0:c0 + 16, :], bank(7, 32).rearrange("p (c g) -> p c g", g=2),
                                pcol[:, 1, 48 * l + c0:48 * l + c0 + 16].unsqueeze(2).broadcast_to([P, 16, 2]),
                                ALU.add).then_inc(S("mod_ready"), 1)

            def amplitude(m, l, sc, gain):
                dve.wait_ge(S("mod_ready"), 3 * l + sc // 16 + 1)
                link(V.tensor_scalar_add(amp[:, m, :, :], mod[:, l, sc:sc + KC, :], 1.0))
                link(mul(amp[:, m, :, :], amp[:, m, :, :],
                         pcol[:, 0, gain:gain + KC].unsqueeze(2).broadcast_to([P, KC, 2])))

            def running_sum(src, w, sem, v0, done):
                for k in range(1, KC):
                    dve.wait_ge(S(sem), v0 + k + 1)
                    ins = V.tensor_tensor(sums[:, 0:w], src[:, k, :], src[:, 0, :] if k == 1 else sums[:, 0:w], ALU.add)
                    if k < KC - 1:
                        link(ins)
                    else:
                        ins.then_inc(S(done), 1)

            def norm_sum(n):
                running_sum(hfk, TOK, "sq_ready", KC * n, "sqsum_ready")

            def inv_std(n):
                dve.wait_ge(S("std_ready"), n + 1)
                link(V.reciprocal(rstd, std))

            def modulate(n, l, sh):
                for k in range(KC):
                    link(mul(hfk[:, k, :], xT[:, k, :], rstd))
                    for g, t0, t1 in GROUPS:
                        ins = V.tensor_scalar(hfk[:, k, t0:t1], hfk[:, k, t0:t1], amp[:, n, k, g:g + 1],
                                              mod[:, l, sh + k, g:g + 1], ALU.mult, ALU.add)
                        if g == 0:
                            ins.then_inc(S("hf_part"), 1)
                        else:
                            ins.then_inc(S("hf_ready"), 1)

            norm_sum(0)
            inv_std(0)
            modulation(0)
            amplitude(0, 0, SC1, N1)
            modulate(0, 0, SH1)

            for c in range(8):
                z, cc = c // 4, c % 4
                g = hfk[:, c, :]
                dve.wait_ge(S(f"pb_free{c % 3}"), c // 3 + 1)
                link(V.tensor_scalar(g, g, lbw[:, 4, c:c + 1], lbw[:, 3, c:c + 1], ALU.mult, ALU.add))
                V.tensor_scalar((KS, KR)[z][:, cc * TOK:(cc + 1) * TOK], g, -1.0, 1.0, ALU.mult, ALU.add)\
                    .then_inc(S("k_ready"), 1)
            for q in range(8, 12):
                dve.wait_ge(S(f"pb_free{q % 3}"), q // 3 + 1)
            mul(QP, q_t, ff).then_inc(S("qinit_done"), 1)
            mul(QQ, q_t, fb).then_inc(S("qinit_done"), 1)

            dve.wait_ge(S("in_con"), 16)

            def level_views(l):
                h = 1 << (l - 1)
                halves = lambda t: t.rearrange("p (n z h) -> p n z h", z=2, h=h)
                tot = lambda t, z: halves(t)[:, :, z, h - 1:h]
                wide = lambda t, z: tot(t, z).broadcast_to([P, 1536 // (2 * h), h])
                return halves, tot, wide

            def level_keys(l):
                halves, _, wide = level_views(l)
                dve.wait_ge(S("x_ready"), l)
                ge(dve, "ks_level", 2 * (l - 1))
                mul(halves(KS)[:, :, 0, :], halves(KS)[:, :, 0, :], wide(ff, 1)).then_inc(S("ks_level"), 1)
                mul(halves(KR)[:, :, 1, :], halves(KR)[:, :, 1, :], wide(fb, 0)).then_inc(S("ks_level"), 1)

            def level_pairs(l, b):
                i = NB * l + b
                dve.wait_ge(S("gram_done"), i + 1)
                V.copy_predicated(AT[:, b, :, :], mask[:, l, :].unsqueeze(1).broadcast_to([P, HEADS, P]),
                                  bank(3 + 2 * (i % 2), 1024).rearrange("p (n i) -> p n i", n=HEADS))\
                    .then_inc(S("gram_copied"), 1)

            def level_decays(l):
                halves, tot, wide = level_views(l)
                dve.wait_ge(S("gram_done"), NB * (l + 1))
                ge(dve, "q_level", 2 * (l - 1))
                mul(halves(QP)[:, :, 1, :], halves(QP)[:, :, 1, :], wide(ff, 0)).then_inc(S("q_level"), 1)
                mul(halves(QQ)[:, :, 0, :], halves(QQ)[:, :, 0, :], wide(fb, 1)).then_inc(S("q_level"), 1)
                dve.wait_ge(S("ks_level"), 2 * l)
                dve.wait_ge(S("q_level"), 2 * l)
                mul(tot(ff, 1), tot(ff, 1), tot(ff, 0)).then_inc(S("tot_level"), 1)
                link(mul(tot(fb, 1), tot(fb, 1), tot(fb, 0)))

            for l in range(len(GRAM_AFTER)):
                if l == 3:
                    modulation(1)
                if l:
                    level_keys(l)
                for b in range(NB):
                    level_pairs(l, b)
                if l:
                    level_decays(l)

            blocks = lambda t: t.rearrange("p (c b t) -> p c b t", c=4, b=NB)[:, :, :, P - 1]
            for step, *at in TAIL:
                if step == "x":
                    level_keys(at[0])
                elif step == "gram":
                    level_pairs(*at)
                elif step == "decay":
                    level_decays(at[0])
                    if at[0] == LEVELS:
                        dve.wait_ge(S("tot_level"), LEVELS)
                        V.tensor_copy(totc[:, 0, :, :], blocks(ff)).then_inc(S("totc_ready"), 1)
                        link(V.tensor_copy(totc[:, 1, :, :], blocks(fb)))
                        V.memset(hf[:, 0:2048], 0.0).then_inc(S("sbd_zero"), 1)
                elif step == "sum":
                    c = at[0]
                    gain = KG if c == 4 else QG
                    dve.wait_ge(S("qstd_ready"), SUM_ORDER.index(c) + 1)
                    link(V.reciprocal(hstd[:, c, :], hstd[:, c, :]))
                    V.scalar_tensor_tensor(out=qk[:, c, :], in0=qk[:, c, :], scalar=pcol[:, 0, gain:gain + 1],
                                           in1=hstd[:, c, :], op0=ALU.mult, op1=ALU.mult).then_inc(S("qn_ready"), 1)
                elif step == "rot":
                    c = at[0]
                    dve.wait_ge(S("qrot_ready"), SUM_ORDER.index(c) + 1)
                    link(mul(qsq[:, c, 0:256], bank(1, 256), con[:, C_SIN:C_SIN + 256]))
                    link(mul(qk[:, c, 128:384], qk[:, c, 128:384], con[:, C_COS:C_COS + 256]))
                    V.tensor_tensor(qk[:, c, 128:384], qk[:, c, 128:384], qsq[:, c, 0:256], ALU.add).then_inc(S("roped"), 1)
                elif step == "att":
                    i = at[0]
                    if i < len(ITEMS):
                        w = P if ITEMS[i][0] == 0 else TOK
                        dve.wait_ge(S("score_ready"), i + 1)
                        V.tensor_reduce(nmax[:, i:i + 1], bank(0, w), axis=AX, op=ALU.max, negate=True)\
                            .then_inc(S("nmax_ready"), 1)
                    if 1 <= i <= len(ITEMS):
                        j = i - 1
                        w = P if ITEMS[j][0] == 0 else TOK
                        dve.wait_ge(S("prob_ready"), j + 1)
                        link(V.reciprocal(rsum[:, 1, j:j + 1], rsum[:, 0, j:j + 1]))
                        V.tensor_scalar_mul(prob[j % 2][:, 0:w], prob[j % 2][:, 0:w], rsum[:, 1, j:j + 1])\
                            .then_inc(S("pnorm_ready"), 1)
                    if i in (9, 17, 25):
                        b = (i - 9) // 8
                        dve.wait_ge(S("oahi_ready"), b + 1)
                        V.tensor_tensor(hlo[:, 0:4, P * b:P * b + P], bank(2).rearrange("p (c t) -> p c t", c=4),
                                        hhi[:, 0:4, P * b:P * b + P].bitcast(F32), ALU.subtract).then_inc(S("oalo_ready"), 1)
                elif step == "cols":
                    modulation(at[0])
                    amplitude(*((1, 0, SC2, N2) if at[0] == 2 else (2, 1, SC1, N1 + KC)))
                elif step == "state":
                    g = at[0]
                    fwd, b = UPDATES[g]
                    dve.wait_ge(S("in_state"), 64)
                    dve.wait_ge(S("u_full"), g + 1)
                    for z in range(2):
                        r = slice(HD * z, HD * z + HD)
                        U = bank(5 + g % 2).rearrange("p (c e) -> p c e", c=4)[r, :, HD * z:HD * z + HD]
                        if g < 2:
                            src, dst = (0, 1) if fwd else (2, 3)
                            w = 0 if fwd else 1
                            link(mul(Sbd[r, dst, :, HD * z:HD * z + HD], Sbd[r, src, :, HD * z:HD * z + HD],
                                     totc[r, w, :, b:b + 1].broadcast_to([HD, 4, HD])))
                            V.tensor_tensor(Sbd[r, dst, :, HD * z:HD * z + HD], U, Sbd[r, dst, :, HD * z:HD * z + HD], ALU.add)\
                                .then_inc(S("state_ready"), 1)
                        else:
                            V.tensor_copy(send[r, g - 2, :, :], U).then_inc(S("state_ready"), 1)
                elif step == "hnorm":
                    c = at[0]
                    dve.wait_ge(S("ostd_ready"), c + 1)
                    link(V.reciprocal(ostd[:, c, :], ostd[:, c, :]))
                    link(V.scalar_tensor_tensor(out=o_t[:, c, :], in0=o_t[:, c, :], scalar=pcol[:, 0, OG:OG + 1],
                                                in1=ostd[:, c, :], op0=ALU.mult, op1=ALU.mult))
                    mul(o_t[:, c, :], o_t[:, c, :], sgb[:, c, :]).then_inc(S("of_ready"), 1)
                    if c:
                        dve.wait_ge(S("obhi_ready"), c)
                        V.tensor_tensor(hlo[:, 3 + c, :], o_t[:, c - 1, :], hhi[:, 3 + c, :].bitcast(F32), ALU.subtract).then_inc(S("oblo_ready"), 1)
            dve.wait_ge(S("obhi_ready"), 4)
            V.tensor_tensor(hlo[:, 7, :], o_t[:, 3, :], hhi[:, 7, :].bitcast(F32), ALU.subtract).then_inc(S("oblo_ready"), 1)

            def residual(src, l, gate, k, last):
                for g, t0, t1 in GROUPS:
                    ins = V.scalar_tensor_tensor(out=xT[:, k, t0:t1], in0=src[:, t0:t1], scalar=mod[:, l, gate + k, g:g + 1],
                                                 in1=xT[:, k, t0:t1], op0=ALU.mult, op1=ALU.add)
                    if g:
                        ins.then_inc(S("x_new" if last and k == KC - 1 else "x_chunk"), 1)

            for j in range(8):
                dve.wait_ge(S("unit_used"), U_OUT + j + 1)
                residual(bank(j % 3, TOK), 0, G1, j, True)

            R = lambda s, n=4: rt[:, s, :, 0:n]

            def first_of(out, x, m, tmp):
                link(V.tensor_tensor(tmp, x, m.broadcast_to([P, NB, 4]), ALU.is_equal))
                link(mul(tmp, tmp, con[:, C_DESC:C_DESC + 4].unsqueeze(1).broadcast_to([P, NB, 4])))
                link(V.tensor_reduce(R(15, 1), tmp, axis=AX, op=ALU.max))
                link(V.tensor_tensor(out, tmp, R(15, 1).broadcast_to([P, NB, 4]), ALU.is_equal))

            def router(l):
                lg = rt[:, 16:18, :, :].rearrange("p a b n -> p (a b n)")[:, 0:60].rearrange("p (b n) -> p b n", b=NB)
                lgg = lg[:, :, 0:4]
                four = lambda t: t.rearrange("p b (g j) -> p b g j", g=4)
                dve.wait_ge(S("logits_ready"), l + 1)
                link(V.tensor_tensor(lg, bank(7, 60).rearrange("p (b n) -> p b n", b=NB),
                                     rb[:, l, :].unsqueeze(1).broadcast_to([P, NB, 20]), ALU.add))
                link(V.tensor_reduce(R(0, 1), lgg, axis=AX, op=ALU.max))
                V.tensor_tensor(R(1), lgg, R(0, 1).broadcast_to([P, NB, 4]), ALU.subtract).then_inc(S("rt_group"), 1)
                first_of(R(3), lgg, R(0, 1), R(4))
                for b in range(NB):
                    link(mul(four(rt[:, 5, b:b + 1, :]), four(lg[:, b:b + 1, 4:20]),
                             R(3)[:, b:b + 1, :].unsqueeze(3).broadcast_to([P, 1, 4, 4])))
                link(V.tensor_reduce(R(6), rt[:, 5, :, :].rearrange("p b (g j) -> p b j g", g=4), axis=AX, op=ALU.add))
                link(V.tensor_reduce(R(7, 1), R(6), axis=AX, op=ALU.max))
                first_of(R(8), R(6), R(7, 1), R(4))
                link(V.tensor_scalar_mul(R(9), R(8), -3.0e38))
                link(V.tensor_tensor(R(9), R(9), R(6), ALU.add))
                link(V.tensor_reduce(R(10, 1), R(9), axis=AX, op=ALU.max))
                first_of(R(11), R(9), R(10, 1), R(4))
                V.tensor_tensor(R(12, 1), R(10, 1), R(7, 1), ALU.subtract).then_inc(S("rt_second"), 1)
                dve.wait_ge(S("rt_exp"), 2 * l + 2)
                link(V.tensor_reduce(R(14, 1), R(2), axis=AX, op=ALU.add))
                link(V.reciprocal(R(14, 1), R(14, 1)))
                link(V.tensor_scalar_add(R(18, 1), R(13, 1), 1.0))
                link(V.reciprocal(R(18, 1), R(18, 1)))
                link(mul(R(18, 1), R(18, 1), R(14, 1)))
                link(mul(R(19, 1), R(18, 1), R(13, 1)))
                link(mul(R(8), R(8), R(18, 1).broadcast_to([P, NB, 4])))
                link(mul(R(11), R(11), R(19, 1).broadcast_to([P, NB, 4])))
                link(V.tensor_tensor(R(8), R(8), R(11), ALU.add))
                for b in range(NB):
                    ins = mul(four(rt[:, 20, b:b + 1, :]), R(3)[:, b:b + 1, :].unsqueeze(3).broadcast_to([P, 1, 4, 4]),
                              R(8)[:, b:b + 1, :].unsqueeze(2).broadcast_to([P, 1, 4, 4]))
                    ins.then_inc(S("combine_ready"), 1)
                dve.wait_ge(S("combine_T"), l + 1)
                V.tensor_copy(combT, ps[0:16, 7 * 512:7 * 512 + TOK]).then_inc(S("combT_ready"), 1)

            def experts(l):
                C0 = EXPERTS * l

                def hid(e, par, u, comb_e):
                    n = 2 * (e + C0)
                    for f in range(2):
                        dve.wait_ge(S("silu_ready"), n + f + 1)
                        dve.wait_ge(S("unit_used"), u + 2 * f + 2)
                        ge(dve, "hidlo_ready", n - 2 + f + 1)
                        mul(tact[:, f, :], sact[:, f, :], bank(2 * f + 1, TOK)).then_inc(S("hmul_done"), 1)
                        dve.wait_ge(S("hmul_done"), n + f + 1)
                        mul(tact[:, f, :], tact[:, f, :], comb_e).then_inc(S("tact_ready"), 1)
                    for f in range(2):
                        dve.wait_ge(S("hidhi_ready"), n + f + 1)
                        V.tensor_tensor(hidlo[:, par, f, :], tact[:, f, :], hidhi[:, par, f, :].bitcast(F32),
                                        ALU.subtract).then_inc(S("hidlo_ready"), 1)

                def gather(e, u):
                    for d in range(2):
                        for z in range(2):
                            t = 4 * (e + C0) + 2 * d + z
                            if z:
                                dve.wait_ge(S("unit_used"), u + d + 1)
                            else:
                                dve.wait_ge(S("y_ready"), 2 * (e + C0) + d + 1)
                            ge(dve, "y_free", t - 3)
                            k = 4 * d + 2 * z
                            src = ps[:, (4 + 2 * z) * 512:(6 + 2 * z) * 512].rearrange("p (c t) -> p c t", c=2)[:, :, 0:TOK]
                            V.tensor_tensor(acc[:, k:k + 2, :], acc[:, k:k + 2, :], src, ALU.add).then_inc(S("y_free"), 1)

                U0 = (U_MOE0, U_MOE1)[l]
                link(V.memset(acc, 0.0))
                dve.wait_ge(S("comb_ready"), 16 * l + 16)
                hid(0, 0, U0, comb[:, 0:TOK])
                hid(1, 1, U0 + 4, comb[:, TOK:2 * TOK])
                gather(0, U0 + 8)
                with dve.Fori(0, 7) as i:
                    for z in range(2):
                        e = 2 * i + (2 + z)
                        hid(e, z, 12 * i + (U0 + 10 + 6 * z), comb[:, bass.ds(TOK * e, TOK)])
                        gather(2 * i + (1 + z), 12 * i + (U0 + 14 + 6 * z))
                gather(EXPERTS - 1, U0 + 94)
                dve.wait_ge(S("y_free"), 4 * (C0 + EXPERTS))
                for k in range(KC):
                    residual(acc[:, k, :], l, G2, k, True)

            norm_sum(1)
            inv_std(1)
            modulate(1, 0, SH2)
            router(0)
            experts(0)

            norm_sum(2)
            inv_std(2)
            link(V.memset(upad, 0.0))
            modulate(2, 1, SH1)
            def gated(k):
                dve.wait_ge(S("usig_ready"), k + 1)
                a = bank((2 * k) % 4, TOK)
                mul(upad[:, k, PAD:PAD + P], a[:, 0:P], usig[:, k % 2, 0:P]).then_inc(S("u_ready"), 1)
                mul(upad[:, k, 2 * PAD + P:2 * PAD + 3 * P], a[:, P:TOK], usig[:, k % 2, P:TOK]).then_inc(S("u_ready"), 1)

            def taps(k0, k1, between):
                dve.wait_ge(S("u_ready"), 2 * k1 + 2)
                for t in range(TAPS):
                    for k in (k0, k1):
                        if t == 0:
                            link(V.tensor_scalar(cacc[:, k, :], upad[:, k, 0:CONV_N], tapw(pcol, 0, k),
                                                 pcol[:, 0, DWB + k:DWB + k + 1], ALU.mult, ALU.add), back=1)
                        else:
                            ins = V.scalar_tensor_tensor(out=cacc[:, k, :], in0=upad[:, k, t:t + CONV_N], scalar=tapw(pcol, t, k),
                                                         in1=cacc[:, k, :], op0=ALU.mult, op1=ALU.add)
                            if t < TAPS - 1:
                                link(ins, back=0 if t == TAPS - 2 and k == k1 else 1)
                            else:
                                ins.then_inc(S("conv_ready"), 1)
                    if t in between:
                        between[t]()

            for k in range(4):
                gated(k)
            taps(2, 3, {8: lambda: gated(4), 18: lambda: gated(5), 28: lambda: gated(6)})
            taps(4, 5, {2: lambda: gated(7), 22: lambda: modulation(4)})
            taps(6, 7, {})
            dve.wait_ge(S("conv_ready"), len(DVE_CHUNKS))
            order = DVE_CHUNKS + POOL_CHUNKS
            for i in range(1, KC):
                if i == len(DVE_CHUNKS):
                    dve.wait_ge(S("padd_done"), 2 * TAPS)
                ins = V.tensor_tensor(sums, cacc[:, order[i], :], cacc[:, order[0], :] if i == 1 else sums, ALU.add)
                if i < KC - 1:
                    link(ins)
                else:
                    ins.then_inc(S("convsum_ready"), 1)
            dve.wait_ge(S("csum_ready"), 1)
            for k in range(KC):
                for b0, b1, o in ((0, 1, 0), (1, 3, BLK[1])):
                    n = P * (b1 - b0)
                    ins = V.scalar_tensor_tensor(out=cen[:, k, P * b0:P * b1], in0=bank(4, n, P * b0), scalar=-1.0 / D,
                                                 in1=cacc[:, k, o:o + n], op0=ALU.mult, op1=ALU.add)
                    ins.then_inc(S("cen_ready" if b0 else "cen_part"), 1)
            running_sum(hfk, TOK, "csq_ready", 0, "csqsum_ready")
            modulation(5)
            amplitude(3, 1, SC2, N2 + KC)
            dve.wait_ge(S("cstd_ready"), 1)
            link(V.reciprocal(rstd, std))
            for k in range(KC):
                mul(cen[:, k, :], cen[:, k, :], rstd).then_inc(S("cn_ready"), 1)
            for j in range(8):
                dve.wait_ge(S("unit_used"), U_PW2 + j + 1)
                residual(bank(j % 4, TOK), 1, G1, j, True)

            norm_sum(3)
            inv_std(3)
            modulate(3, 1, SH2)
            router(1)
            experts(1)

            norm_sum(4)
            inv_std(4)
            for k in range(KC):
                V.scalar_tensor_tensor(out=hfk[:, k, :], in0=xT[:, k, :], scalar=pcol[:, 0, NF + k:NF + k + 1],
                                       in1=rstd, op0=ALU.mult, op1=ALU.mult).then_inc(S("yf_ready"), 1)

        @block.tensor
        def _(pe):
            mm = nc.tensor.matmul
            slot = [0]

            def ada(n_slots):
                for _ in range(n_slots):
                    n, i = ada_at[slot[0]], slot[0] % 8
                    if i == 0:
                        ge(pe, "mod_ready", slot[0] // 8)
                    pe.wait_ge(S(f"raw_full{n % RAW}"), 16 * (n // RAW + 1))
                    q = 32 * (i // 2)
                    for k in range(KC):
                        last = mm(ps[q:q + 2, 7 * 512 + 256 * (i % 2):7 * 512 + 256 * (i % 2) + 256], scond[:, k, :],
                                  raw_k(n % RAW)[:, k, :], start=(k == 0), stop=(k == KC - 1))
                    last.then_inc(S("ada_used"), 1)
                    slot[0] += 1

            def ada_columns(b):
                pe.wait_ge(S("adarow_ready"), 4 * b + 4)
                for c in range(16):
                    last = nc.tensor.transpose(bank(7, 2, 2 * c), adarow[:, P * c:P * c + P], ident[0:2, 0:2])
                last.then_inc(S("modT_ready"), 1)

            ada_at = [n for n, s in enumerate(SLOTS) if s[0] == "ada"]

            def three(out, ahi, alo, bhi, blo, start, stop):
                mm(out, ahi, bhi, start=start, stop=False)
                mm(out, ahi, blo, start=False, stop=False)
                return mm(out, alo, bhi, start=False, stop=stop)

            def unit_ready(u, i=None):
                pe.wait_ge(S("lo_done"), u + 1 if i is None else 12 * i + (u + 1))

            def project(u, b, i=None, per_chunk=None):
                unit_ready(u, i)
                wh, wl = unit_view(whi, u, False), unit_view(wlo, u, False)
                for k in range(KC):
                    if per_chunk:
                        pe.wait_ge(S(per_chunk[0]), per_chunk[1] + k + 1)
                    last = three(bank(b, TOK), wh[:, k, :], wl[:, k, :], hhi[:, k, :], hlo[:, k, :], k == 0, k == KC - 1)
                last.then_inc(S("unit_used"), 1)

            def project_tok(u, b):
                unit_ready(u)
                wh, wl = unit_view(whi, u, False), unit_view(wlo, u, False)
                for t in range(NB):
                    r = slice(P * t, P * t + P)
                    for k in range(KC):
                        last = three(bank(b, P, P * t), hhi[:, k, r], hlo[:, k, r], wh[:, k, :], wl[:, k, :], k == 0, k == KC - 1)
                last.then_inc(S("unit_used"), 1)

            def norm(n):
                pe.wait_ge(S("sqsum_ready"), n + 1)
                mm(bank(4, TOK), ones, sums[:, 0:TOK], start=True, stop=True).then_inc(S("ssum_ready"), 1)

            pe.wait_ge(S("in_con"), 16)
            pe.wait_ge(S("in_rows"), 16 * 18)
            for g in range(4):
                nc.tensor.transpose(bank(7, PROWS[g], P * g), prow[0:PROWS[g], g, :], ident[0:PROWS[g], 0:PROWS[g]])\
                    .then_inc(S("prow_T"), 1)
            pe.wait_ge(S("in_x"), 48)
            for k in range(KC):
                ge(pe, "xT_ready", k - 3)
                for t in range(NB):
                    last = nc.tensor.transpose(bank(3 + k % 4, P, P * t), xtok[:, t, P * k:P * k + P], ident)
                last.then_inc(S("x_T"), 1)
            pe.wait_ge(S("scond_ready"), 1)
            pe.wait_ge(S("pcol_ready"), 4)
            ada(5)
            norm(0)
            ada(3)
            ada_columns(0)

            pair_cols = lambda c, b: slice(TOK * c + P * b, TOK * c + P * b + P)
            zt = Z[:, :].tensor

            def query_side(z, l, c, b):
                h = 1 << (l - 1)
                o = TOK * c + P * b
                return bass.AP(zt, HD * z * Z_LEN + o, [[Z_LEN, HD], [2 * h, P // (2 * h)], [1536 + h, 2], [1, h]])

            def gram(l, b):
                if b == 0 and l == 0:
                    pe.wait_ge(S("k_ready"), 8)
                    for q in range(8, 12):
                        pe.wait_ge(S(f"pb_free{q % 3}"), q // 3 + 1)
                elif b == 0:
                    pe.wait_ge(S("x_ready"), l)
                    if l == 1:
                        pe.wait_ge(S("qinit_done"), 2)
                    ge(pe, "q_level", 2 * (l - 1))
                i = NB * l + b
                ge(pe, "gram_copied", i - 1)
                for c in range(4):
                    for z in range(2):
                        r = slice(HD * z, HD * z + HD)
                        out = bank(3 + 2 * (i % 2) + z, P, P * c)
                        cols = pair_cols(c, b)
                        if l == 0:
                            mm(out, KS[r, cols], q_t[r, cols], start=True, stop=False)
                            last = mm(out, KR[r, cols], q_t[r, cols], start=False, stop=True)
                        else:
                            last = mm(out, Xs[l % 2][r, cols], query_side(z, l, c, b), start=True, stop=True)
                last.then_inc(S("gram_done"), 1)

            for q in range(N_IN):
                ge(pe, f"pb_free{q % 3}", q // 3)
                if IN_ORDER[q // 2] in (9, 10) or q == VAT_Q:
                    project_tok(q, q % 3)
                else:
                    project(q, q % 3, per_chunk=("hlo_ready", 0) if q == 0 else None)
                if q == 17:
                    ada_columns(1)
                if q % 2:
                    ada(ADA_AFTER[q // 2])
                if q in GRAM_AFTER:
                    for b in range(NB):
                        gram(GRAM_AFTER[q], b)

            for step, *at in TAIL:
                if step == "gram":
                    gram(*at)
                elif step == "ada":
                    ada(at[0])
                elif step == "cols":
                    ada_columns(at[0])
                elif step == "sum":
                    i = SUM_ORDER.index(at[0])
                    pe.wait_ge(S("qsq_ready"), 1)
                    ge(pe, "qstd_ready", i - 1)
                    mm(bank(2 * (i % 2), TOK), head_ones, qsq[:, at[0], :], start=True, stop=True).then_inc(S("qsum_ready"), 1)
                elif step == "rot":
                    i = SUM_ORDER.index(at[0])
                    pe.wait_ge(S("qn_ready"), i + 1)
                    ge(pe, "roped", i)
                    mm(bank(1, 256), con[:, C_ROT:C_ROT + P], qk[:, at[0], 128:384], start=True, stop=True)\
                        .then_inc(S("qrot_ready"), 1)
                elif step == "kout":
                    pe.wait_ge(S("roped"), 1)
                    nc.tensor.transpose(bank(1, P), qk[:, 4, 0:P], ident).then_inc(S("kout_T"), 1)
                    pe.wait_ge(S("kout_ready"), 1)
                elif step == "ckt":
                    pe.wait_ge(S("in_small"), 160)
                    pe.wait_ge(S("roped"), 3)
                    for h in range(2):
                        last = nc.tensor.transpose(bank(1, P, P * h), ck[:, h, :, :].rearrange("p z d -> p (z d)"), ident)
                    last.then_inc(S("ckT_ready"), 1)
                    pe.wait_ge(S("kcache_ready"), 1)
                elif step == "att":
                    i = at[0]
                    if i < len(ITEMS):
                        b, n = ITEMS[i]
                        r = slice(HD * (n % 2), HD * (n % 2) + HD)
                        k0, k1 = (0, P) if b == 0 else (P, 512)
                        if i == 0:
                            pe.wait_ge(S("roped"), 5)
                            pe.wait_ge(S("qstd_ready"), 5)
                            pe.wait_ge(S("kall_ready"), 128)
                            pe.wait_ge(S("in_cv"), 16)
                        ge(pe, "prob_ready", i)
                        mm(bank(0, k1 - k0), qk[r, n // 2, P * b:P * b + P], kall[r, n // 4, k0:k1],
                           start=True, stop=True).then_inc(S("score_ready"), 1)
                    if i >= 2:
                        j = i - 2
                        b, n = ITEMS[j]
                        z, kv = n % 2, n // 4
                        pe.wait_ge(S("PT_ready"), j + 1)
                        if n == 0:
                            ge(pe, "oalo_ready", b)
                        blocks = [0] if b == 0 else [1, 2, 3]
                        for t, vb in enumerate(blocks):
                            last = mm(ps[HD * z:HD * z + HD, 512 * 2 + P * (n // 2):512 * 2 + P * (n // 2) + P],
                                      vat[:, vb, HD * kv:HD * kv + HD], PT[j % 2][:, P * t:P * t + P],
                                      start=(t == 0), stop=(t == len(blocks) - 1))
                        last.then_inc(S("pv_done"), 1)
                    if 1 <= i <= len(ITEMS):
                        j = i - 1
                        pe.wait_ge(S("pnorm_ready"), j + 1)
                        ge(pe, "PT_ready", j)
                        for t in range(1 if ITEMS[j][0] == 0 else NB):
                            last = nc.tensor.transpose(bank(1, P, P * t), prob[j % 2][:, P * t:P * t + P], ident)
                        last.then_inc(S("pT_done"), 1)
                elif step == "kt":
                    g = at[0]
                    fwd, b = UPDATES[g]
                    if g < 2:
                        pe.wait_ge(S("ks_level"), 2 * LEVELS)
                        pe.wait_ge(S("gram_copied"), NB * (LEVELS + 1))
                    else:
                        pe.wait_ge(S("kt_ready"), g - 1)
                    for c in range(4):
                        last = nc.tensor.transpose(bank(3 + g % 2, P, P * c), (KS if fwd else KR)[:, pair_cols(c, b)], ident)
                    last.then_inc(S("kt_T"), 1)
                elif step == "state":
                    g = at[0]
                    pe.wait_ge(S("kt_ready"), g + 1)
                    ge(pe, "state_ready", 2 * (g - 1))
                    for c in range(4):
                        last = mm(bank(5 + g % 2, P, P * c), KT[g][:, P * c:P * c + P], v_t[:, UPDATES[g][1], P * c:P * c + P],
                                  start=True, stop=True)
                    last.then_inc(S("u_full"), 1)
                elif step == "hout":
                    b = at[0]
                    pe.wait_ge(S("q_level"), 2 * LEVELS)
                    pe.wait_ge(S("state_ready"), (0, 4, 8)[b] or 4)
                    pe.wait_ge(S("kt_ready"), 4)
                    for c in range(4):
                        out = bank(3 + b, P, P * c)
                        if b:
                            f, w = (0, 3) if b == 1 else (1, 2)
                            mm(out, Sbd[:, f, c, :], QP[:, pair_cols(c, b)], start=True, stop=False)
                            mm(out, Sbd[:, w, c, :], QQ[:, pair_cols(c, b)], start=False, stop=False)
                        for z in range(2):
                            r = slice(HD * z, HD * z + HD)
                            last = mm(ps[r, 512 * (3 + b) + P * c:512 * (3 + b) + P * c + P],
                                      v_t[:, b, P * c + HD * z:P * c + HD * z + HD],
                                      AT[:, b, 4 * z + c, :], start=(b == 0), stop=True)
                    last.then_inc(S("o_full"), 1)
                elif step == "hsum":
                    pe.wait_ge(S("osq_ready"), 1)
                    pe.wait_ge(S("state_ready"), 8)
                    for c in range(4):
                        mm(bank(3 + c, TOK), head_ones, osq[:, TOK * c:TOK * c + TOK], start=True, stop=True)\
                            .then_inc(S("osum_ready"), 1)

            pe.wait_ge(S("oblo_ready"), 4)
            pe.wait_ge(S("oalo_ready"), NB)
            for j in range(8):
                ge(pe, "x_chunk", j - 2)
                project(U_OUT + j, j % 3)

            def experts(l, U0):
                C0 = EXPERTS * l
                h_chunks = ("hlo_ready", KC * (1 if l == 0 else 3))

                def up(e, u, i=None, per_chunk=None):
                    n = 2 * (e + C0)
                    for f in range(2):
                        ge(pe, "silu_ready", n - 2 + f + 1)
                        project(u + 2 * f, 2 * f, i, per_chunk if f == 0 else None)
                        ge(pe, "hmul_done", n - 2 + f + 1)
                        project(u + 2 * f + 1, 2 * f + 1, i)

                def down(e, u, par, i=None):
                    for d in range(2):
                        unit_ready(u + d, i)
                        if d == 0:
                            pe.wait_ge(S("hidlo_ready"), 2 * (e + C0) + 2)
                        wh, wl = unit_view(whi, u + d, True), unit_view(wlo, u + d, True)
                        for z in range(2):
                            ge(pe, "y_free", 4 * (e + C0) + 2 * d + z - 1)
                            for c in (2 * z, 2 * z + 1):
                                for k in range(2):
                                    last = three(bank(4 + c, TOK), wh[:, k, P * c:P * c + P], wl[:, k, P * c:P * c + P],
                                                 hidhi[:, par, k, :], hidlo[:, par, k, :], k == 0, k == 1)
                            last.then_inc(S("unit_used" if z else "y_ready"), 1)

                pe.wait_ge(S("hf_ready"), h_chunks[1] + KC)
                for t in range(NB):
                    for k in range(KC):
                        last = mm(bank(7, 20, 20 * t), hfk[:, k, P * t:P * t + P], wr[:, l, k, :],
                                  start=(k == 0), stop=(k == KC - 1))
                last.then_inc(S("logits_ready"), 1)
                up(0, U0, per_chunk=h_chunks)
                pe.wait_ge(S("combine_ready"), NB * (l + 1))
                for t in range(NB):
                    last = nc.tensor.transpose(ps[0:16, 7 * 512 + P * t:7 * 512 + P * t + P], rt[:, 20, t, :], ident)
                last.then_inc(S("combine_T"), 1)
                up(1, U0 + 4)
                pe.wait_ge(S("combT_ready"), l + 1)
                down(0, U0 + 8, 0)
                with pe.Fori(0, 7) as i:
                    for z in range(2):
                        up(2 * i + (2 + z), U0 + 10 + 6 * z, i)
                        down(2 * i + (1 + z), U0 + 14 + 6 * z, 1 - z, i)
                down(EXPERTS - 1, U0 + 94, 1)

            norm(1)
            experts(0, U_MOE0)

            norm(2)
            for j in range(16):
                g = j // 2
                ge(pe, "usig_ready" if j % 2 else "u_ready", g - 1 if j % 2 else 2 * (g - 1))
                project(U_PW1 + j, j % 4, per_chunk=("hlo_ready", 2 * KC) if j == 0 else None)
                if j % 4 == 3:
                    ada(2)
            ada_columns(4)
            ada(8)
            ada_columns(5)
            pe.wait_ge(S("convsum_ready"), 1)
            mm(bank(4, P), ones, sums[:, 0:P], start=True, stop=True)
            mm(bank(4, 256, P), ones, sums[:, BLK[1]:BLK[1] + 256], start=True, stop=True).then_inc(S("csum_ready"), 1)
            pe.wait_ge(S("csqsum_ready"), 1)
            mm(bank(4, TOK), ones, sums[:, 0:TOK], start=True, stop=True).then_inc(S("cvar_ready"), 1)
            for j in range(8):
                ge(pe, "x_chunk", 14 + j - 3 if j >= 4 else 0)
                project(U_PW2 + j, j % 4, per_chunk=("clo_ready", 0) if j == 0 else None)
            norm(3)
            experts(1, U_MOE1)

            norm(4)
            pe.wait_ge(S("yf_ready"), KC)
            for i in range(2 * NB):
                t, h = i // 2, i % 2
                ge(pe, "ytok_ready", i - 1)
                for c in range(4):
                    last = nc.tensor.transpose(bank(5 + i % 2, P, P * c), hfk[:, 4 * h + c, P * t:P * t + P], ident)
                last.then_inc(S("yT_ready"), 1)


INPUTS = ["x_prompt", "x_sample", "cache_k", "cache_v", "state_hgrn", "c", "c_ctx", "ada_w", "ada_b", "norm1_g",
          "norm2_g", "mix_w_in", "mix_w_out", "attn_q_gain", "attn_k_gain", "hgrn_lower_bound", "hgrn_out_gain",
          "conv_pw1", "conv_dw", "conv_dw_b", "conv_ln_g", "conv_ln_b", "conv_pw2", "moe_w_group", "moe_b_group",
          "moe_w_expert", "moe_b_expert", "moe_w1", "moe_w3", "moe_w2", "final_g"]
OUTPUTS = [(1, 128, D), (1, 256, D), (1, 1, 128, 2, HD), (1, 1, 128, 2, HD), (1, 1, 2, HEADS, HD, HD)]


def kernel(**inputs):
    import concourse.bacc as bacc
    from concourse.bass_utils import run_bass_kernel_spmd

    nc = bacc.Bacc("TRN2", target_bir_lowering=False, num_devices=1, dynamic_dma_scratch_size=1024)
    arrays = {n: np.ascontiguousarray(inputs[n]) for n in INPUTS}
    arrays["shape_constants"] = shape_constants()
    aps = {n: nc.dram_tensor(n, a.shape, mybir.dt.from_np(a.dtype), kind="ExternalInput").ap()
           for n, a in arrays.items()}
    for i, shape in enumerate(OUTPUTS):
        aps[f"out{i}"] = nc.dram_tensor(f"out{i}", shape, F32, kind="ExternalOutput").ap()
    build(nc, aps)
    r = run_bass_kernel_spmd(nc, [arrays], core_ids=[0]).results[0]
    return tuple(r[f"out{i}"] for i in range(len(OUTPUTS)))
```

```python
from contextlib import ExitStack

import numpy as np

import concourse.bass as bass
from concourse import mybir

F32 = mybir.dt.float32
F32R = mybir.dt.float32r

ALU = mybir.AluOpType
ACT = mybir.ActivationFunctionType
AX = mybir.AxisListType.X

P = 128
D = 1024
KC = D // P
TOK = 384
NB = TOK // P
GROUPS = ((0, 0, 128), (1, 128, 384))
HD = 64
HEADS = 8
EPS = 1e-6
EXPERTS = 16
TAPS = 31
PAD = TAPS // 2
UW = PAD + 128 + PAD + 256 + PAD
CONV_N = UW - 2 * PAD
RAW = 3
UNITS = 6
AHEAD = 4
LEVELS = 7

SH1, SC1, G1, SH2, SC2, G2 = (KC * i for i in range(6))

CCTX, CC, N1, N2, NF, LB, DWB, LNG, LNB, QG, KG, OG = 0, 8, 16, 32, 48, 56, 64, 72, 80, 88, 89, 90
PROWS = (91, 96, 120, 128)

C_ID, C_ROT, C_COS, C_SIN, C_SEL, C_ONE, C_DESC, C_MASK = 0, 128, 256, 512, 768, 788, 916, 920
C_W = C_MASK + (LEVELS + 1) * P


def shape_constants():
    c = np.zeros((P, C_W), np.float32)
    c[:, C_ID:C_ID + P] = np.eye(P, dtype=np.float32)
    inv = (10000.0 ** (-np.arange(0, 32, 2, dtype=np.float32) / 32)).astype(np.float32)
    t = np.arange(256)
    for p in range(P):
        d = p % 64
        pos = (t // 64 if d < 32 else t % 64).astype(np.float32)
        ang = (pos * inv[d % 16]).astype(np.float32)
        c[p, C_COS:C_COS + 256] = np.cos(ang)
        c[p, C_SIN:C_SIN + 256] = np.sin(ang)
        if d % 32 < 16:
            c[p + 16, C_ROT + p] = -1.0
        else:
            c[p - 16, C_ROT + p] = 1.0
    c[:64, C_SEL + 8] = 1.0
    c[64:, C_SEL + 9] = 1.0
    c[:, C_ONE:C_ONE + P] = 1.0
    c[:, C_DESC:C_DESC + 4] = [4.0, 3.0, 2.0, 1.0]
    c[:, C_MASK:] = level_masks()
    return c


def level_masks():
    m = np.zeros((P, LEVELS + 1, P), np.float32)
    j, i = np.meshgrid(np.arange(P), np.arange(P), indexing="ij")
    m[:, 0] = j == i
    for l in range(1, LEVELS + 1):
        h = 1 << (l - 1)
        m[:, l] = (j // (2 * h) == i // (2 * h)) & (j // h != i // h)
    return m.reshape(P, (LEVELS + 1) * P)


IN_ORDER = [5, 6, 7, 8, 3, 4, 9, 10, 2, 0, 1, 11, 12]
ADA_AFTER = [1, 1, 1, 1, 1, 1, 1, 1, 0, 2, 1, 1, 1]
N_IN = 2 * len(IN_ORDER)
GRAM_AFTER = {11: 0, 13: 1, 16: 2, 19: 3, 22: 4}
X_AFTER = {11: 1, 14: 2, 16: 3, 19: 4, 23: 5}
VAT_Q = 2 * IN_ORDER.index(2) + 1


def expert_slots(layer):
    s = [("w1", layer, 0), ("w3", layer, 0)]
    for e in range(1, EXPERTS):
        s += [("w1", layer, e), ("w3", layer, e), ("w2", layer, e - 1)]
    return s + [("w2", layer, EXPERTS - 1)]


def plan_slots():
    ada = [("ada", l, j) for l in range(2) for j in range(24)]
    plan, ada = ada[:8], ada[8:]
    for j, n in zip(IN_ORDER, ADA_AFTER):
        plan, ada = plan + [("in", 0, j)] + ada[:n], ada[n:]
    plan += ada[:-16] + [("out", 0, j) for j in range(4)]
    ada, p1 = ada[-16:], []
    for a in range(4):
        p1 += [("pw1", 0, a), ("pw1", 0, a + 4)]
    p1 += ada + [("pw2", 0, j) for j in range(4)]
    bases = (len(plan), len(plan) + 3 * EXPERTS, len(plan) + 3 * EXPERTS + len(p1))
    return plan + expert_slots(0) + p1 + expert_slots(1), bases


def plan_units(slots):
    units, freed, n_ada, n = [], [None] * len(slots), 0, 0
    while n < len(slots):
        kind = slots[n][0]
        if kind == "ada":
            n_ada += 1
            freed[n] = ("ada_used", n_ada)
            n += 1
        elif kind in ("w1", "pw1"):
            for half in range(2):
                for z in range(2):
                    units.append((n + z, half, False))
                    freed[n + z] = ("lo_done", len(units))
            n += 2
        else:
            for half in range(2):
                units.append((n, half, kind == "w2"))
            freed[n] = ("lo_done", len(units))
            n += 1
    return units, freed


NORM_ORDER = [4, 0, 1, 2, 3]

DVE_CHUNKS, POOL_CHUNKS, PE_CHUNK = (0, 1, 4, 5, 6), (2, 3), 7
PRODS = 4
DIAGS = 6
CONV_TAPS_AT = [0] * 8 + [2] * 8


def tapw(pcol, t, k):
    return pcol[:, 2, 8 * t + k:8 * t + k + 1] if t < 15 else pcol[:, 3, 8 * (t - 15) + k:8 * (t - 15) + k + 1]


SLOTS, (B_MOE0, B_P1, B_MOE1) = plan_slots()
UNIT, FREED = plan_units(SLOTS)
U_OUT = N_IN
U_MOE0 = U_OUT + 8
U_PW1 = U_MOE0 + 6 * EXPERTS
U_PW2 = U_PW1 + 16
U_MOE1 = U_PW2 + 8
U_END = U_MOE1 + 6 * EXPERTS
assert len(UNIT) == U_END and U_OUT % UNITS == 2

Y_FREE = 4 * (EXPERTS - 2)
ITEMS = [(b, n) for b in range(NB) for n in range(HEADS)]
UPDATES = [(True, 1), (False, 2), (True, 0), (False, 0)]

TAIL = [("square",), ("gram", 5, 0), ("gram", 5, 1), ("ckt",), ("qsum",), ("gram", 5, 2), ("qnorm", 4), ("decay", 5),
        ("x", 6), ("rot", 4), ("qnorm", 0), ("kout",), ("rot", 0), ("qnorm", 1), ("gram", 6, 0), ("rot", 1),
        ("qnorm", 2), ("gram", 6, 1), ("rot", 2), ("qnorm", 3), ("gram", 6, 2), ("rot", 3), ("decay", 6), ("x", 7),
        ("att", 0), ("att", 1), ("att", 2), ("ada", 1), ("att", 3), ("gram", 7, 0), ("att", 4), ("gram", 7, 1), ("att", 5), ("gram", 7, 2),
        ("att", 6), ("decay", 7), ("ada", 1), ("att", 7), ("kt", 0), ("att", 8), ("kt", 1), ("ada", 1), ("rows", 2),
        ("att", 9), ("state", 0), ("kt", 2), ("att", 10), ("state", 1), ("kt", 3), ("cols", 2), ("att", 11),
        ("state", 2), ("att", 12), ("state", 3), ("hout", 0), ("att", 13), ("hout", 1), ("ada", 1), ("att", 14),
        ("hout", 2), ("att", 15), ("hsum",), ("ada", 1), ("att", 16), ("hnorm", 0), ("ada", 1), ("att", 17),
        ("hnorm", 1), ("ada", 1), ("att", 18), ("hnorm", 2), ("ada", 1), ("att", 19), ("hnorm", 3), ("ada", 1),
        ("att", 20), ("ada", 1), ("att", 21), ("ada", 1), ("rows", 3), ("att", 22), ("att", 23), ("cols", 3),
        ("split", 0), ("att", 24), ("split", 2), ("att", 25)]

Z_LEN = 17792
BLK = (0, PAD + 128, PAD + 256)


def build(nc, A):
    with ExitStack() as ctx:
        sems = {}

        def S(name):
            if name not in sems:
                sems[name] = ctx.enter_context(nc.semaphore(name))
            return sems[name]

        def ge(eng, name, v):
            if isinstance(v, int) and v <= 0:
                return
            eng.wait_ge(S(name), v)

        def sb(name, shape, dt=F32):
            return ctx.enter_context(nc.sbuf_tensor(name, shape, dt))

        ps = ctx.enter_context(nc.psum_tensor("ps", [P, 8 * 512], F32))

        def bank(b, n=512, o=0):
            return ps[:, b * 512 + o:b * 512 + o + n]

        raw = sb("raw", [P, RAW, 2048])
        xT = sb("xT", [P, KC, TOK])
        hf = sb("hf", [P, KC * TOK])
        hhi = sb("hhi", [P, KC, TOK], F32R)
        hlo = sb("hlo", [P, KC, TOK], F32R)
        con = sb("con", [P, C_W])
        pcol = sb("pcol", [P, 4, P])
        scond = sb("scond", [P, KC, 2])
        mod = sb("mod", [P, 2, 48, 2])
        amp = sb("amp", [P, 4, KC, 2])
        lbw = sb("lbw", [P, 5, 8])
        wr = sb("wr", [P, 2, KC, 20])
        rb = sb("rb", [P, 2, 20])
        sums = sb("sums", [P, CONV_N])[:, :]
        std = sb("std", [P, TOK])[:, :]
        rstd = sb("rstd", [P, TOK])[:, :]
        totc = sb("totc", [P, 2, 4, NB])
        send = sb("send", [P, 2, 4, HD])
        ck = sb("ck", [P, 2, 2, HD])
        nmax = sb("nmax", [P, len(ITEMS)])
        rsum = sb("rsum", [P, 2, len(ITEMS)])
        Z = sb("Z", [P, Z_LEN])
        with nc.sbuf_tensor("whi", [P, UNITS, 1024], F32R) as whi, nc.sbuf_tensor("wlo", [P, UNITS, 1024], F32R) as wlo, \
                nc.sbuf_tensor("hid", [P, 2, 2, 2, TOK], F32R) as hid:
            hidhi, hidlo = hid[:, 0], hid[:, 1]
        with nc.sbuf_tensor("att", [P, 2 * UNITS * 1024], F32) as att, nc.sbuf_tensor("adarow", [2, 2048], F32) as adarow:
            pass
        ident = con[:, C_ID:C_ID + P]
        ones = con[:, C_ONE:C_ONE + P]
        head_rows = lambda c, rows: con[:, C_SEL + 8 - 2 * c:C_SEL + 8 - 2 * c + rows]
        mask = con[:, C_MASK:].rearrange("p (l i) -> p l i", i=P).bitcast(mybir.dt.uint32)
        hfk = hf[:, :].rearrange("p (k t) -> p k t", k=KC)

        xtok = Z[:, 0:3072].rearrange("p (b d) -> p b d", b=NB)
        prow = Z[:, 3072:3584].rearrange("p (g r) -> p g r", g=4)
        QQ, QP = Z[:, 0:1536], Z[:, 1536:3072]
        KS, KR = Z[:, 3072:4608], Z[:, 4608:6144]
        Xs = [Z[:, 6144:7680], Z[:, 7680:9216]]
        q_t = Z[:, 9216:10752]
        v_t = Z[:, 10752:12288].rearrange("p (b d) -> p b d", b=NB)
        AT = Z[:, 12288:15360].rearrange("p (b n i) -> p b n i", b=NB, n=HEADS)
        qk = Z[:, 15360:17280].rearrange("p (c t) -> p c t", c=5)
        vat = Z[:, 17280:17792].rearrange("p (b d) -> p b d", b=4)
        ff, fb = hf[:, 0:1536], hf[:, 1536:3072]
        sgb = q_t.rearrange("p (c t) -> p c t", c=4)
        KT = [Z[:, 6144 + 512 * g:6656 + 512 * g] for g in range(4)]
        Sbd = hf[:, 0:2048].rearrange("p (s c e) -> p s c e", s=4, c=4)
        o_f, osq = Z[:, 3072:4608], Z[:, 4608:6144]
        o_t = o_f.rearrange("p (c t) -> p c t", c=4)
        orow = Z[0:8, 12288:12288 + TOK]
        kall = att[:, 0:1024].rearrange("p (h t) -> p h t", h=2)
        prob = [att[:, 1024 + TOK * z:1024 + TOK * (z + 1)] for z in range(2)]
        PT = [att[:, 6144 + TOK * z:6144 + TOK * (z + 1)] for z in range(2)]
        qrow = att[0:10, 6912:6912 + TOK]
        kout = att[:, 7296:7424]
        qsq = att[:, 2048:3968].rearrange("p (c t) -> p c t", c=5)
        comb = Z[:, 0:6144]
        acc = Z[:, 6144:9216].rearrange("p (c t) -> p c t", c=KC)
        sact = Z[:, 9216:9984].rearrange("p (c t) -> p c t", c=2)
        tact = Z[:, 9984:10752].rearrange("p (c t) -> p c t", c=2)
        combT = Z[0:16, 10752:11136]
        lgT = Z[0:20, 12288:12672]
        rt = Z[:, 11136:12288].rearrange("p (s b n) -> p s b n", s=24, b=NB)
        upad = Z[:, 0:3432].rearrange("p (c t) -> p c t", c=KC)
        cacc = Z[:, 3432:6624].rearrange("p (c t) -> p c t", c=KC)
        usig = Z[:, 6624:7392].rearrange("p (c t) -> p c t", c=2)
        prod = Z[:, 10464:10464 + PRODS * CONV_N].rearrange("p (r t) -> p r t", r=PRODS)
        diag = Z[:, 12060:12060 + DIAGS * P].rearrange("p (r n) -> p r n", r=DIAGS)
        cen = Z[:, 7392:10464].rearrange("p (c t) -> p c t", c=KC)
        ytok = Z[:, 0:3072].rearrange("p (b d) -> p b d", b=NB)

        comb_dram = nc.dram_tensor("comb_scratch", [2, EXPERTS * TOK], F32, kind="Internal").ap()

        raw_k = lambda r: raw[:, r, :].rearrange("p (k n) -> p k n", k=KC)
        raw_2 = lambda r: raw[:, r, :].rearrange("p (k n) -> p k n", k=2)

        def raw_unit(n, half, down):
            return raw_2(n % RAW)[:, :, 512 * half:512 * half + 512] if down \
                else raw_k(n % RAW)[:, :, 128 * half:128 * half + 128]

        def unit_view(t, u, down):
            return t[:, u % UNITS, :].rearrange("p (k n) -> p k n", k=2 if down else KC)

        def level_views(l):
            h = 1 << (l - 1)
            halves = lambda t: t.rearrange("p (n z h) -> p n z h", z=2, h=h)
            tot = lambda t, z: halves(t)[:, :, z, h - 1:h]
            wide = lambda t, z: tot(t, z).broadcast_to([P, 1536 // (2 * h), h])
            return halves, tot, wide

        block = ctx.enter_context(nc.Block())

        @block.sync
        def _(sp):
            def load(n, dst, src):
                sp.dma_start(dst, src).then_inc(S(f"raw_full{n % RAW}"), 16)

            def fetch(n, what, where, j):
                if what in ("w1", "w3", "w2"):
                    src = A["moe_" + what][where, j].rearrange("(k p) n -> p k n", p=P)
                    load(n, raw_2(n % RAW) if what == "w2" else raw_k(n % RAW), src)
                else:
                    w = {"ada": A["ada_w"], "in": A["mix_w_in"], "out": A["mix_w_out"],
                         "pw1": A["conv_pw1"], "pw2": A["conv_pw2"]}[what][where]
                    load(n, raw_k(n % RAW), w[:, 256 * j:256 * j + 256].rearrange("(k p) n -> p k n", p=P))

            def static(a, b):
                for n in range(a, b):
                    if n >= RAW:
                        name, v = FREED[n - RAW]
                        sp.wait_ge(S(name), v)
                    fetch(n, *SLOTS[n])

            for layer, first, base in ((0, 0, B_MOE0), (1, B_P1, B_MOE1)):
                static(first, base + 5)
                with sp.Fori(0, 7) as i:
                    for j in range(6):
                        n = base + 5 + j
                        what, _, e = SLOTS[n]
                        sp.wait_ge(S("lo_done"), 12 * i + FREED[n - RAW][1])
                        fetch(n, what, layer, 2 * i + e)
                static(base + 47, base + 48)
            sp.wait_ge(S("out_kv"), 32)
            sp.wait_ge(S("out_state"), 64)
            sp.wait_ge(S("out_y"), 48)
            sp.wait_ge(S("comb_stored"), 32)

        @block.gpsimd
        def _(pool):
            def lo(u, value):
                n, half, down = UNIT[u]
                pool.wait_ge(S("hi_done"), value)
                nc.gpsimd.tensor_tensor(unit_view(wlo, u, down), raw_unit(n, half, down),
                                        unit_view(whi, u, down).bitcast(F32), ALU.subtract)\
                    .then_inc(S("lo_done"), 1)

            def lo_h(hi_sem, n, k0=0, k1=KC):
                for k in range(k0, k1):
                    pool.wait_ge(S(hi_sem), KC * n + k + 1)
                    nc.gpsimd.tensor_tensor(hlo[:, k, :], hfk[:, k, :], hhi[:, k, :].bitcast(F32), ALU.subtract)\
                        .then_inc(S("hlo_ready" if hi_sem == "hhi_ready" else "clo_ready"), 1)

            taps = [0]

            def tap():
                g = taps[0]
                k = POOL_CHUNKS[g % 2]
                pool.wait_ge(S("prod_ready"), g + 1)
                if g < 2:
                    nc.gpsimd.tensor_scalar(cacc[:, k, :], prod[:, g % PRODS, :], pcol[:, 0, DWB + k:DWB + k + 1], None, ALU.add)\
                        .then_inc(S("padd_done"), 1)
                else:
                    pool.wait_ge(S("padd_done"), g - 1)
                    nc.gpsimd.tensor_tensor(cacc[:, k, :], cacc[:, k, :], prod[:, g % PRODS, :], ALU.add)\
                        .then_inc(S("padd_done"), 1)
                taps[0] += 1

            for n, first, base in ((0, 0, U_MOE0), (2, U_MOE0 + 94, U_MOE1)):
                for u in range(first, base + 10):
                    if u == U_PW1 + AHEAD:
                        pool.wait_ge(S("tact_ready"), 2 * EXPERTS)
                        for o in (0, PAD + P, 2 * PAD + 3 * P):
                            nc.gpsimd.memset(upad[:, :, o:o + PAD], 0.0).then_inc(S("pads_zero"), 1)
                        lo_h("hhi_ready", 2)
                    if u == base + AHEAD:
                        lo_h("hhi_ready", n + 1)
                    if u < 2:
                        lo_h("hhi_ready", 0, 4 * u, 4 * u + 4)
                    if u == U_OUT:
                        for l in (LEVELS - 1, LEVELS):
                            halves, _, wide = level_views(l)
                            pool.wait_ge(S("x_ready"), l)
                            pool.wait_ge(S("tot_level"), l - 1)
                            pool.wait_ge(S("ks_level"), 2 * (l - 1))
                            nc.gpsimd.tensor_tensor(halves(KS)[:, :, 0, :], halves(KS)[:, :, 0, :], wide(ff, 1), ALU.mult)\
                                .then_inc(S("ks_level"), 1)
                            nc.gpsimd.tensor_tensor(halves(KR)[:, :, 1, :], halves(KR)[:, :, 1, :], wide(fb, 0), ALU.mult)\
                                .then_inc(S("ks_level"), 1)
                    if u == U_PW2:
                        while taps[0] < 2 * TAPS:
                            tap()
                    if U_PW2 <= u < U_PW2 + 2:
                        lo_h("chi_ready", 0, 4 * (u - U_PW2), 4 * (u - U_PW2) + 4)
                    if u == 13:
                        pool.wait_ge(S("k_ready"), 8)
                        nc.gpsimd.tensor_tensor(Xs[0], KS, KR, ALU.add).then_inc(S("diag_keys"), 1)
                    lo(u, u + 1)
                    if 0 <= u - AHEAD - U_PW1 < 12:
                        for _ in range(CONV_TAPS_AT[u - AHEAD - U_PW1]):
                            tap()
                with pool.Fori(0, 7) as i:
                    for j in range(12):
                        lo(base + 10 + j, 12 * i + (base + 11 + j))
            for u in range(U_MOE1 + 94, U_END):
                lo(u, u + 1)

        @block.scalar
        def _(act):
            def hi(u, i=None):
                if u >= U_END:
                    return
                n, half, down = UNIT[u]
                full, used = 16 * (n // RAW + 1), u - UNITS + 1
                act.wait_ge(S(f"raw_full{n % RAW}"), full if i is None else 32 * i + full)
                ge(act, "unit_used", used if i is None else 12 * i + used)
                nc.scalar.activation(unit_view(whi, u, down), raw_unit(n, half, down), ACT.Copy)\
                    .then_inc(S("hi_done"), 1)

            rows = [(0, CCTX, 8, A["c_ctx"].rearrange("(k p) -> k p", p=P)),
                    (0, CC, 8, A["c"][0].rearrange("(k p) -> k p", p=P)),
                    (0, N1, 16, A["norm1_g"].rearrange("l (k p) -> (l k) p", p=P)),
                    (0, N2, 16, A["norm2_g"].rearrange("l (k p) -> (l k) p", p=P)),
                    (0, NF, 8, A["final_g"].rearrange("(k p) -> k p", p=P)),
                    (0, LB, 8, A["hgrn_lower_bound"][0].rearrange("z (k p) -> (z k) p", p=P)),
                    (0, DWB, 8, A["conv_dw_b"][0].rearrange("(k p) -> k p", p=P)),
                    (0, LNG, 8, A["conv_ln_g"][0].rearrange("(k p) -> k p", p=P)),
                    (0, LNB, 8, A["conv_ln_b"][0].rearrange("(k p) -> k p", p=P)),
                    (1, 0, 96, A["ada_b"].rearrange("l (k p) -> (l k) p", p=P)),
                    (2, 0, 120, A["conv_dw"][0, 0:15].rearrange("t (k p) -> (t k) p", p=P)),
                    (3, 0, 128, A["conv_dw"][0, 15:31].rearrange("t (k p) -> (t k) p", p=P))]
            act.dma_start(con[:, :], A["shape_constants"]).then_inc(S("in_con"), 16)
            for g, r, n, src in rows:
                act.dma_start(prow[r:r + n, g, :], src).then_inc(S("in_rows"), 16)
            for r, name in ((QG, "attn_q_gain"), (KG, "attn_k_gain"), (OG, "hgrn_out_gain")):
                for z in range(2):
                    act.dma_start(prow[r:r + 1, 0, HD * z:HD * z + HD], A[name]).then_inc(S("in_rows"), 16)
            act.dma_start(xtok[:, 0, :], A["x_prompt"][0]).then_inc(S("in_x"), 16)
            for b in range(2):
                act.dma_start(xtok[:, 1 + b, :], A["x_sample"][0, P * b:P * b + P, :]).then_inc(S("in_x"), 16)
            for l in range(2):
                act.dma_start(wr[:, l, :, 0:4], A["moe_w_group"][l].rearrange("(k p) g -> p k g", p=P)).then_inc(S("in_small"), 16)
                act.dma_start(wr[:, l, :, 4:20], A["moe_w_expert"][l].rearrange("(k p) g -> p k g", p=P)).then_inc(S("in_small"), 16)
                act.dma_start(rb[:, l, 0:4], A["moe_b_group"][l].partition_broadcast(P)).then_inc(S("in_small"), 16)
                act.dma_start(rb[:, l, 4:20], A["moe_b_expert"][l].partition_broadcast(P)).then_inc(S("in_small"), 16)
            for z in range(2):
                act.dma_start(ck[:, :, z, :], A["cache_k"][0, 0]).then_inc(S("in_small"), 16)

            act.wait_ge(S("pcol_ready"), 4)
            nc.scalar.activation(scond[:, :, :].rearrange("p k g -> p g k"),
                                 pcol[:, 0, 0:16].rearrange("p (g k) -> p g k", g=2), ACT.Silu)\
                .then_inc(S("scond_ready"), 1)
            act.wait_ge(S("lb_shifted"), 1)
            nc.scalar.activation(lbw[:, 1, :], lbw[:, 0, :], ACT.Exp).then_inc(S("lb_exp"), 1)

            def square(n, k):
                if n == 0:
                    act.wait_ge(S("xT_ready"), k + 1)
                elif k < KC - 1:
                    act.wait_ge(S("x_chunk"), (KC - 1) * (n - 1) + k + 1)
                else:
                    act.wait_ge(S("x_new"), n)
                nc.scalar.activation(hfk[:, k, :], xT[:, k, :], ACT.Square).then_inc(S("sq_ready"), 1)

            def norm_act(n, k0=0):
                for k in range(k0, KC):
                    square(n, k)
                act.wait_ge(S("ssum_ready"), n + 1)
                nc.scalar.activation(std, bank(4, TOK), ACT.Sqrt, scale=1.0 / D, bias=EPS).then_inc(S("std_ready"), 1)

            def ada_rows(b):
                act.wait_ge(S("ada_used"), 8 * b + 8)
                ge(act, "modT_ready", b)
                for q in range(4):
                    nc.scalar.activation(adarow[:, 512 * q:512 * q + 512], ps[32 * q:32 * q + 2, 7 * 512:8 * 512], ACT.Copy)\
                        .then_inc(S("adarow_ready"), 1)

            def split_h(n, k0=0, k1=KC):
                for k in range(k0, k1):
                    act.wait_ge(S("hf_ready"), KC * n + k + 1)
                    nc.scalar.activation(hhi[:, k, :], hfk[:, k, :], ACT.Copy).then_inc(S("hhi_ready"), 1)

            norm_act(0)
            ada_rows(0)
            split_h(0, 0, 4)
            hi(0)
            split_h(0, 4)
            for u in range(1, AHEAD):
                hi(u)

            def key_side(l):
                h = 1 << (l - 1)
                halves = lambda t: t.rearrange("p (n z h) -> p n z h", z=2, h=h)
                act.wait_ge(S("diag_keys"), 1)
                ge(act, "ks_level", 2 * (l - 1))
                ge(act, "gram_done", NB * (l - 1))
                nc.scalar.activation(halves(Xs[l % 2])[:, :, 0, :], halves(KS)[:, :, 0, :], ACT.Copy).then_inc(S("x_lower"), 1)
                nc.scalar.activation(halves(Xs[l % 2])[:, :, 1, :], halves(KR)[:, :, 1, :], ACT.Copy).then_inc(S("x_ready"), 1)

            for q in range(N_IN):
                b, slot, half = q % 3, IN_ORDER[q // 2], q % 2
                done = S(f"pb_free{b}")
                act.wait_ge(S("unit_used"), q + 1)
                if slot in (5, 6, 7, 8):
                    c = (slot - 5) * 2 + half
                    if q == 0:
                        act.wait_ge(S("hlo_ready"), KC)
                    nc.scalar.activation(hfk[:, c, :], bank(b, TOK), ACT.Sigmoid).then_inc(done, 1)
                elif slot in (3, 4):
                    c = (slot - 3) * 2 + half
                    nc.scalar.activation(q_t[:, c * TOK:(c + 1) * TOK], bank(b, TOK), ACT.Copy).then_inc(done, 1)
                elif slot in (9, 10):
                    c0, b0, b1 = (slot - 9) * 256, 2 * half, 2 + half
                    nc.scalar.activation(v_t[:, b0:b1, c0:c0 + 256], bank(b, 256 * (b1 - b0)).rearrange("p (b d) -> p b d", d=256),
                                         ACT.Copy).then_inc(done, 1)
                elif slot in (0, 1):
                    nc.scalar.activation(qk[:, slot * 2 + half, :], bank(b, TOK), ACT.Copy).then_inc(done, 1)
                elif slot == 2 and half == 0:
                    nc.scalar.activation(qk[:, 4, :], bank(b, TOK), ACT.Copy).then_inc(done, 1)
                elif slot == 2:
                    nc.scalar.activation(vat[:, 0, :], bank(b, P), ACT.Copy).then_inc(S("vat_prompt"), 1)
                    nc.scalar.activation(vat[:, 2:4, :], bank(b, 256, P).rearrange("p (b d) -> p b d", b=2),
                                         ACT.Copy).then_inc(done, 1)
                else:
                    if q == N_IN - 4:
                        act.wait_ge(S("gram_done"), NB)
                        act.wait_ge(S("qinit_done"), 2)
                    nc.scalar.activation(sgb[:, (slot - 11) * 2 + half, :], bank(b, TOK), ACT.Silu).then_inc(done, 1)
                if q in X_AFTER:
                    key_side(X_AFTER[q])
                if q == 16:
                    ada_rows(1)
                if q + AHEAD < N_IN:
                    hi(q + AHEAD)

            for step, *at in TAIL:
                if step == "x":
                    key_side(at[0])
                elif step == "square":
                    for b in range(3):
                        act.wait_ge(S(f"pb_free{b}"), (N_IN - b + 2) // 3)
                    nc.scalar.activation(qsq, qk, ACT.Square).then_inc(S("qsq_ready"), 1)
                    act.wait_ge(S("vat_prompt"), 1)
                    act.dma_start(A["out3"][0, 0].rearrange("t h d -> t (h d)"), vat[:, 0, :]).then_inc(S("out_kv"), 16)
                    act.dma_start(vat[:, 1, :], A["cache_v"][0, 0].rearrange("t h d -> t (h d)")).then_inc(S("in_cv"), 16)
                elif step == "qsum":
                    act.wait_ge(S("qsum_ready"), 1)
                    nc.scalar.activation(qrow, ps[0:10, 0:TOK], ACT.Sqrt, scale=1.0 / HD, bias=EPS).then_inc(S("qstd_ready"), 1)
                elif step == "kout":
                    act.wait_ge(S("kout_T"), 1)
                    nc.scalar.activation(kout, bank(1, P), ACT.Copy).then_inc(S("kout_ready"), 1)
                    act.wait_ge(S("roped"), 1)
                    for kv in range(2):
                        for z in range(2):
                            for s0, s1, d0 in ((0, 128, 0), (128, 384, 256)):
                                act.dma_start(kall[HD * z:HD * z + HD, kv, d0:d0 + s1 - s0],
                                              qk[HD * kv:HD * kv + HD, 4, s0:s1]).then_inc(S("kall_ready"), 16)
                    act.wait_ge(S("kout_ready"), 1)
                    act.dma_start(A["out2"][0, 0].rearrange("t h d -> t (h d)"), kout).then_inc(S("out_kv"), 16)
                elif step == "ckt":
                    act.wait_ge(S("ckT_ready"), 1)
                    nc.scalar.activation(kall[:, :, 128:256], bank(1, 256).rearrange("p (h t) -> p h t", h=2), ACT.Copy)\
                        .then_inc(S("kcache_ready"), 1)
                elif step == "att":
                    i = at[0]
                    if i < len(ITEMS):
                        w = P if ITEMS[i][0] == 0 else TOK
                        act.wait_ge(S("nmax_ready"), i + 1)
                        ge(act, "pT_done", i - 1)
                        nc.scalar.activation(prob[i % 2][:, 0:w], bank(0, w), ACT.Exp, bias=nmax[:, i:i + 1],
                                             accum_out=rsum[:, 0, i:i + 1]).then_inc(S("prob_ready"), 1)
                    if 1 <= i <= len(ITEMS):
                        w = P if ITEMS[i - 1][0] == 0 else TOK
                        act.wait_ge(S("pT_done"), i)
                        ge(act, "pv_done", i - 2)
                        nc.scalar.activation(PT[(i - 1) % 2][:, 0:w], bank(1, w), ACT.Copy).then_inc(S("PT_ready"), 1)
                    if i in (9, 17, 25):
                        b = (i - 9) // 8
                        act.wait_ge(S("pv_done"), 8 * b + 8)
                        nc.scalar.activation(hhi[:, 0:4, P * b:P * b + P], bank(2).rearrange("p (c t) -> p c t", c=4),
                                             ACT.Copy).then_inc(S("oahi_ready"), 1)
                elif step == "decay" and at[0] == LEVELS:
                    act.wait_ge(S("sbd_zero"), 1)
                    for which, way in ((0, 0), (2, 1)):
                        for z in range(2):
                            act.dma_start(Sbd[HD * z:HD * z + HD, which, :, HD * z:HD * z + HD],
                                          A["state_hgrn"][0, 0, way].rearrange("(c z) d e -> z d c e", z=2)[z])\
                               .then_inc(S("in_state"), 16)
                elif step == "kt":
                    g = at[0]
                    act.wait_ge(S("kt_T"), g + 1)
                    nc.scalar.activation(KT[g], bank(3 + g % 2), ACT.Copy).then_inc(S("kt_ready"), 1)
                elif step == "rows":
                    ada_rows(at[0])
                elif step == "hout":
                    b = at[0]
                    act.wait_ge(S("o_full"), b + 1)
                    nc.scalar.activation(o_t[:, :, P * b:P * b + P], bank(3 + b).rearrange("p (c t) -> p c t", c=4), ACT.Copy)\
                        .then_inc(S("o_copied"), 1)
                elif step == "hsum":
                    act.wait_ge(S("o_copied"), NB)
                    nc.scalar.activation(osq, o_f, ACT.Square).then_inc(S("osq_ready"), 1)
                    act.wait_ge(S("osum_ready"), 1)
                    nc.scalar.activation(orow, ps[0:8, 6 * 512:6 * 512 + TOK], ACT.Sqrt, scale=1.0 / HD, bias=EPS)\
                        .then_inc(S("ostd_ready"), 1)
                    act.wait_ge(S("state_ready"), 8)
                    for way in range(2):
                        for z in range(2):
                            act.dma_start(A["out4"][0, 0, way].rearrange("(c z) d e -> z d c e", z=2)[z],
                                          send[HD * z:HD * z + HD, way, :, :]).then_inc(S("out_state"), 16)
                elif step == "split":
                    act.wait_ge(S("roped"), 5)
                    for u in (U_OUT + at[0], U_OUT + at[0] + 1):
                        hi(u)
                elif step == "hnorm":
                    c = at[0]
                    act.wait_ge(S("of_ready"), c + 1)
                    nc.scalar.activation(hhi[:, 4 + c, :], o_t[:, c, :], ACT.Copy).then_inc(S("obhi_ready"), 1)

            for j in range(8):
                act.wait_ge(S("unit_used"), U_OUT + j + 1)
                hi(U_OUT + j + AHEAD)
                if j:
                    square(1, j - 1)

            def experts(layer, U0):
                C0 = EXPERTS * layer

                def silu(e, u, f):
                    act.wait_ge(S("unit_used"), u + 2 * f + 1)
                    ge(act, "hmul_done", 2 * (e + C0 - 1) + f + 1)
                    nc.scalar.activation(sact[:, f, :], bank(2 * f, TOK), ACT.Silu).then_inc(S("silu_ready"), 1)

                def hid(e, par, f):
                    act.wait_ge(S("tact_ready"), 2 * (e + C0) + f + 1)
                    nc.scalar.activation(hidhi[:, par, f, :], tact[:, f, :], ACT.Copy).then_inc(S("hidhi_ready"), 1)

                def up(e, u, par, split):
                    silu(e, u, 0)
                    split(0)
                    split(1)
                    hid(e, par, 0)
                    silu(e, u, 1)
                    split(2)
                    split(3)
                    hid(e, par, 1)

                act.wait_ge(S("rt_group"), layer + 1)
                nc.scalar.activation(rt[:, 2, :, 0:4], rt[:, 1, :, 0:4], ACT.Exp).then_inc(S("rt_exp"), 1)
                act.wait_ge(S("rt_second"), layer + 1)
                nc.scalar.activation(rt[:, 13, :, 0:1], rt[:, 12, :, 0:1], ACT.Exp).then_inc(S("rt_exp"), 1)
                silu(0, U0, 0)
                hi(U0 + AHEAD)
                hi(U0 + 1 + AHEAD)
                act.wait_ge(S("combT_ready"), layer + 1)
                act.dma_start(comb_dram[layer].rearrange("(e t) -> e t", e=EXPERTS), combT).then_inc(S("comb_stored"), 16)
                silu(0, U0, 1)
                hi(U0 + 2 + AHEAD)
                act.wait_ge(S("comb_stored"), 16 * layer + 16)
                for c0, c1, done in ((0, 2 * TOK, "comb_ready"), (2 * TOK, EXPERTS * TOK, "comb_rest")):
                    act.dma_start(comb[:, c0:c1], comb_dram[layer, c0:c1].partition_broadcast(P)).then_inc(S(done), 16)
                hi(U0 + 3 + AHEAD)
                hid(0, 0, 0)
                hid(0, 0, 1)
                up(1, U0 + 4, 1, lambda j: hi(U0 + 4 + j + AHEAD))
                hi(U0 + 8 + AHEAD)
                hi(U0 + 9 + AHEAD)
                with act.Fori(0, 6) as i:
                    for z in range(2):
                        ub = U0 + 10 + 6 * z
                        split = lambda j, ub=ub: hi(ub + j + AHEAD, i)
                        up(2 * i + (2 + z), 12 * i + ub, z, split)
                        split(4)
                        split(5)
                for z in range(2):
                    ub = U0 + 82 + 6 * z
                    split = lambda j, ub=ub: hi(ub + j + AHEAD)
                    up(14 + z, ub, z, split)
                    split(4)
                    split(5)
                hi(U0 + 94 + AHEAD)
                hi(U0 + 95 + AHEAD)

            norm_act(1, KC - 1)
            split_h(1)
            experts(0, U_MOE0)

            norm_act(2)
            split_h(2)

            def products(g):
                t, k = g // 2, POOL_CHUNKS[g % 2]
                act.wait_ge(S("u_ready"), 2 * k + 2)
                ge(act, "padd_done", g - PRODS + 1)
                nc.scalar.activation(prod[:, g % PRODS, :], upad[:, k, t:t + CONV_N], ACT.Copy, scale=tapw(pcol, t, k))\
                    .then_inc(S("prod_ready"), 1)

            g = 0
            for j in range(16):
                u = U_PW1 + j
                act.wait_ge(S("unit_used"), u + 1)
                if j % 2:
                    ge(act, "u_ready", 2 * (j // 2 - 1))
                    nc.scalar.activation(usig[:, (j // 2) % 2, :], bank(j % 4, TOK), ACT.Sigmoid).then_inc(S("usig_ready"), 1)
                if j < 12:
                    hi(u + AHEAD)
                for _ in range(CONV_TAPS_AT[j]):
                    products(g)
                    g += 1
            for t in range(TAPS):
                if t == 19:
                    ada_rows(4)
                ge(act, "diag_used", t - DIAGS + 1)
                nc.scalar.activation(diag[:, t % DIAGS, :], ident, ACT.Copy, scale=tapw(pcol, t, PE_CHUNK))\
                    .then_inc(S("diag_ready"), 1)
                for _ in range(1 + t % 2):
                    products(g)
                    g += 1
            while g < 2 * TAPS:
                products(g)
                g += 1
            act.wait_ge(S("pconv_done"), 1)
            nc.scalar.activation(cacc[:, PE_CHUNK, :], bank(5, CONV_N), ACT.Identity,
                                 bias=pcol[:, 0, DWB + PE_CHUNK:DWB + PE_CHUNK + 1]).then_inc(S("pconv_ready"), 1)
            for k in range(KC):
                act.wait_ge(S("cen_ready"), k + 1)
                nc.scalar.activation(hfk[:, k, :], cen[:, k, :], ACT.Square).then_inc(S("csq_ready"), 1)
            act.wait_ge(S("cvar_ready"), 1)
            nc.scalar.activation(std, bank(4, TOK), ACT.Sqrt, scale=1.0 / D, bias=EPS).then_inc(S("cstd_ready"), 1)
            ada_rows(5)
            for k in range(KC):
                if k == 4:
                    hi(U_PW2)
                act.wait_ge(S("cn_ready"), k + 1)
                nc.scalar.activation(hfk[:, k, :], cen[:, k, :], ACT.Silu, scale=pcol[:, 0, LNG + k:LNG + k + 1],
                                     bias=pcol[:, 0, LNB + k:LNB + k + 1]).then_inc(S("cs_ready"), 1)
                act.wait_ge(S("cs_ready"), k + 1)
                nc.scalar.activation(hhi[:, k, :], hfk[:, k, :], ACT.Copy).then_inc(S("chi_ready"), 1)
            for u in range(U_PW2 + 1, U_PW2 + AHEAD):
                hi(u)
            for j in range(8):
                act.wait_ge(S("unit_used"), U_PW2 + j + 1)
                hi(U_PW2 + j + AHEAD)
                if j:
                    square(3, j - 1)
            norm_act(3, KC - 1)
            split_h(3)
            experts(1, U_MOE1)

            norm_act(4)
            for i in range(2 * NB):
                b, h = i // 2, i % 2
                act.wait_ge(S("yT_ready"), i + 1)
                nc.scalar.activation(ytok[:, b, 512 * h:512 * h + 512], bank(5 + i % 2), ACT.Copy).then_inc(S("ytok_ready"), 1)
                if h:
                    act.wait_ge(S("ytok_ready"), i + 1)
                    dst = A["out0"][0] if b == 0 else A["out1"][0, P * (b - 1):P * b, :]
                    act.dma_start(dst, ytok[:, b, :]).then_inc(S("out_y"), 16)

        @block.vector
        def _(dve):
            V = nc.vector
            count = [0]

            def link(ins, back=0):
                count[0] += 1
                ins.then_inc(S("dve_link"), 1)
                ge(dve, "dve_link", count[0] - back)

            def mul(out, a, b):
                return V.tensor_tensor(out, a, b, ALU.mult)

            for g in range(4):
                dve.wait_ge(S("prow_T"), 4)
                V.tensor_copy(pcol[:, g, 0:PROWS[g]], bank(7, PROWS[g], P * g)).then_inc(S("pcol_ready"), 1)
            dve.wait_ge(S("pcol_ready"), 4)
            lbs = pcol[:, 0, LB:LB + 8]
            V.tensor_tensor(lbw[:, 0, :], lbs, lbs, ALU.subtract).then_inc(S("lb_shifted"), 1)
            link(V.tensor_scalar_mul(pcol[:, 0, QG:QG + 1], pcol[:, 0, QG:QG + 1], HD ** -0.5))
            dve.wait_ge(S("lb_exp"), 1)
            link(V.reciprocal(lbw[:, 2, :], lbw[:, 1, :]))
            link(mul(lbw[:, 3, :], lbw[:, 1, :], lbw[:, 2, :]))
            link(V.tensor_tensor(lbw[:, 3, :], lbw[:, 3, :], lbw[:, 3, :], ALU.subtract))
            link(V.tensor_scalar(lbw[:, 4, :], lbw[:, 3, :], -1.0, 1.0, ALU.mult, ALU.add))
            for k in range(KC):
                dve.wait_ge(S("x_T"), k + 1)
                V.tensor_copy(xT[:, k, :], bank(3 + k % 4, TOK)).then_inc(S("xT_ready"), 1)

            def modulation(b):
                l, c0 = b // 3, 16 * (b % 3)
                dve.wait_ge(S("modT_ready"), b + 1)
                V.tensor_tensor(mod[:, l, c0:c0 + 16, :], bank(7, 32).rearrange("p (c g) -> p c g", g=2),
                                pcol[:, 1, 48 * l + c0:48 * l + c0 + 16].unsqueeze(2).broadcast_to([P, 16, 2]),
                                ALU.add).then_inc(S("mod_ready"), 1)

            def amplitude(m, l, sc, gain):
                dve.wait_ge(S("mod_ready"), 3 * l + sc // 16 + 1)
                link(V.tensor_scalar_add(amp[:, m, :, :], mod[:, l, sc:sc + KC, :], 1.0))
                link(mul(amp[:, m, :, :], amp[:, m, :, :],
                         pcol[:, 0, gain:gain + KC].unsqueeze(2).broadcast_to([P, KC, 2])))

            def running_sum(src, w, sem, v0, done, k0=1, k1=KC):
                for k in range(k0, k1):
                    dve.wait_ge(S(sem), v0 + k + 1)
                    ins = V.tensor_tensor(sums[:, 0:w], src[:, k, :], src[:, 0, :] if k == 1 else sums[:, 0:w], ALU.add)
                    if k < KC - 1:
                        link(ins)
                    else:
                        ins.then_inc(S(done), 1)

            def norm_sum(n, k0=1, k1=KC):
                running_sum(hfk, TOK, "sq_ready", KC * n, "sqsum_ready", k0, k1)

            def norm_behind(n, k):
                if 2 <= k < KC - 1:
                    norm_sum(n, k - 1, k)
                elif k == KC - 1:
                    norm_sum(n, k - 1)

            def inv_std(n):
                dve.wait_ge(S("std_ready"), n + 1)
                link(V.reciprocal(rstd, std))

            def modulate(n, l, sh):
                for k in range(KC):
                    link(mul(hfk[:, k, :], xT[:, k, :], rstd))
                    for g, t0, t1 in GROUPS:
                        ins = V.tensor_scalar(hfk[:, k, t0:t1], hfk[:, k, t0:t1], amp[:, n, k, g:g + 1],
                                              mod[:, l, sh + k, g:g + 1], ALU.mult, ALU.add)
                        if g == 0:
                            ins.then_inc(S("hf_part"), 1)
                        else:
                            ins.then_inc(S("hf_ready"), 1)

            norm_sum(0)
            inv_std(0)
            modulation(0)
            amplitude(0, 0, SC1, N1)
            modulate(0, 0, SH1)

            for c in range(8):
                z, cc = c // 4, c % 4
                g = hfk[:, c, :]
                dve.wait_ge(S(f"pb_free{c % 3}"), c // 3 + 1)
                link(V.tensor_scalar(g, g, lbw[:, 4, c:c + 1], lbw[:, 3, c:c + 1], ALU.mult, ALU.add))
                V.tensor_scalar((KS, KR)[z][:, cc * TOK:(cc + 1) * TOK], g, -1.0, 1.0, ALU.mult, ALU.add)\
                    .then_inc(S("k_ready"), 1)
            for q in range(8, 12):
                dve.wait_ge(S(f"pb_free{q % 3}"), q // 3 + 1)
            mul(QP, q_t, ff).then_inc(S("qinit_done"), 1)
            mul(QQ, q_t, fb).then_inc(S("qinit_done"), 1)

            dve.wait_ge(S("in_con"), 16)

            def level_keys(l):
                halves, _, wide = level_views(l)
                dve.wait_ge(S("x_ready"), l)
                ge(dve, "ks_level", 2 * (l - 1))
                mul(halves(KS)[:, :, 0, :], halves(KS)[:, :, 0, :], wide(ff, 1)).then_inc(S("ks_level"), 1)
                mul(halves(KR)[:, :, 1, :], halves(KR)[:, :, 1, :], wide(fb, 0)).then_inc(S("ks_level"), 1)

            def level_pairs(l, b):
                i = NB * l + b
                dve.wait_ge(S("gram_done"), i + 1)
                V.copy_predicated(AT[:, b, :, :], mask[:, l, :].unsqueeze(1).broadcast_to([P, HEADS, P]),
                                  bank(3 + 2 * (i % 2), 1024).rearrange("p (n i) -> p n i", n=HEADS))\
                    .then_inc(S("gram_copied"), 1)

            def level_decays(l):
                halves, tot, wide = level_views(l)
                dve.wait_ge(S("gram_done"), NB * (l + 1))
                ge(dve, "q_level", 2 * (l - 1))
                mul(halves(QP)[:, :, 1, :], halves(QP)[:, :, 1, :], wide(ff, 0)).then_inc(S("q_level"), 1)
                mul(halves(QQ)[:, :, 0, :], halves(QQ)[:, :, 0, :], wide(fb, 1)).then_inc(S("q_level"), 1)
                dve.wait_ge(S("ks_level"), 2 * l)
                dve.wait_ge(S("q_level"), 2 * l)
                mul(tot(ff, 1), tot(ff, 1), tot(ff, 0))
                mul(tot(fb, 1), tot(fb, 1), tot(fb, 0)).then_inc(S("tot_level"), 1)
                dve.wait_ge(S("tot_level"), l)

            for l in range(len(GRAM_AFTER)):
                if l == 3:
                    modulation(1)
                if l:
                    level_keys(l)
                for b in range(NB):
                    level_pairs(l, b)
                if l:
                    level_decays(l)
            level_keys(len(GRAM_AFTER))

            blocks = lambda t: t.rearrange("p (c b t) -> p c b t", c=4, b=NB)[:, :, :, P - 1]
            for step, *at in TAIL:
                if step == "gram":
                    level_pairs(*at)
                elif step == "decay":
                    level_decays(at[0])
                    if at[0] == LEVELS:
                        dve.wait_ge(S("tot_level"), LEVELS)
                        V.tensor_copy(totc[:, 0, :, :], blocks(ff)).then_inc(S("totc_ready"), 1)
                        link(V.tensor_copy(totc[:, 1, :, :], blocks(fb)))
                        V.memset(hf[:, 0:2048], 0.0).then_inc(S("sbd_zero"), 1)
                elif step == "qsum":
                    dve.wait_ge(S("qstd_ready"), 1)
                    V.reciprocal(qrow, qrow).then_inc(S("qrow_ready"), 1)
                elif step == "qnorm":
                    c = at[0]
                    gain = KG if c == 4 else QG
                    i = NORM_ORDER.index(c)
                    dve.wait_ge(S("qbc_ready"), i + 1)
                    V.scalar_tensor_tensor(out=qk[:, c, :], in0=qk[:, c, :], scalar=pcol[:, 0, gain:gain + 1],
                                           in1=bank(2 * (i % 2), TOK), op0=ALU.mult, op1=ALU.mult).then_inc(S("qn_ready"), 1)
                elif step == "rot":
                    c = at[0]
                    dve.wait_ge(S("qrot_ready"), NORM_ORDER.index(c) + 1)
                    link(mul(qsq[:, c, 0:256], bank(1, 256), con[:, C_SIN:C_SIN + 256]))
                    link(mul(qk[:, c, 128:384], qk[:, c, 128:384], con[:, C_COS:C_COS + 256]))
                    V.tensor_tensor(qk[:, c, 128:384], qk[:, c, 128:384], qsq[:, c, 0:256], ALU.add).then_inc(S("roped"), 1)
                elif step == "att":
                    i = at[0]
                    if 1 <= i <= len(ITEMS):
                        j = i - 1
                        w = P if ITEMS[j][0] == 0 else TOK
                        dve.wait_ge(S("prob_ready"), j + 1)
                        link(V.reciprocal(rsum[:, 1, j:j + 1], rsum[:, 0, j:j + 1]))
                        V.tensor_scalar_mul(prob[j % 2][:, 0:w], prob[j % 2][:, 0:w], rsum[:, 1, j:j + 1])\
                            .then_inc(S("pnorm_ready"), 1)
                    if i < len(ITEMS):
                        w = P if ITEMS[i][0] == 0 else TOK
                        dve.wait_ge(S("score_ready"), i + 1)
                        V.tensor_reduce(nmax[:, i:i + 1], bank(0, w), axis=AX, op=ALU.max, negate=True)\
                            .then_inc(S("nmax_ready"), 1)
                    if i in (9, 17, 25):
                        b = (i - 9) // 8
                        dve.wait_ge(S("oahi_ready"), b + 1)
                        V.tensor_tensor(hlo[:, 0:4, P * b:P * b + P], bank(2).rearrange("p (c t) -> p c t", c=4),
                                        hhi[:, 0:4, P * b:P * b + P].bitcast(F32), ALU.subtract).then_inc(S("oalo_ready"), 1)
                elif step == "cols":
                    modulation(at[0])
                    amplitude(*((1, 0, SC2, N2) if at[0] == 2 else (2, 1, SC1, N1 + KC)))
                elif step == "state":
                    g = at[0]
                    fwd, b = UPDATES[g]
                    dve.wait_ge(S("in_state"), 64)
                    dve.wait_ge(S("u_full"), g + 1)
                    for z in range(2):
                        r = slice(HD * z, HD * z + HD)
                        U = bank(5 + g % 2).rearrange("p (c e) -> p c e", c=4)[r, :, HD * z:HD * z + HD]
                        if g < 2:
                            src, dst = (0, 1) if fwd else (2, 3)
                            w = 0 if fwd else 1
                            link(mul(Sbd[r, dst, :, HD * z:HD * z + HD], Sbd[r, src, :, HD * z:HD * z + HD],
                                     totc[r, w, :, b:b + 1].broadcast_to([HD, 4, HD])))
                            V.tensor_tensor(Sbd[r, dst, :, HD * z:HD * z + HD], U, Sbd[r, dst, :, HD * z:HD * z + HD], ALU.add)\
                                .then_inc(S("state_ready"), 1)
                        else:
                            V.tensor_copy(send[r, g - 2, :, :], U).then_inc(S("state_ready"), 1)
                elif step == "hsum":
                    dve.wait_ge(S("ostd_ready"), 1)
                    V.reciprocal(orow, orow).then_inc(S("orow_ready"), 1)
                elif step == "hnorm":
                    c = at[0]
                    dve.wait_ge(S("obc_ready"), c + 1)
                    link(V.scalar_tensor_tensor(out=o_t[:, c, :], in0=o_t[:, c, :], scalar=pcol[:, 0, OG:OG + 1],
                                                in1=bank(3 + c, TOK), op0=ALU.mult, op1=ALU.mult))
                    mul(o_t[:, c, :], o_t[:, c, :], sgb[:, c, :]).then_inc(S("of_ready"), 1)
                    if c:
                        dve.wait_ge(S("obhi_ready"), c)
                        V.tensor_tensor(hlo[:, 3 + c, :], o_t[:, c - 1, :], hhi[:, 3 + c, :].bitcast(F32), ALU.subtract).then_inc(S("oblo_ready"), 1)
            dve.wait_ge(S("obhi_ready"), 4)
            V.tensor_tensor(hlo[:, 7, :], o_t[:, 3, :], hhi[:, 7, :].bitcast(F32), ALU.subtract).then_inc(S("oblo_ready"), 1)

            def add_gated(src, l, gate, k, done):
                for g, t0, t1 in GROUPS:
                    ins = V.scalar_tensor_tensor(out=xT[:, k, t0:t1], in0=src[:, t0:t1], scalar=mod[:, l, gate + k, g:g + 1],
                                                 in1=xT[:, k, t0:t1], op0=ALU.mult, op1=ALU.add)
                    if g:
                        ins.then_inc(S(done), 1)

            def residual(src, l, gate, k):
                add_gated(src, l, gate, k, "x_new" if k == KC - 1 else "x_chunk")

            for j in range(8):
                dve.wait_ge(S("unit_used"), U_OUT + j + 1)
                residual(bank(j % 3, TOK), 0, G1, j)
                norm_behind(1, j)

            R = lambda s, n=4: rt[:, s, :, 0:n]

            def first_of(out, x, m, tmp):
                link(V.tensor_tensor(tmp, x, m.broadcast_to([P, NB, 4]), ALU.is_equal))
                link(mul(tmp, tmp, con[:, C_DESC:C_DESC + 4].unsqueeze(1).broadcast_to([P, NB, 4])))
                link(V.tensor_reduce(R(15, 1), tmp, axis=AX, op=ALU.max))
                link(V.tensor_tensor(out, tmp, R(15, 1).broadcast_to([P, NB, 4]), ALU.is_equal))

            def router(l):
                lg = rt[:, 16:18, :, :].rearrange("p a b n -> p (a b n)")[:, 0:60].rearrange("p (b n) -> p b n", b=NB)
                lgg = lg[:, :, 0:4]
                four = lambda t: t.rearrange("p b (g j) -> p b g j", g=4)
                dve.wait_ge(S("logitsT_ready"), l + 1)
                V.tensor_copy(lgT, ps[0:20, 7 * 512:7 * 512 + TOK]).then_inc(S("logits_copied"), 1)
                dve.wait_ge(S("logits_ready"), l + 1)
                link(V.tensor_tensor(lg, bank(7, 60).rearrange("p (b n) -> p b n", b=NB),
                                     rb[:, l, :].unsqueeze(1).broadcast_to([P, NB, 20]), ALU.add))
                link(V.tensor_reduce(R(0, 1), lgg, axis=AX, op=ALU.max))
                V.tensor_tensor(R(1), lgg, R(0, 1).broadcast_to([P, NB, 4]), ALU.subtract).then_inc(S("rt_group"), 1)
                first_of(R(3), lgg, R(0, 1), R(4))
                for b in range(NB):
                    link(mul(four(rt[:, 5, b:b + 1, :]), four(lg[:, b:b + 1, 4:20]),
                             R(3)[:, b:b + 1, :].unsqueeze(3).broadcast_to([P, 1, 4, 4])))
                link(V.tensor_reduce(R(6), rt[:, 5, :, :].rearrange("p b (g j) -> p b j g", g=4), axis=AX, op=ALU.add))
                link(V.tensor_reduce(R(7, 1), R(6), axis=AX, op=ALU.max))
                first_of(R(8), R(6), R(7, 1), R(4))
                link(V.tensor_scalar_mul(R(9), R(8), -3.0e38))
                link(V.tensor_tensor(R(9), R(9), R(6), ALU.add))
                link(V.tensor_reduce(R(10, 1), R(9), axis=AX, op=ALU.max))
                first_of(R(11), R(9), R(10, 1), R(4))
                V.tensor_tensor(R(12, 1), R(10, 1), R(7, 1), ALU.subtract).then_inc(S("rt_second"), 1)
                dve.wait_ge(S("rt_exp"), 2 * l + 2)
                link(V.tensor_reduce(R(14, 1), R(2), axis=AX, op=ALU.add))
                link(V.reciprocal(R(14, 1), R(14, 1)))
                link(V.tensor_scalar_add(R(18, 1), R(13, 1), 1.0))
                link(V.reciprocal(R(18, 1), R(18, 1)))
                link(mul(R(18, 1), R(18, 1), R(14, 1)))
                link(mul(R(19, 1), R(18, 1), R(13, 1)))
                link(mul(R(8), R(8), R(18, 1).broadcast_to([P, NB, 4])))
                link(mul(R(11), R(11), R(19, 1).broadcast_to([P, NB, 4])))
                link(V.tensor_tensor(R(8), R(8), R(11), ALU.add))
                for b in range(NB):
                    ins = mul(four(rt[:, 20, b:b + 1, :]), R(3)[:, b:b + 1, :].unsqueeze(3).broadcast_to([P, 1, 4, 4]),
                              R(8)[:, b:b + 1, :].unsqueeze(2).broadcast_to([P, 1, 4, 4]))
                    ins.then_inc(S("combine_ready"), 1)
                dve.wait_ge(S("combine_T"), l + 1)
                V.tensor_copy(combT, ps[0:16, 7 * 512:7 * 512 + TOK]).then_inc(S("combT_ready"), 1)

            def experts(l):
                C0 = EXPERTS * l

                def hid(e, par, u, comb_e, first=False):
                    n = 2 * (e + C0)
                    for f in range(2):
                        dve.wait_ge(S("silu_ready"), n + f + 1)
                        dve.wait_ge(S("unit_used"), u + 2 * f + 2)
                        ge(dve, "hidlo_ready", n - 2 + f + 1)
                        mul(tact[:, f, :], sact[:, f, :], bank(2 * f + 1, TOK)).then_inc(S("hmul_done"), 1)
                        if not first:
                            dve.wait_ge(S("hmul_done"), n + f + 1)
                            mul(tact[:, f, :], tact[:, f, :], comb_e).then_inc(S("tact_ready"), 1)
                    if first:
                        dve.wait_ge(S("comb_ready"), 16 * l + 16)
                        dve.wait_ge(S("hmul_done"), n + 2)
                        for f in range(2):
                            mul(tact[:, f, :], tact[:, f, :], comb_e).then_inc(S("tact_ready"), 1)
                    for f in range(2):
                        dve.wait_ge(S("hidhi_ready"), n + f + 1)
                        V.tensor_tensor(hidlo[:, par, f, :], tact[:, f, :], hidhi[:, par, f, :].bitcast(F32),
                                        ALU.subtract).then_inc(S("hidlo_ready"), 1)

                def gather(e, u, complete=False):
                    for d in range(2):
                        for z in range(2):
                            t = 4 * e + (Y_FREE * l + 2 * d + z)
                            if z:
                                dve.wait_ge(S("unit_used"), u + d + 1)
                            else:
                                dve.wait_ge(S("y_ready"), 2 * (e + C0) + d + 1)
                            ge(dve, "y_free", t - 3)
                            k = 4 * d + 2 * z
                            src = ps[:, (4 + 2 * z) * 512:(6 + 2 * z) * 512].rearrange("p (c t) -> p c t", c=2)[:, :, 0:TOK]
                            V.tensor_tensor(acc[:, k:k + 2, :], acc[:, k:k + 2, :], src, ALU.add).then_inc(S("y_free"), 1)
                            if complete:
                                dve.wait_ge(S("y_free"), t + 1)
                                for kk in (k, k + 1):
                                    add_gated(acc[:, kk, :], l, G2, kk, "x_part")

                def finish(e, u, last):
                    for k in range(KC):
                        if k % 4 >= 2:
                            dve.wait_ge(S("unit_used"), u + k // 4 + 1)
                        else:
                            dve.wait_ge(S("y_ready"), 2 * (e + C0) + k // 4 + 1)
                        dve.wait_ge(S("x_part"), KC * (2 * l + (1 if last else 0)) + k + 1)
                        if last:
                            residual(bank(4 + k % 4, TOK), l, G2, k)
                            norm_behind(2 * l + 2, k)
                        else:
                            add_gated(bank(4 + k % 4, TOK), l, G2, k, "x_part")

                U0 = (U_MOE0, U_MOE1)[l]
                link(V.memset(acc, 0.0))
                hid(0, 0, U0, comb[:, 0:TOK], True)
                hid(1, 1, U0 + 4, comb[:, TOK:2 * TOK])
                gather(0, U0 + 8)
                dve.wait_ge(S("comb_rest"), 16 * l + 16)
                with dve.Fori(0, 6) as i:
                    for z in range(2):
                        e = 2 * i + (2 + z)
                        hid(e, z, 12 * i + (U0 + 10 + 6 * z), comb[:, bass.ds(TOK * e, TOK)])
                        gather(2 * i + (1 + z), 12 * i + (U0 + 14 + 6 * z))
                hid(14, 0, U0 + 82, comb[:, TOK * 14:TOK * 15])
                gather(13, U0 + 86, True)
                hid(15, 1, U0 + 88, comb[:, TOK * 15:TOK * 16])
                finish(14, U0 + 92, False)
                finish(15, U0 + 94, True)

            inv_std(1)
            modulate(1, 0, SH2)
            router(0)
            experts(0)

            inv_std(2)
            modulate(2, 1, SH1)
            def gated(k):
                dve.wait_ge(S("usig_ready"), k + 1)
                a = bank((2 * k) % 4, TOK)
                mul(upad[:, k, PAD:PAD + P], a[:, 0:P], usig[:, k % 2, 0:P]).then_inc(S("u_ready"), 1)
                mul(upad[:, k, 2 * PAD + P:2 * PAD + 3 * P], a[:, P:TOK], usig[:, k % 2, P:TOK]).then_inc(S("u_ready"), 1)

            def taps(chunks, between):
                n = len(chunks)
                dve.wait_ge(S("u_ready"), 2 * chunks[-1] + 2)
                for t in range(TAPS):
                    for k in chunks:
                        if t == 0:
                            link(V.tensor_scalar(cacc[:, k, :], upad[:, k, 0:CONV_N], tapw(pcol, 0, k),
                                                 pcol[:, 0, DWB + k:DWB + k + 1], ALU.mult, ALU.add), back=n - 1)
                        else:
                            ins = V.scalar_tensor_tensor(out=cacc[:, k, :], in0=upad[:, k, t:t + CONV_N], scalar=tapw(pcol, t, k),
                                                         in1=cacc[:, k, :], op0=ALU.mult, op1=ALU.add)
                            if t < TAPS - 1:
                                link(ins, back=0 if t == TAPS - 2 and k == chunks[-1] else n - 1)
                            else:
                                ins.then_inc(S("conv_ready"), 1)
                    if t in between:
                        between[t]()

            dve.wait_ge(S("pads_zero"), 3)
            gated(0)
            gated(1)
            taps((0, 1), {6: lambda: gated(2), 12: lambda: gated(3), 20: lambda: gated(4), 26: lambda: gated(5),
                          28: lambda: gated(6)})
            taps((4, 5, 6), {4: lambda: gated(7), 24: lambda: modulation(4)})
            dve.wait_ge(S("conv_ready"), len(DVE_CHUNKS))
            order = DVE_CHUNKS + (PE_CHUNK,) + POOL_CHUNKS
            for i in range(1, KC):
                if order[i] == PE_CHUNK:
                    dve.wait_ge(S("pconv_ready"), 1)
                if order[i] == POOL_CHUNKS[0]:
                    dve.wait_ge(S("padd_done"), 2 * TAPS)
                ins = V.tensor_tensor(sums, cacc[:, order[i], :], cacc[:, order[0], :] if i == 1 else sums, ALU.add)
                if i < KC - 1:
                    link(ins)
                else:
                    ins.then_inc(S("convsum_ready"), 1)
            dve.wait_ge(S("csum_ready"), 1)
            for k in range(KC):
                for b0, b1, o in ((0, 1, 0), (1, 3, BLK[1])):
                    n = P * (b1 - b0)
                    ins = V.scalar_tensor_tensor(out=cen[:, k, P * b0:P * b1], in0=bank(4, n, P * b0), scalar=-1.0 / D,
                                                 in1=cacc[:, k, o:o + n], op0=ALU.mult, op1=ALU.add)
                    ins.then_inc(S("cen_ready" if b0 else "cen_part"), 1)
            running_sum(hfk, TOK, "csq_ready", 0, "csqsum_ready")
            dve.wait_ge(S("cstd_ready"), 1)
            link(V.reciprocal(rstd, std))
            for k in range(KC):
                mul(cen[:, k, :], cen[:, k, :], rstd).then_inc(S("cn_ready"), 1)
            modulation(5)
            amplitude(3, 1, SC2, N2 + KC)
            for j in range(8):
                dve.wait_ge(S("unit_used"), U_PW2 + j + 1)
                residual(bank(j % 4, TOK), 1, G1, j)
                norm_behind(3, j)

            inv_std(3)
            modulate(3, 1, SH2)
            router(1)
            experts(1)

            inv_std(4)
            for k in range(KC):
                V.scalar_tensor_tensor(out=hfk[:, k, :], in0=xT[:, k, :], scalar=pcol[:, 0, NF + k:NF + k + 1],
                                       in1=rstd, op0=ALU.mult, op1=ALU.mult).then_inc(S("yf_ready"), 1)

        @block.tensor
        def _(pe):
            mm = nc.tensor.matmul
            slot = [0]

            def ada(n_slots):
                for _ in range(n_slots):
                    n, i = ada_at[slot[0]], slot[0] % 8
                    if i == 0:
                        ge(pe, "mod_ready", slot[0] // 8)
                    pe.wait_ge(S(f"raw_full{n % RAW}"), 16 * (n // RAW + 1))
                    q = 32 * (i // 2)
                    for k in range(KC):
                        last = mm(ps[q:q + 2, 7 * 512 + 256 * (i % 2):7 * 512 + 256 * (i % 2) + 256], scond[:, k, :],
                                  raw_k(n % RAW)[:, k, :], start=(k == 0), stop=(k == KC - 1))
                    last.then_inc(S("ada_used"), 1)
                    slot[0] += 1

            def ada_columns(b):
                pe.wait_ge(S("adarow_ready"), 4 * b + 4)
                for c in range(16):
                    last = nc.tensor.transpose(bank(7, 2, 2 * c), adarow[:, P * c:P * c + P], ident[0:2, 0:2])
                last.then_inc(S("modT_ready"), 1)

            ada_at = [n for n, s in enumerate(SLOTS) if s[0] == "ada"]

            def three(out, ahi, alo, bhi, blo, start, stop):
                mm(out, ahi, bhi, start=start, stop=False)
                mm(out, ahi, blo, start=False, stop=False)
                return mm(out, alo, bhi, start=False, stop=stop)

            def unit_ready(u, i=None):
                pe.wait_ge(S("lo_done"), u + 1 if i is None else 12 * i + (u + 1))

            def project(u, b, i=None, per_chunk=None, between=None, order=range(KC), late=None):
                unit_ready(u, i)
                wh, wl = unit_view(whi, u, False), unit_view(wlo, u, False)
                for k in order:
                    if between:
                        between(k)
                    if late and k == 0:
                        pe.wait_ge(S(late[0]), late[1])
                    if per_chunk:
                        pe.wait_ge(S(per_chunk[0]), per_chunk[1] + k + 1)
                    last = three(bank(b, TOK), wh[:, k, :], wl[:, k, :], hhi[:, k, :], hlo[:, k, :], k == order[0], k == order[-1])
                last.then_inc(S("unit_used"), 1)

            def project_tok(u, b):
                unit_ready(u)
                wh, wl = unit_view(whi, u, False), unit_view(wlo, u, False)
                for t in range(NB):
                    r = slice(P * t, P * t + P)
                    for k in range(KC):
                        last = three(bank(b, P, P * t), hhi[:, k, r], hlo[:, k, r], wh[:, k, :], wl[:, k, :], k == 0, k == KC - 1)
                last.then_inc(S("unit_used"), 1)

            def project_tok_pair(u, b0, b1):
                unit_ready(u + 1)
                pair = lambda t, k: t[:, u % UNITS:u % UNITS + 2, P * k:P * k + P]
                for t in range(NB):
                    r = slice(P * t, P * t + P)
                    out = bank(b1 if t == 2 else b0, 256, 256 * (t % 2)).rearrange("p (z n) -> p z n", z=2)
                    for k in range(KC):
                        last = three(out, hhi[:, k, r], hlo[:, k, r], pair(whi, k), pair(wlo, k), k == 0, k == KC - 1)
                last.then_inc(S("unit_used"), 2)

            def norm(n):
                pe.wait_ge(S("sqsum_ready"), n + 1)
                mm(bank(4, TOK), ones, sums[:, 0:TOK], start=True, stop=True).then_inc(S("ssum_ready"), 1)

            pe.wait_ge(S("in_con"), 16)
            pe.wait_ge(S("in_rows"), 16 * 18)
            for g in range(4):
                nc.tensor.transpose(bank(7, PROWS[g], P * g), prow[0:PROWS[g], g, :], ident[0:PROWS[g], 0:PROWS[g]])\
                    .then_inc(S("prow_T"), 1)
            pe.wait_ge(S("scond_ready"), 1)
            pe.wait_ge(S("pcol_ready"), 4)
            ada(3)
            pe.wait_ge(S("in_x"), 48)
            for k in range(KC):
                ge(pe, "xT_ready", k - 3)
                for t in range(NB):
                    last = nc.tensor.transpose(bank(3 + k % 4, P, P * t), xtok[:, t, P * k:P * k + P], ident)
                last.then_inc(S("x_T"), 1)
            ada(2)
            norm(0)
            ada(3)
            ada_columns(0)

            pair_cols = lambda c, b: slice(TOK * c + P * b, TOK * c + P * b + P)
            zt = Z[:, :].tensor

            def query_side(z, l, c, b):
                h = 1 << (l - 1)
                o = TOK * c + P * b
                return bass.AP(zt, HD * z * Z_LEN + o, [[Z_LEN, HD], [2 * h, P // (2 * h)], [1536 + h, 2], [1, h]])

            def gram(l, b):
                if b == 0 and l == 0:
                    pe.wait_ge(S("diag_keys"), 1)
                    for q in range(8, 12):
                        pe.wait_ge(S(f"pb_free{q % 3}"), q // 3 + 1)
                elif b == 0:
                    pe.wait_ge(S("x_ready"), l)
                    if l == 1:
                        pe.wait_ge(S("qinit_done"), 2)
                    ge(pe, "q_level", 2 * (l - 1))
                i = NB * l + b
                ge(pe, "gram_copied", i - 1)
                for c in range(4):
                    for z in range(2):
                        r = slice(HD * z, HD * z + HD)
                        out = bank(3 + 2 * (i % 2) + z, P, P * c)
                        cols = pair_cols(c, b)
                        if l == 0:
                            last = mm(out, Xs[0][r, cols], q_t[r, cols], start=True, stop=True)
                        else:
                            last = mm(out, Xs[l % 2][r, cols], query_side(z, l, c, b), start=True, stop=True)
                last.then_inc(S("gram_done"), 1)

            for q in range(N_IN):
                ge(pe, f"pb_free{q % 3}", q // 3)
                if IN_ORDER[q // 2] in (9, 10):
                    if q % 2 == 0:
                        ge(pe, f"pb_free{(q + 1) % 3}", (q + 1) // 3)
                        project_tok_pair(q, q % 3, (q + 1) % 3)
                elif q == VAT_Q:
                    project_tok(q, q % 3)
                else:
                    project(q, q % 3, per_chunk=("hlo_ready", 0) if q == 0 else None)
                if q == 17:
                    ada_columns(1)
                if q % 2 == 0:
                    ada(ADA_AFTER[q // 2])
                if q in GRAM_AFTER:
                    for b in range(NB):
                        gram(GRAM_AFTER[q], b)

            def head_features(row, c, b):
                n = row.shape[0]
                for z in range(2):
                    h = 2 * c + z
                    last = mm(ps[HD * z:HD * z + HD, 512 * b:512 * b + TOK], ident[0:n, h:h + 1].broadcast_to([n, HD]), row,
                              start=True, stop=True)
                return last

            for step, *at in TAIL:
                if step == "gram":
                    gram(*at)
                elif step == "ada":
                    ada(at[0])
                elif step == "cols":
                    ada_columns(at[0])
                elif step == "qsum":
                    pe.wait_ge(S("qsq_ready"), 1)
                    for c in range(5):
                        last = mm(ps[0:10, 0:TOK], head_rows(c, 10), qsq[:, c, :], start=(c == 0), stop=(c == 4))
                    last.then_inc(S("qsum_ready"), 1)
                elif step == "qnorm":
                    c = at[0]
                    i = NORM_ORDER.index(c)
                    pe.wait_ge(S("qrow_ready"), 1)
                    ge(pe, "qn_ready", i - 1)
                    head_features(qrow, c, 2 * (i % 2)).then_inc(S("qbc_ready"), 1)
                elif step == "rot":
                    i = NORM_ORDER.index(at[0])
                    pe.wait_ge(S("qn_ready"), i + 1)
                    ge(pe, "roped", i)
                    pe.wait_ge(S("kcache_ready" if i == 0 else "kout_ready"), 1)
                    mm(bank(1, 256), con[:, C_ROT:C_ROT + P], qk[:, at[0], 128:384], start=True, stop=True)\
                        .then_inc(S("qrot_ready"), 1)
                elif step == "kout":
                    pe.wait_ge(S("roped"), 1)
                    nc.tensor.transpose(bank(1, P), qk[:, 4, 0:P], ident).then_inc(S("kout_T"), 1)
                elif step == "ckt":
                    pe.wait_ge(S("in_small"), 160)
                    pe.wait_ge(S("qsq_ready"), 1)
                    for h in range(2):
                        last = nc.tensor.transpose(bank(1, P, P * h), ck[:, h, :, :].rearrange("p z d -> p (z d)"), ident)
                    last.then_inc(S("ckT_ready"), 1)
                elif step == "att":
                    i = at[0]
                    if i < len(ITEMS):
                        b, n = ITEMS[i]
                        r = slice(HD * (n % 2), HD * (n % 2) + HD)
                        k0, k1 = (0, P) if b == 0 else (P, 512)
                        if i == 0:
                            pe.wait_ge(S("roped"), 5)
                            pe.wait_ge(S("qn_ready"), 5)
                            pe.wait_ge(S("kall_ready"), 128)
                            pe.wait_ge(S("in_cv"), 16)
                        ge(pe, "prob_ready", i)
                        mm(bank(0, k1 - k0), qk[r, n // 2, P * b:P * b + P], kall[r, n // 4, k0:k1],
                           start=True, stop=True).then_inc(S("score_ready"), 1)
                    if i >= 2:
                        j = i - 2
                        b, n = ITEMS[j]
                        z, kv = n % 2, n // 4
                        pe.wait_ge(S("PT_ready"), j + 1)
                        if n == 0:
                            ge(pe, "oalo_ready", b)
                        blocks = [0] if b == 0 else [1, 2, 3]
                        for t, vb in enumerate(blocks):
                            last = mm(ps[HD * z:HD * z + HD, 512 * 2 + P * (n // 2):512 * 2 + P * (n // 2) + P],
                                      vat[:, vb, HD * kv:HD * kv + HD], PT[j % 2][:, P * t:P * t + P],
                                      start=(t == 0), stop=(t == len(blocks) - 1))
                        last.then_inc(S("pv_done"), 1)
                    if 1 <= i <= len(ITEMS):
                        j = i - 1
                        pe.wait_ge(S("pnorm_ready"), j + 1)
                        ge(pe, "PT_ready", j)
                        for t in range(1 if ITEMS[j][0] == 0 else NB):
                            last = nc.tensor.transpose(bank(1, P, P * t), prob[j % 2][:, P * t:P * t + P], ident)
                        last.then_inc(S("pT_done"), 1)
                elif step == "kt":
                    g = at[0]
                    fwd, b = UPDATES[g]
                    if g < 2:
                        pe.wait_ge(S("ks_level"), 2 * LEVELS)
                        pe.wait_ge(S("gram_copied"), NB * (LEVELS + 1))
                    else:
                        pe.wait_ge(S("kt_ready"), g - 1)
                    for c in range(4):
                        last = nc.tensor.transpose(bank(3 + g % 2, P, P * c), (KS if fwd else KR)[:, pair_cols(c, b)], ident)
                    last.then_inc(S("kt_T"), 1)
                elif step == "state":
                    g = at[0]
                    pe.wait_ge(S("kt_ready"), g + 1)
                    ge(pe, "state_ready", 2 * (g - 1))
                    for c in range(4):
                        last = mm(bank(5 + g % 2, P, P * c), KT[g][:, P * c:P * c + P], v_t[:, UPDATES[g][1], P * c:P * c + P],
                                  start=True, stop=True)
                    last.then_inc(S("u_full"), 1)
                elif step == "hout":
                    b = at[0]
                    pe.wait_ge(S("q_level"), 2 * LEVELS)
                    pe.wait_ge(S("state_ready"), (0, 4, 8)[b] or 4)
                    pe.wait_ge(S("kt_ready"), 4)
                    for c in range(4):
                        out = bank(3 + b, P, P * c)
                        if b:
                            f, w = (0, 3) if b == 1 else (1, 2)
                            mm(out, Sbd[:, f, c, :], QP[:, pair_cols(c, b)], start=True, stop=False)
                            mm(out, Sbd[:, w, c, :], QQ[:, pair_cols(c, b)], start=False, stop=False)
                        for z in range(2):
                            r = slice(HD * z, HD * z + HD)
                            last = mm(ps[r, 512 * (3 + b) + P * c:512 * (3 + b) + P * c + P],
                                      v_t[:, b, P * c + HD * z:P * c + HD * z + HD],
                                      AT[:, b, 4 * z + c, :], start=(b == 0), stop=True)
                    last.then_inc(S("o_full"), 1)
                elif step == "hsum":
                    pe.wait_ge(S("osq_ready"), 1)
                    pe.wait_ge(S("state_ready"), 8)
                    for c in range(4):
                        last = mm(ps[0:8, 6 * 512:6 * 512 + TOK], head_rows(c, 8), osq[:, TOK * c:TOK * c + TOK],
                                  start=(c == 0), stop=(c == 3))
                    last.then_inc(S("osum_ready"), 1)
                elif step == "hnorm":
                    pe.wait_ge(S("orow_ready"), 1)
                    head_features(orow, at[0], 3 + at[0]).then_inc(S("obc_ready"), 1)

            pe.wait_ge(S("oblo_ready"), 4)
            for j in range(8):
                ge(pe, "x_chunk", j - 2)
                if j == 0:
                    project(U_OUT, 0, order=(4, 5, 6, 7, 0, 1, 2, 3), late=("oalo_ready", NB))
                else:
                    project(U_OUT + j, j % 3)

            def experts(l, U0):
                C0 = EXPERTS * l
                h_chunks = ("hlo_ready", KC * (1 if l == 0 else 3))

                def up(e, u, i=None, per_chunk=None, between=None, behind1=None, behind3=None):
                    n = 2 * (e + C0)
                    for f in range(2):
                        ge(pe, "silu_ready", n - 2 + f + 1)
                        project(u + 2 * f, 2 * f, i, per_chunk if f == 0 else None, between if f == 0 else None)
                        if behind1 and f == 0:
                            behind1()
                        ge(pe, "hmul_done", n - 2 + f + 1)
                        project(u + 2 * f + 1, 2 * f + 1, i)
                    if behind3:
                        behind3()

                def down(e, u, par, i=None):
                    for d in range(2):
                        unit_ready(u + d, i)
                        if d == 0:
                            pe.wait_ge(S("hidlo_ready"), 2 * (e + C0) + 2)
                        wh, wl = unit_view(whi, u + d, True), unit_view(wlo, u + d, True)
                        for z in range(2):
                            if isinstance(e, int) and e == EXPERTS - 1 and d:
                                pe.wait_ge(S("x_chunk"), (KC - 1) * (2 * l + 1) + 2 * z + 2)
                            elif isinstance(e, int) and 2 * e + d > 2 * (EXPERTS - 2):
                                pe.wait_ge(S("x_part"), KC * (2 * l + 1) + (4 if e == EXPERTS - 1 else 0) + 2 * z + 2)
                            else:
                                ge(pe, "y_free", 4 * e + (Y_FREE * l + 2 * d + z - 1))
                            for c in (2 * z, 2 * z + 1):
                                for k in range(2):
                                    last = three(bank(4 + c, TOK), wh[:, k, P * c:P * c + P], wl[:, k, P * c:P * c + P],
                                                 hidhi[:, par, k, :], hidlo[:, par, k, :], k == 0, k == 1)
                            last.then_inc(S("unit_used" if z else "y_ready"), 1)

                def logits(k):
                    pe.wait_ge(S("hf_ready"), h_chunks[1] + k + 1)
                    ins = mm(ps[0:20, 7 * 512:7 * 512 + TOK], wr[:, l, k, :], hfk[:, k, :], start=(k == 0), stop=(k == KC - 1))
                    if k == KC - 1:
                        ins.then_inc(S("logitsT_ready"), 1)

                def logit_tokens():
                    pe.wait_ge(S("logits_copied"), l + 1)
                    for t in range(NB):
                        last = nc.tensor.transpose(bank(7, 20, 20 * t), lgT[:, P * t:P * t + P], ident[0:20, 0:20])
                    last.then_inc(S("logits_ready"), 1)

                def combine_rows():
                    pe.wait_ge(S("combine_ready"), NB * (l + 1))
                    for t in range(NB):
                        last = nc.tensor.transpose(ps[0:16, 7 * 512 + P * t:7 * 512 + P * t + P], rt[:, 20, t, :], ident)
                    last.then_inc(S("combine_T"), 1)

                up(0, U0, None, h_chunks, logits, logit_tokens, combine_rows)
                up(1, U0 + 4)
                pe.wait_ge(S("combT_ready"), l + 1)
                down(0, U0 + 8, 0)
                with pe.Fori(0, 6) as i:
                    for z in range(2):
                        up(2 * i + (2 + z), U0 + 10 + 6 * z, i)
                        down(2 * i + (1 + z), U0 + 14 + 6 * z, 1 - z, i)
                for z in range(2):
                    up(14 + z, U0 + 82 + 6 * z)
                    down(13 + z, U0 + 86 + 6 * z, 1 - z)
                down(EXPERTS - 1, U0 + 94, 1)

            norm(1)
            experts(0, U_MOE0)

            norm(2)
            for j in range(16):
                g = j // 2
                ge(pe, "usig_ready" if j % 2 else "u_ready", g - 1 if j % 2 else 2 * (g - 1))
                project(U_PW1 + j, j % 4, per_chunk=("hlo_ready", 2 * KC) if j == 0 else None)
            pe.wait_ge(S("u_ready"), 2 * PE_CHUNK + 2)
            for t in range(TAPS):
                pe.wait_ge(S("diag_ready"), t + 1)
                mm(bank(5, CONV_N), diag[:, t % DIAGS, :], upad[:, PE_CHUNK, t:t + CONV_N], start=(t == 0), stop=(t == TAPS - 1))\
                    .then_inc(S("pconv_done" if t == TAPS - 1 else "diag_used"), 1)
                if t == 21:
                    ada_columns(4)
                if t % 2 and (t < 16 or t > 24):
                    ada(1)
            pe.wait_ge(S("convsum_ready"), 1)
            mm(bank(4, P), ones, sums[:, 0:P], start=True, stop=True)
            mm(bank(4, 256, P), ones, sums[:, BLK[1]:BLK[1] + 256], start=True, stop=True).then_inc(S("csum_ready"), 1)
            ada(48 - slot[0])
            pe.wait_ge(S("csqsum_ready"), 1)
            mm(bank(4, TOK), ones, sums[:, 0:TOK], start=True, stop=True).then_inc(S("cvar_ready"), 1)
            ada_columns(5)
            for j in range(8):
                ge(pe, "x_chunk", 14 + j - 3 if j >= 4 else 0)
                project(U_PW2 + j, j % 4, per_chunk=("clo_ready", 0) if j == 0 else None)
            norm(3)
            experts(1, U_MOE1)

            norm(4)
            for i in range(2 * NB):
                t, h = i // 2, i % 2
                pe.wait_ge(S("yf_ready"), 4 * h + 4)
                ge(pe, "ytok_ready", i - 1)
                for c in range(4):
                    last = nc.tensor.transpose(bank(5 + i % 2, P, P * c), hfk[:, 4 * h + c, P * t:P * t + P], ident)
                last.then_inc(S("yT_ready"), 1)


INPUTS = ["x_prompt", "x_sample", "cache_k", "cache_v", "state_hgrn", "c", "c_ctx", "ada_w", "ada_b", "norm1_g",
          "norm2_g", "mix_w_in", "mix_w_out", "attn_q_gain", "attn_k_gain", "hgrn_lower_bound", "hgrn_out_gain",
          "conv_pw1", "conv_dw", "conv_dw_b", "conv_ln_g", "conv_ln_b", "conv_pw2", "moe_w_group", "moe_b_group",
          "moe_w_expert", "moe_b_expert", "moe_w1", "moe_w3", "moe_w2", "final_g"]
OUTPUTS = [(1, 128, D), (1, 256, D), (1, 1, 128, 2, HD), (1, 1, 128, 2, HD), (1, 1, 2, HEADS, HD, HD)]


def kernel(**inputs):
    import concourse.bacc as bacc
    from concourse.bass_utils import run_bass_kernel_spmd

    nc = bacc.Bacc("TRN2", target_bir_lowering=False, num_devices=1, dynamic_dma_scratch_size=1024)
    arrays = {n: np.ascontiguousarray(inputs[n]) for n in INPUTS}
    arrays["shape_constants"] = shape_constants()
    aps = {n: nc.dram_tensor(n, a.shape, mybir.dt.from_np(a.dtype), kind="ExternalInput").ap()
           for n, a in arrays.items()}
    for i, shape in enumerate(OUTPUTS):
        aps[f"out{i}"] = nc.dram_tensor(f"out{i}", shape, F32, kind="ExternalOutput").ap()
    build(nc, aps)
    r = run_bass_kernel_spmd(nc, [arrays], core_ids=[0]).results[0]
    return tuple(r[f"out{i}"] for i in range(len(OUTPUTS)))
```
